# Optimizing a Trainium2 kernel written in Bass

```python
import math
import jax, jax.numpy as jnp
from jax import lax
import numpy as np

D_MODEL = 1024
BATCH = 1
SEQ = 2048
DEPTH = 1
DEC_BATCH = 1
DEC_SEQ = 32
PAST_LEN = 1024

CHUNK = 64
MIX_WIDTH = D_MODEL
MLSTM_WIDTH = MIX_WIDTH // 2
MLSTM_HEADS = 4
QK_DIM = MLSTM_WIDTH // MLSTM_HEADS
V_DIM = MLSTM_WIDTH // MLSTM_HEADS
ATT_WIDTH = MIX_WIDTH - MLSTM_WIDTH
ATT_HEADS = 8
ATT_HEAD_DIM = ATT_WIDTH // ATT_HEADS
KV_HEADS = 2
GQA_GROUP = ATT_HEADS // KV_HEADS
WINDOW = 128
WINDOW_CHUNKS = WINDOW // CHUNK
D_FF = 4 * D_MODEL
PLE_DIM = 256
EPS = 1e-6
PROJ_SIZES = (MLSTM_WIDTH, MLSTM_WIDTH, MLSTM_WIDTH, MLSTM_WIDTH, MLSTM_HEADS, MLSTM_HEADS,
              ATT_WIDTH, KV_HEADS * ATT_HEAD_DIM, KV_HEADS * ATT_HEAD_DIM)
PROJ_WIDTH = sum(PROJ_SIZES)

kernel_name = "hymba_mlstm_swa_sink_alibi_stream_step"

def _rmsnorm(x, g):
    x32 = x.astype(jnp.float32)
    y = x32 * lax.rsqrt(jnp.mean(x32 * x32, axis=-1, keepdims=True) + EPS)
    return (y * g.astype(jnp.float32)).astype(x.dtype)

def _split_cols(proj):
    outs, off = [], 0
    for s in PROJ_SIZES:
        outs.append(proj[..., off:off + s])
        off += s
    return outs

def _alibi_slopes():
    return 2.0 ** (-(jnp.arange(1, ATT_HEADS + 1, dtype=jnp.float32) * (8.0 / ATT_HEADS)))

def _mlstm_chunkwise(q, k, v, i_pre, f_pre, c0, n0, m0, chunk):
    B, S, H, dk = q.shape
    dv = v.shape[-1]
    nc = S // chunk
    f32 = jnp.float32

    def to_chunks(a):
        a = a.astype(f32).reshape((B, nc, chunk, H) + a.shape[3:])
        return jnp.moveaxis(jnp.moveaxis(a, 1, 0), 3, 2)

    qc, kc, vc = to_chunks(q), to_chunks(k), to_chunks(v)
    ic, lfc = to_chunks(i_pre), to_chunks(jax.nn.log_sigmoid(f_pre.astype(f32)))
    causal = jnp.tril(jnp.ones((chunk, chunk), dtype=bool))

    def step(carry, xs):
        c, n, m = carry
        qb, kb, vb, ib, lfb = xs
        b = jnp.cumsum(lfb, axis=-1)
        a = b + m[..., None]
        dmat = jnp.where(causal, b[..., :, None] - b[..., None, :] + ib[..., None, :], -jnp.inf)
        mt = jnp.maximum(a, jnp.max(dmat, axis=-1))
        w_inter = jnp.exp(a - mt)
        s = jnp.einsum('bhtd,bhsd->bhts', qb, kb) * jnp.exp(dmat - mt[..., None])
        num = jnp.einsum('bhts,bhsv->bhtv', s, vb) + w_inter[..., None] * jnp.einsum('bhtd,bhdv->bhtv', qb, c)
        den = jnp.sum(s, axis=-1) + w_inter * jnp.einsum('bhtd,bhd->bht', qb, n)
        h = num / jnp.maximum(jnp.abs(den), jnp.exp(-mt))[..., None]
        m_new = mt[..., -1]
        w_c = jnp.exp(b[..., -1] + m - m_new)
        w_s = jnp.exp(b[..., -1:] - b + ib - m_new[..., None])
        c_new = w_c[..., None, None] * c + jnp.einsum('bhs,bhsd,bhsv->bhdv', w_s, kb, vb)
        n_new = w_c[..., None] * n + jnp.einsum('bhs,bhsd->bhd', w_s, kb)
        return (c_new, n_new, m_new), h

    (c1, n1, m1), hs = lax.scan(step, (c0.astype(f32), n0.astype(f32), m0.astype(f32)),
                                (qc, kc, vc, ic, lfc))
    hs = jnp.moveaxis(jnp.moveaxis(hs, 2, 3), 0, 1).reshape(B, S, H, dv)
    return hs.astype(q.dtype), c1, n1, m1

def _swa_attention(qb, kb, vb, q_pos, k_pos, sinks):
    f32 = jnp.float32
    s = jnp.einsum('bnqkgd,bnskd->bnkgqs', qb.astype(f32), kb.astype(f32)) * (ATT_HEAD_DIM ** -0.5)
    qp, kp = q_pos[:, :, None], k_pos[:, None, :]
    cdiff = qp // CHUNK - kp // CHUNK
    mask = (cdiff >= 0) & (cdiff <= WINDOW_CHUNKS) & (kp >= 0)
    dist = jnp.abs(qp - kp).astype(f32)
    slopes = _alibi_slopes().reshape(KV_HEADS, GQA_GROUP)
    s = s - slopes[None, None, :, :, None, None] * dist[None, :, None, None]
    s = jnp.where(mask[None, :, None, None], s, -jnp.inf)
    sink = sinks.astype(f32).reshape(KV_HEADS, GQA_GROUP)[None, None, :, :, None]
    mx = jnp.maximum(jnp.max(s, axis=-1), sink)
    p = jnp.exp(s - mx[..., None])
    den = jnp.sum(p, axis=-1) + jnp.exp(sink - mx)
    o = jnp.einsum('bnkgqs,bnskd->bnqkgd', p / den[..., None], vb.astype(f32))
    B, N, Lq = o.shape[:3]
    return o.reshape(B, N * Lq, ATT_WIDTH).astype(qb.dtype)

def _layer(x, p, c0, n0, m0, cache_k, cache_v, n_keep, prompt,
           g_mix, w_in, b_igate, b_fgate, g_head, attn_sinks, w_out,
           g_mlp, w_up, w_down, g_ple, w_ple_gate, w_ple_proj):
    B, S, _ = x.shape
    h = _rmsnorm(x, g_mix)
    q_m, k_m, v_m, o_m, i_pre, f_pre, q_a, k_a, v_a = _split_cols(h @ w_in)

    qm = q_m.reshape(B, S, MLSTM_HEADS, QK_DIM)
    km = k_m.reshape(B, S, MLSTM_HEADS, QK_DIM) * (QK_DIM ** -0.5)
    vm = v_m.reshape(B, S, MLSTM_HEADS, V_DIM)
    chunk = CHUNK if prompt else S
    h_til, c1, n1, m1 = _mlstm_chunkwise(qm, km, vm, i_pre + b_igate, f_pre + b_fgate,
                                         c0, n0, m0, chunk)
    h_m = jax.nn.sigmoid(o_m) * _rmsnorm(h_til, g_head.reshape(MLSTM_HEADS, V_DIM)).reshape(B, S, MLSTM_WIDTH)

    qa = q_a.reshape(B, S, KV_HEADS, GQA_GROUP, ATT_HEAD_DIM)
    ka = k_a.reshape(B, S, KV_HEADS, ATT_HEAD_DIM)
    va = v_a.reshape(B, S, KV_HEADS, ATT_HEAD_DIM)
    if prompt:
        nc = S // CHUNK
        pad = WINDOW_CHUNKS * CHUNK
        band = lambda a: jnp.concatenate(
            [a[:, j:j + nc] for j in range(WINDOW_CHUNKS + 1)], axis=2)
        kp = jnp.pad(ka, ((0, 0), (pad, 0), (0, 0), (0, 0))).reshape(B, nc + WINDOW_CHUNKS, CHUNK, KV_HEADS, ATT_HEAD_DIM)
        vp = jnp.pad(va, ((0, 0), (pad, 0), (0, 0), (0, 0))).reshape(B, nc + WINDOW_CHUNKS, CHUNK, KV_HEADS, ATT_HEAD_DIM)
        kb, vb = band(kp), band(vp)
        qb = qa.reshape(B, nc, CHUNK, KV_HEADS, GQA_GROUP, ATT_HEAD_DIM)
        q_pos = jnp.arange(S, dtype=jnp.int32).reshape(nc, CHUNK)
        k_pos = (jnp.arange(nc, dtype=jnp.int32) * CHUNK)[:, None] - pad + \
            jnp.arange((WINDOW_CHUNKS + 1) * CHUNK, dtype=jnp.int32)[None, :]
        k_all, v_all = ka, va
    else:
        k_all = jnp.concatenate([cache_k.astype(ka.dtype), ka], axis=1)
        v_all = jnp.concatenate([cache_v.astype(va.dtype), va], axis=1)
        kb, vb, qb = k_all[:, None], v_all[:, None], qa[:, None]
        q_pos = (PAST_LEN + jnp.arange(S, dtype=jnp.int32))[None]
        k_pos = (PAST_LEN - n_keep + jnp.arange(n_keep + S, dtype=jnp.int32))[None]
    o_a = _swa_attention(qb, kb, vb, q_pos, k_pos, attn_sinks)
    new_k, new_v = k_all[:, -n_keep:], v_all[:, -n_keep:]

    x = x + jnp.concatenate([h_m, o_a], axis=-1) @ w_out
    x = x + jnp.square(jax.nn.relu(_rmsnorm(x, g_mlp) @ w_up)) @ w_down
    x = x + jax.nn.sigmoid(_rmsnorm(x, g_ple) @ w_ple_gate) * (p @ w_ple_proj)
    return x, new_k, new_v, c1, n1, m1

def setup_inputs(seed: int = 0) -> dict:
    key = jax.random.key(seed)
    ks = jax.random.split(key, 24)
    nrm = lambda k, shape, scale: jax.random.normal(k, shape, jnp.float32) * scale
    w_keep = min(WINDOW, PAST_LEN)
    return {
        "x_prompt": nrm(ks[0], (BATCH, SEQ, D_MODEL), 1.0),
        "x_sample": nrm(ks[1], (DEC_BATCH, DEC_SEQ, D_MODEL), 1.0),
        "cache_swa_k": nrm(ks[2], (DEPTH, DEC_BATCH, w_keep, KV_HEADS, ATT_HEAD_DIM), 1.0),
        "cache_swa_v": nrm(ks[3], (DEPTH, DEC_BATCH, w_keep, KV_HEADS, ATT_HEAD_DIM), 1.0),
        "state_mlstm_c": nrm(ks[4], (DEPTH, DEC_BATCH, MLSTM_HEADS, QK_DIM, V_DIM), 0.1),
        "state_mlstm_n": nrm(ks[5], (DEPTH, DEC_BATCH, MLSTM_HEADS, QK_DIM), 0.1),
        "state_mlstm_m": nrm(ks[6], (DEPTH, DEC_BATCH, MLSTM_HEADS), 1.0),
        "p_prompt": nrm(ks[7], (DEPTH, BATCH, SEQ, PLE_DIM), 1.0),
        "p_sample": nrm(ks[8], (DEPTH, DEC_BATCH, DEC_SEQ, PLE_DIM), 1.0),
        "g_mix": 1.0 + nrm(ks[9], (DEPTH, D_MODEL), 0.02),
        "w_in": nrm(ks[10], (DEPTH, D_MODEL, PROJ_WIDTH), D_MODEL ** -0.5),
        "b_igate": nrm(ks[11], (DEPTH, MLSTM_HEADS), 0.1),
        "b_fgate": 3.0 + nrm(ks[12], (DEPTH, MLSTM_HEADS), 0.1),
        "g_head": 1.0 + nrm(ks[13], (DEPTH, MLSTM_WIDTH), 0.02),
        "attn_sinks": nrm(ks[14], (DEPTH, ATT_HEADS), 0.5),
        "w_out": nrm(ks[15], (DEPTH, MIX_WIDTH, D_MODEL), MIX_WIDTH ** -0.5),
        "g_mlp": 1.0 + nrm(ks[16], (DEPTH, D_MODEL), 0.02),
        "w_up": nrm(ks[17], (DEPTH, D_MODEL, D_FF), D_MODEL ** -0.5),
        "w_down": nrm(ks[18], (DEPTH, D_FF, D_MODEL), D_FF ** -0.5),
        "g_ple": 1.0 + nrm(ks[19], (DEPTH, D_MODEL), 0.02),
        "w_ple_gate": nrm(ks[20], (DEPTH, D_MODEL, D_MODEL), D_MODEL ** -0.5),
        "w_ple_proj": nrm(ks[21], (DEPTH, PLE_DIM, D_MODEL), PLE_DIM ** -0.5),
        "g_final": 1.0 + nrm(ks[22], (D_MODEL,), 0.02),
    }

def reference(x_prompt, x_sample, cache_swa_k, cache_swa_v, state_mlstm_c, state_mlstm_n,
              state_mlstm_m, p_prompt, p_sample, g_mix, w_in, b_igate, b_fgate, g_head,
              attn_sinks, w_out, g_mlp, w_up, w_down, g_ple, w_ple_gate, w_ple_proj, g_final):
    n_keep = cache_swa_k.shape[2]
    xp, xs = x_prompt, x_sample
    pk, pv, pc, pn, pm = [], [], [], [], []
    sk, sv, sc, sn, sm = [], [], [], [], []
    for l in range(DEPTH):
        lw = (g_mix[l], w_in[l], b_igate[l], b_fgate[l], g_head[l], attn_sinks[l], w_out[l],
              g_mlp[l], w_up[l], w_down[l], g_ple[l], w_ple_gate[l], w_ple_proj[l])
        zc = jnp.zeros((BATCH, MLSTM_HEADS, QK_DIM, V_DIM), jnp.float32)
        zn = jnp.zeros((BATCH, MLSTM_HEADS, QK_DIM), jnp.float32)
        zm = jnp.zeros((BATCH, MLSTM_HEADS), jnp.float32)
        xp, k1, v1, c1, n1, m1 = _layer(xp, p_prompt[l], zc, zn, zm, None, None, n_keep, True, *lw)
        xs, k2, v2, c2, n2, m2 = _layer(xs, p_sample[l], state_mlstm_c[l], state_mlstm_n[l],
                                        state_mlstm_m[l], cache_swa_k[l], cache_swa_v[l],
                                        n_keep, False, *lw)
        pk.append(k1); pv.append(v1); pc.append(c1); pn.append(n1); pm.append(m1)
        sk.append(k2); sv.append(v2); sc.append(c2); sn.append(n2); sm.append(m2)
    y_prompt = _rmsnorm(xp, g_final)
    y_sample = _rmsnorm(xs, g_final)
    return (y_prompt, y_sample,
            jnp.stack(pk), jnp.stack(pv), jnp.stack(pc), jnp.stack(pn), jnp.stack(pm),
            jnp.stack(sk), jnp.stack(sv), jnp.stack(sc), jnp.stack(sn), jnp.stack(sm))


_drawn_inputs = setup_inputs


def setup_inputs(seed=0):
    import zlib

    import numpy as np

    out = dict(_drawn_inputs(seed))
    spreads = {}
    factors = {'g_head': 7.795, 'attn_sinks': 8.0, 'g_mlp': 3.424, 'g_ple': 8.0, 'g_final': 2.821}
    for name, (base, spread) in spreads.items():
        noise = np.random.default_rng([zlib.crc32(name.encode()), seed]).standard_normal(out[name].shape)
        drawn = base * np.exp(spread * noise) if base else spread * noise
        out[name] = __import__('jax').numpy.asarray(drawn.astype(out[name].dtype))
    for name, factor in factors.items():
        out[name] = (out[name] * factor).astype(out[name].dtype)
    return out
```

```python
from contextlib import ExitStack
from typing import NamedTuple

import concourse.bass as bass
from concourse import mybir

F32 = mybir.dt.float32
F32R = mybir.dt.float32r
ALU = mybir.AluOpType
ACT = mybir.ActivationFunctionType
AX = mybir.AxisListType

P = 128
D = 1024
KC = D // P
SEQ, DEC = 2048, 32
NT = SEQ // P
TOK = SEQ + DEC
HEADS, QK = 4, 128
VA = QK + 1
MW = HEADS * QK
GATE_COL = 4 * MW
Q_COL = GATE_COL + 2 * HEADS
AH, KVH, HD = 8, 2, 64
GRP = AH // KVH
AW = AH * HD
KV_COL = Q_COL + AW
KVW = KVH * HD
FF = 4 * D
PLE = 256
EPS = 1e-6
MASKED = -1e30
MLP_BLOCK = 256
NB = 512


class Tile(NamedTuple):
    i: object
    slot: int
    n: int


def tile_at(i, slot):
    return Tile(i, slot, DEC if isinstance(i, int) and i == NT else P)


def reached(eng, sem, count):
    if isinstance(count, int) and count <= 0:
        return
    eng.wait_ge(sem, count)


def all_of(eng, sem, i, per=1):
    reached(eng, sem, (i + 1) * per)


def slot_loaded(eng, sems, t):
    reached(eng, sems[t.slot], t.i * 8 + 16 - 8 * t.slot)


def rounds(eng, body, last):
    for r in range(3):
        body(r, r % 2)
    with eng.Fori(0, (NT - 6) // 2) as turn:
        body(turn * 2 + 3, 1)
        body(turn * 2 + 4, 0)
    for r in range(NT - 3, last + 1):
        body(r, r % 2)


def exists(i):
    return not isinstance(i, int) or 0 <= i <= NT


def split_product(eng, out, lhs, rhs, chunks, first=True, last=True):
    (lh, ll), (rh, rl) = lhs, rhs
    for k in chunks:
        f, e = first and k == chunks[0], last and k == chunks[-1]
        eng.matmul(out, lh(k), rh(k), start=f, stop=False)
        eng.matmul(out, lh(k), rl(k), start=False, stop=False)
        ins = eng.matmul(out, ll(k), rh(k), start=False, stop=e)
    return ins


def token_rows(eng, i, n):
    return slice(i * P, i * P + n) if isinstance(i, int) else bass.ds(eng.snap(i * P), n)


def norm_rows(dve, sem, rooted, i, x, gain, out, stats, ms):
    base = i * NORM
    groups = 2 * D // NB
    for c in range(D // NB):
        ins = dve.bn_stats(stats[:, c, :], x[:, c * NB:(c + 1) * NB])
    ins.then_inc(sem, 1)
    by_group = stats.rearrange("p c (g s) -> p (c g) s", s=3)
    mean, spread = by_group[:, :, 1], by_group[:, :, 2]
    dve.wait_ge(sem, base + 1)
    dve.tensor_tensor(ms[:, 0:groups], mean, mean, ALU.mult).then_inc(sem, 1)
    dve.wait_ge(sem, base + 2)
    dve.scalar_tensor_tensor(ms[:, 0:groups], ms[:, 0:groups], float(D // groups), spread, ALU.mult, ALU.add).then_inc(sem, 1)
    dve.wait_ge(sem, base + 3)
    dve.reduce_sum(ms[:, 4:5], ms[:, 0:groups], AX.X).then_inc(sem, 1)
    dve.wait_ge(sem, base + 4)
    dve.tensor_scalar(ms[:, 5:6], ms[:, 4:5], 1.0 / D, EPS, ALU.mult, ALU.add).then_inc(sem, 1)
    all_of(dve, rooted, i)
    dve.scalar_tensor_tensor(out, x, ms[:, 6:7], gain, ALU.mult, ALU.mult).then_inc(sem, 1)


def norm_root(pool, sem, rooted, i, ms, minus_half):
    reached(pool, sem, i * NORM + 5)
    pool.tensor_tensor(ms[:, 6:7], ms[:, 5:6], minus_half, ALU.pow).then_inc(rooted, 1)


NORM = 6


def make_identity(pool, ident, made):
    pool.memset(ident, 0.0).then_inc(made, 1)
    pool.wait_ge(made, 1)
    pool.affine_select(out=ident, in_=ident, compare_op=ALU.not_equal, fill=1.0, base=0,
                       pattern=[[-1, P]], channel_multiplier=1).then_inc(made, 1)


def mlstm_phase(nc, x_prompt, x_sample, g_mix, w_in, b_igate, b_fgate, g_head, state_c, state_n, state_m,
                mixed, out_c, out_n, out_m):
    MC = Q_COL
    PIECES = 4
    PC = MC // PIECES
    with ExitStack() as ctx:
        def sb(name, shape, dt=F32):
            return ctx.enter_context(nc.sbuf_tensor("m_" + name, shape, dt))

        def ps(name, shape):
            return ctx.enter_context(nc.psum_tensor("m_" + name, shape, F32))

        def sem(name):
            return ctx.enter_context(nc.semaphore("m_" + name))

        w_hi, w_lo = sb("w_hi", [P, KC, MC], F32R), sb("w_lo", [P, KC, MC], F32R)
        w_raw = sb("w_raw", [P, 2, PC])
        x = sb("x", [P, 2, D])
        hT_hi, hT_lo = sb("hT_hi", [P, 2, KC, P], F32R), sb("hT_lo", [P, 2, KC, P], F32R)
        gmix = sb("gmix", [P, D])
        q, k = sb("q", [P, 2, MW]), sb("k", [P, 2, MW])
        v, o = sb("v", [P, 2, HEADS, VA]), sb("o", [P, 2, MW])
        qT, kT, qsT = sb("qT", [P, HEADS, P]), sb("kT", [P, HEADS, P]), sb("qsT", [P, HEADS, P])
        decay = sb("decay", [P, HEADS, P])
        C, C_new, C_dec = (sb(n, [P, HEADS, VA]) for n in ("C", "C_new", "C_dec"))
        heads_out = sb("heads_out", [P, MW])
        ghead = sb("ghead", [P, MW])
        causal = sb("causal", [P, P])
        ident = sb("ident", [P, P])
        pick = sb("pick", [HEADS, HEADS, P])
        gates = sb("gates", [P, 2 * HEADS])
        gbias = sb("gbias", [HEADS, 2])
        rows = sb("rows", [HEADS, 8, P])
        m_rows = sb("m_rows", [HEADS, 2, P])
        m_dec = sb("m_dec", [HEADS, 1])
        ones_row, zero_row = sb("ones_row", [HEADS, P]), sb("zero_row", [HEADS, P])
        cols = sb("cols", [P, 16])
        stats, ms = sb("stats", [P, 2, 6]), sb("ms", [P, 8])
        minus_half = sb("minus_half", [P, HEADS])
        fin = sb("fin", [P, 8, HEADS])
        I_ROW, F_ROW, F_ABS, F_EXP, B, G, U, W = range(8)
        LOG1P, LF = F_EXP, F_ROW
        E_ROW = F_ABS

        proj = [ps("proj0", [P, NB]), ps("proj1", [P, NB])]
        turned = ps("turned", [P, KC, P])
        wide = ps("wide", [P, HEADS, P])
        small = ps("small", [P, NB])
        acc = ps("acc", [P, HEADS, 256])
        GATES, ROWS, COLS = small[:, 0:2 * HEADS], small[0:HEADS, 128:384], small[:, 16:32]
        junk = wide

        ident_made, consts_in, const_sb, dec_in = sem("ident_made"), sem("consts_in"), sem("const_sb"), sem("dec_in")
        w_in_sem, w_hi_made, w_lo_made = [sem("w_raw0"), sem("w_raw1")], sem("w_hi_made"), sem("w_lo_made")
        x_in, normed, h_turned = [sem("x_in0"), sem("x_in1")], sem("normed"), sem("h_turned")
        h_hi, h_lo, rooted, heads_rooted = sem("h_hi"), sem("h_lo"), sem("rooted"), sem("heads_rooted")
        gates_ps, gates_sb, rows_ps, row_step, row_act = (sem(n) for n in ("gates_ps", "gates_sb", "rows_ps", "row_step", "row_act"))
        q_ps, k_ps, v_ps, o_ps = (sem(n) for n in ("q_ps", "k_ps", "v_ps", "o_ps"))
        q_sb, k_sb, v_sb, o_sb = (sem(n) for n in ("q_sb", "k_sb", "v_sb", "o_sb"))
        cols_ps, cols_sb, masked, decayed = (sem(n) for n in ("cols_ps", "cols_sb", "masked", "decayed"))
        qk_turned, qT_sb, kT_sb, q_scaled, k_scaled = (sem(n) for n in ("qk_turned", "qT_sb", "kT_sb", "q_scaled", "k_scaled"))
        qs_turned, qsT_sb, scores_ps, state_ps = (sem(n) for n in ("qs_turned", "qsT_sb", "scores_ps", "state_ps"))
        weighted, C_made, C_moved, num_ps, squared, fin_step, out_done, state_out = (
            sem(n) for n in ("weighted", "C_made", "C_moved", "num_ps", "squared", "fin_step", "out_done", "state_out"))
        ROW_STEPS, ROW_ACTS, FIN_STEPS = 8, 4, 12
        N_CONST = 7

        block = ctx.enter_context(nc.Block())

        @block.sync
        def _(sp):
            sp.dma_start(x[:, 0, :], x_prompt[0:P, :]).then_inc(x_in[0], 16)
            sp.dma_start(x[:, 1, :], x_prompt[P:2 * P, :]).then_inc(x_in[1], 16)
            sp.dma_start(gmix[:], g_mix.partition_broadcast(P)).then_inc(consts_in, 16)
            sp.dma_start(gbias[:, 0:1], b_igate.rearrange("(h a) -> h a", a=1)).then_inc(consts_in, 16)
            sp.dma_start(gbias[:, 1:2], b_fgate.rearrange("(h a) -> h a", a=1)).then_inc(consts_in, 16)
            sp.dma_start(ghead[:], g_head.partition_broadcast(P)).then_inc(consts_in, 16)
            sp.dma_start(C_dec[:, :, 0:QK], state_c.rearrange("h d v -> d h v")).then_inc(consts_in, 16)
            sp.dma_start(C_dec[:, :, QK], state_n.rearrange("h d -> d h"), allow_slow_non_contiguous=True).then_inc(consts_in, 16)
            sp.dma_start(m_dec[:], state_m.rearrange("(h a) -> h a", a=1)).then_inc(consts_in, 16)
            for n in range(PIECES * KC):
                c, col, raw = n // PIECES, n % PIECES * PC, n % 2
                reached(sp, w_lo_made, n - 1)
                sp.dma_start(w_raw[:, raw, :], w_in[c * P:(c + 1) * P, col:col + PC]).then_inc(w_in_sem[raw], 16)

            def body(r, slot):
                j = r - 1
                if exists(r + 2):
                    nxt = tile_at(r + 2, slot)
                    src = x_sample if nxt.n < P else x_prompt[token_rows(sp, nxt.i, P), :]
                    all_of(sp, h_turned, r)
                    sp.dma_start(x[0:nxt.n, nxt.slot, :], src).then_inc(x_in[nxt.slot], 16)
                if exists(j):
                    t = tile_at(j, 1 - slot)
                    dst = mixed[token_rows(sp, j, t.n), :]
                    all_of(sp, fin_step, j, FIN_STEPS)
                    sp.dma_start(dst, heads_out[0:t.n, :]).then_inc(out_done, 16)
                if isinstance(j, int) and j >= NT - 1:
                    which = j - (NT - 1)
                    all_of(sp, C_made, j)
                    all_of(sp, row_step, j, ROW_STEPS)
                    n = tile_at(j, 0).n
                    sp.dma_start(out_c[which].rearrange("h d v -> d h v"), C_new[:, :, 0:QK]).then_inc(state_out, 16)
                    sp.dma_start(out_n[which].rearrange("h d -> d h"), C_new[:, :, QK], allow_slow_non_contiguous=True).then_inc(state_out, 16)
                    sp.dma_start(out_m[which].rearrange("(h a) -> h a", a=1), m_rows[:, j % 2, n - 1:n]).then_inc(state_out, 16)

            rounds(sp, body, NT + 1)
            sp.wait_ge(out_done, 16 * (NT + 1))
            sp.wait_ge(state_out, 16 * 6)

        @block.gpsimd
        def _(pool):
            make_identity(pool, ident[:], ident_made)
            pool.memset(causal[:], 0.0).then_inc(ident_made, 1)
            pool.wait_ge(ident_made, 3)
            pool.affine_select(out=causal[:], in_=causal[:], compare_op=ALU.is_ge, fill=MASKED, base=0,
                               pattern=[[1, P]], channel_multiplier=-1).then_inc(ident_made, 1)
            pool.memset(minus_half[:], -0.5).then_inc(ident_made, 1)
            pool.wait_ge(ident_made, 5)

            def root(t):
                norm_root(pool, normed, rooted, t.i, ms[0:t.n], minus_half[0:t.n, 0:1])

            root(tile_at(0, 0))
            root(tile_at(1, 1))

            def body(r, slot):
                if exists(r + 2):
                    root(tile_at(r + 2, slot))
                if exists(r - 1):
                    m = tile_at(r - 1, 1 - slot).n
                    reached(pool, fin_step, (r - 1) * FIN_STEPS + 6)
                    pool.tensor_tensor(fin[0:m, 3, :], fin[0:m, 6, :], minus_half[0:m, :], ALU.pow).then_inc(heads_rooted, 1)

            rounds(pool, body, NT + 1)

        @block.scalar
        def _(act):
            def split_h(t):
                all_of(act, h_turned, t.i)
                all_of(act, o_ps, t.i - 2)
                act.activation(hT_hi[:, t.slot, :, 0:t.n], turned[:, :, 0:t.n], ACT.Copy).then_inc(h_hi, 1)

            split_h(tile_at(0, 0))
            for n in range(PIECES * KC):
                c, col, raw = n // PIECES, n % PIECES * PC, n % 2
                act.wait_ge(w_in_sem[raw], 16 * (n // 2 + 1))
                act.activation(w_hi[:, c, col:col + PC], w_raw[:, raw, :], ACT.Copy).then_inc(w_hi_made, 1)

            def body(r, slot):
                i, j = r, r - 1
                cur, mix = tile_at(i, slot), tile_at(j, 1 - slot)
                n = cur.n
                if exists(i):
                    all_of(act, q_ps, i)
                    act.activation(q[0:n, slot, :], proj[0][0:n, :], ACT.Copy).then_inc(q_sb, 1)
                if exists(r + 1):
                    split_h(tile_at(r + 1, 1 - slot))
                if exists(j):
                    all_of(act, masked, j)
                    all_of(act, cols_sb, j, 2)
                    for h in range(HEADS):
                        ins = act.activation(decay[0:mix.n, h, 0:mix.n], decay[0:mix.n, h, 0:mix.n], ACT.Exp, bias=cols[0:mix.n, h:h + 1])
                    ins.then_inc(decayed, 1)
                if exists(i):
                    all_of(act, k_ps, i)
                    act.activation(k[0:n, slot, :], proj[1][0:n, :], ACT.Copy, scale=QK ** -0.5).then_inc(k_sb, 1)
                if exists(j):
                    all_of(act, qk_turned, j)
                    act.activation(qT[:, :, 0:mix.n], turned[:, 0:HEADS, 0:mix.n], ACT.Copy).then_inc(qT_sb, 1)
                if exists(i):
                    reached(act, row_step, i * ROW_STEPS + 2)
                    act.activation(rows[:, F_EXP, 0:n], rows[:, F_ABS, 0:n], ACT.Exp, scale=-1.0).then_inc(row_act, 1)
                    reached(act, row_act, i * ROW_ACTS + 1)
                    act.activation(rows[:, LOG1P, 0:n], rows[:, F_EXP, 0:n], ACT.Ln, bias=1.0).then_inc(row_act, 1)
                if exists(j):
                    all_of(act, qs_turned, j)
                    act.activation(qsT[:, :, 0:mix.n], turned[:, 0:HEADS, 0:mix.n], ACT.Copy).then_inc(qsT_sb, 1)
                if exists(i):
                    all_of(act, o_ps, i)
                    all_of(act, fin_step, i - 2, FIN_STEPS)
                    act.activation(o[0:n, slot, :], proj[1][0:n, :], ACT.Exp, scale=-1.0).then_inc(o_sb, 1)
                    reached(act, row_step, i * ROW_STEPS + 7)
                    m_in = m_dec[:] if n < P else m_rows[:, 1 - slot, P - 1:P]
                    act.activation(rows[:, W, 0:n], rows[:, U, 0:n], ACT.Exp, scale=-1.0, bias=m_in).then_inc(row_act, 1)
                    reached(act, row_step, i * ROW_STEPS + 8)
                    act.activation(rows[:, E_ROW, 0:n], m_rows[:, slot, 0:n], ACT.Exp, scale=-1.0).then_inc(row_act, 1)
                if exists(j):
                    all_of(act, num_ps, j)
                    reached(act, fin_step, (j - 1) * FIN_STEPS + 7)
                    for h in range(HEADS):
                        ins = act.activation(junk[0:mix.n, h, :], acc[0:mix.n, h, 0:QK], ACT.Square, accum_out=fin[0:mix.n, 3, h:h + 1])
                    ins.then_inc(squared, 1)
                    all_of(act, C_made, j)
                    act.activation(C[:], C_new[:], ACT.Copy).then_inc(C_moved, 1)

            rounds(act, body, NT + 1)

        @block.tensor
        def _(pe):
            pe.wait_ge(ident_made, 2)

            def turn_h(t):
                all_of(pe, normed, t.i, NORM)
                all_of(pe, qsT_sb, t.i - 3)
                for c in range(KC):
                    ins = pe.transpose(turned[:, c, 0:t.n], x[0:t.n, t.slot, c * P:(c + 1) * P], ident[0:t.n, 0:t.n])
                ins.then_inc(h_turned, 1)

            def project(out, t, c0, width, done):
                split_product(pe, out, (lambda c: hT_hi[:, t.slot, c, :], lambda c: hT_lo[:, t.slot, c, :]),
                              (lambda c: w_hi[:, c, c0:c0 + width], lambda c: w_lo[:, c, c0:c0 + width]),
                              range(KC)).then_inc(done, 1)

            turn_h(tile_at(0, 0))
            pe.wait_ge(w_hi_made, PIECES * KC)
            pe.wait_ge(w_lo_made, PIECES * KC)
            pe.wait_ge(const_sb, 1)

            def body(r, slot):
                i, j = r, r - 1
                cur, mix = tile_at(i, slot), tile_at(j, 1 - slot)
                n, m = cur.n, mix.n
                if exists(i):
                    all_of(pe, h_hi, i)
                    all_of(pe, h_lo, i)
                    all_of(pe, cols_sb, i - 2, 2)
                    reached(pe, row_step, (i - 1) * ROW_STEPS + 3)
                    project(GATES, cur, GATE_COL, 2 * HEADS, gates_ps)
                    all_of(pe, v_sb, i - 1)
                    project(proj[0][:], cur, 0, MW, q_ps)
                if exists(j):
                    all_of(pe, row_act, j, ROW_ACTS)
                    all_of(pe, row_step, j, ROW_STEPS)
                    all_of(pe, squared, j - 1)
                    all_of(pe, gates_sb, min(i, NT) if isinstance(i, int) else i)
                    for h in range(HEADS):
                        pe.matmul(wide[0:m, h, 0:m], pick[:, h, 0:m], rows[:, U, 0:m], start=True, stop=True)
                    for c, row in enumerate((G, W, E_ROW)):
                        pe.transpose(COLS[0:m, c * HEADS:(c + 1) * HEADS], rows[:, row, 0:m], ident[0:HEADS, 0:HEADS])
                    for h in range(HEADS):
                        ins = pe.matmul(COLS[:, 3 * HEADS + h:3 * HEADS + h + 1], pick[:, h, :], rows[:, W, m - 1:m], start=True, stop=True)
                    ins.then_inc(cols_ps, 1)
                if exists(r + 1):
                    turn_h(tile_at(r + 1, 1 - slot))
                if exists(i):
                    all_of(pe, o_sb, i - 1)
                    project(proj[1][:], cur, MW, MW, k_ps)
                if exists(j):
                    if exists(r + 1):
                        all_of(pe, h_hi, r + 1)
                        all_of(pe, h_lo, r + 1)
                    else:
                        all_of(pe, qsT_sb, j - 1)
                    all_of(pe, q_sb, j)
                    all_of(pe, k_sb, j)
                    for h in range(HEADS):
                        pe.transpose(turned[:, h, 0:m], q[0:m, mix.slot, h * QK:(h + 1) * QK], ident[0:m, 0:m])
                    for h in range(HEADS):
                        ins = pe.transpose(turned[:, HEADS + h, 0:m], k[0:m, mix.slot, h * QK:(h + 1) * QK], ident[0:m, 0:m])
                    ins.then_inc(qk_turned, 1)
                if exists(i):
                    all_of(pe, gates_sb, i)
                    all_of(pe, cols_sb, j, 2)
                    pe.transpose(ROWS[:, 0:n], gates[0:n, 0:HEADS], ident[0:n, 0:n])
                    pe.transpose(ROWS[:, P:P + n], gates[0:n, HEADS:2 * HEADS], ident[0:n, 0:n]).then_inc(rows_ps, 1)
                    all_of(pe, q_sb, i)
                    project(proj[0][:], cur, 2 * MW, MW, v_ps)
                if exists(j):
                    all_of(pe, q_scaled, j)
                    all_of(pe, qT_sb, j)
                    all_of(pe, kT_sb, j)
                    for h in range(HEADS):
                        ins = pe.transpose(turned[:, h, 0:m], q[0:m, mix.slot, h * QK:(h + 1) * QK], ident[0:m, 0:m])
                    ins.then_inc(qs_turned, 1)
                    all_of(pe, masked, j)
                    for h in range(HEADS):
                        ins = pe.matmul(wide[0:m, h, 0:m], kT[:, h, 0:m], qT[:, h, 0:m], start=True, stop=True)
                    ins.then_inc(scores_ps, 1)
                    all_of(pe, k_scaled, j)
                    all_of(pe, v_sb, j)
                    all_of(pe, fin_step, j - 1, FIN_STEPS)
                    for h in range(HEADS):
                        ins = pe.matmul(acc[:, h, 0:VA], k[0:m, mix.slot, h * QK:(h + 1) * QK], v[0:m, mix.slot, h, :], start=True, stop=True)
                    ins.then_inc(state_ps, 1)
                if exists(i):
                    all_of(pe, k_sb, i)
                    project(proj[1][:], cur, 3 * MW, MW, o_ps)
                if exists(j):
                    all_of(pe, qsT_sb, j)
                    all_of(pe, weighted, j)
                    all_of(pe, C_made, j)
                    if m == P:
                        all_of(pe, C_moved, j - 1)
                    state = C if m == P else C_dec
                    for h in range(HEADS):
                        pe.matmul(acc[0:m, h, 0:VA], qsT[:, h, 0:m], state[:, h, :], start=True, stop=False)
                        ins = pe.matmul(acc[0:m, h, 0:VA], decay[0:m, h, 0:m], v[0:m, mix.slot, h, :], start=False, stop=True)
                    ins.then_inc(num_ps, 1)

            rounds(pe, body, NT + 1)

        @block.vector
        def _(dve):
            def norm(t):
                slot_loaded(dve, x_in, t)
                xt = x[0:t.n, t.slot, :]
                norm_rows(dve, normed, rooted, t.i, xt, gmix[0:t.n, :], xt, stats[0:t.n], ms[0:t.n])

            def split_h(t):
                all_of(dve, h_hi, t.i)
                dve.tensor_tensor(hT_lo[:, t.slot, :, 0:t.n], turned[:, :, 0:t.n], hT_hi[:, t.slot, :, 0:t.n], ALU.subtract).then_inc(h_lo, 1)

            dve.memset(C[:], 0.0)
            dve.memset(v[:, :, :, QK:VA], 1.0)
            dve.memset(m_rows[:], 0.0)
            dve.memset(ones_row[:], 1.0)
            dve.memset(zero_row[:], 0.0)
            dve.wait_ge(ident_made, 4)
            dve.wait_ge(consts_in, 16 * N_CONST)
            dve.tensor_copy(pick[:], ident[0:HEADS, 0:HEADS].unsqueeze(2).to_broadcast([HEADS, HEADS, P])).then_inc(const_sb, 1)
            dve.wait_ge(const_sb, 1)
            norm(tile_at(0, 0))
            norm(tile_at(1, 1))
            split_h(tile_at(0, 0))
            for n in range(PIECES * KC):
                c, col, raw = n // PIECES, n % PIECES * PC, n % 2
                dve.wait_ge(w_hi_made, n + 1)
                dve.tensor_tensor(w_lo[:, c, col:col + PC], w_raw[:, raw, :], w_hi[:, c, col:col + PC],
                                  ALU.subtract).then_inc(w_lo_made, 1)

            def body(r, slot):
                i, j = r, r - 1
                cur, mix = tile_at(i, slot), tile_at(j, 1 - slot)
                n, m = cur.n, mix.n
                step = i * ROW_STEPS
                if exists(i):
                    all_of(dve, gates_ps, i)
                    dve.tensor_copy(gates[0:n, :], GATES[0:n, :]).then_inc(gates_sb, 1)
                if exists(j):
                    all_of(dve, cols_ps, j)
                    dve.tensor_copy(cols[0:m, 0:12], COLS[0:m, 0:12]).then_inc(cols_sb, 1)
                    dve.tensor_copy(cols[:, 12:16], COLS[:, 12:16]).then_inc(cols_sb, 1)
                    all_of(dve, num_ps, j - 1)
                    dve.scalar_tensor_tensor(decay[0:m, :, 0:m], wide[0:m, :, 0:m], -1.0,
                                             causal[0:m, 0:m].unsqueeze(1).to_broadcast([m, HEADS, m]), ALU.mult, ALU.add).then_inc(masked, 1)
                if exists(r + 1):
                    split_h(tile_at(r + 1, 1 - slot))
                if exists(j):
                    all_of(dve, qk_turned, j)
                    dve.tensor_copy(kT[:, :, 0:m], turned[:, HEADS:2 * HEADS, 0:m]).then_inc(kT_sb, 1)
                    all_of(dve, cols_sb, j, 2)
                    qv = q[0:m, mix.slot, :].rearrange("p (h d) -> p h d", h=HEADS)
                    dve.tensor_tensor(qv, qv, cols[0:m, 4:8].unsqueeze(2).to_broadcast([m, HEADS, QK]), ALU.mult).then_inc(q_scaled, 1)
                    all_of(dve, decayed, j)
                    kv = k[0:m, mix.slot, :].rearrange("p (h d) -> p h d", h=HEADS)
                    dve.tensor_tensor(kv, kv, decay[0:m, :, m - 1:m].to_broadcast([m, HEADS, QK]), ALU.mult).then_inc(k_scaled, 1)
                if exists(i):
                    all_of(dve, rows_ps, i)
                    all_of(dve, cols_ps, i - 1)
                    dve.tensor_scalar(rows[:, F_ROW, 0:n], ROWS[:, P:P + n], gbias[:, 1:2], None, ALU.add).then_inc(row_step, 1)
                    dve.wait_ge(row_step, step + 1)
                    dve.scalar_tensor_tensor(rows[:, F_ABS, 0:n], rows[:, F_ROW, 0:n], -1.0, rows[:, F_ROW, 0:n], ALU.mult, ALU.max).then_inc(row_step, 1)
                    dve.tensor_scalar(rows[:, I_ROW, 0:n], ROWS[:, 0:n], gbias[:, 0:1], None, ALU.add).then_inc(row_step, 1)
                    all_of(dve, v_ps, i)
                    dve.tensor_copy(v[0:n, slot, :, 0:QK], proj[0][0:n, :].rearrange("p (h d) -> p h d", h=HEADS)).then_inc(v_sb, 1)
                if exists(j):
                    all_of(dve, scores_ps, j)
                    all_of(dve, k_scaled, j)
                    dve.tensor_tensor(decay[0:m, :, 0:m], decay[0:m, :, 0:m], wide[0:m, :, 0:m], ALU.mult).then_inc(weighted, 1)
                    all_of(dve, state_ps, j)
                    all_of(dve, C_moved, j - 1)
                    if isinstance(j, int) and j == NT:
                        dve.wait_ge(state_out, 16 * 3)
                    state = C if m == P else C_dec
                    for h in range(HEADS):
                        ins = dve.scalar_tensor_tensor(C_new[:, h, :], state[:, h, :], cols[:, 12 + h:13 + h], acc[:, h, 0:VA], ALU.mult, ALU.add)
                    ins.then_inc(C_made, 1)
                if exists(i):
                    reached(dve, row_act, i * ROW_ACTS + 2)
                    dve.scalar_tensor_tensor(rows[:, LF, 0:n], rows[:, F_ROW, 0:n], 0.0, rows[:, LOG1P, 0:n], ALU.min, ALU.subtract).then_inc(row_step, 1)
                    dve.wait_ge(row_step, step + 4)
                    dve.tensor_tensor_scan(rows[:, B, 0:n], ones_row[:, 0:n], rows[:, LF, 0:n], 0.0, ALU.mult, ALU.add).then_inc(row_step, 1)
                    dve.wait_ge(row_step, step + 5)
                    dve.tensor_tensor(rows[:, G, 0:n], rows[:, I_ROW, 0:n], rows[:, B, 0:n], ALU.subtract).then_inc(row_step, 1)
                    dve.wait_ge(row_step, step + 6)
                    m_in = m_dec[:] if n < P else m_rows[:, 1 - slot, P - 1:P]
                    dve.tensor_tensor_scan(rows[:, U, 0:n], zero_row[:, 0:n], rows[:, G, 0:n], m_in, ALU.add, ALU.max).then_inc(row_step, 1)
                    dve.wait_ge(row_step, step + 7)
                    dve.tensor_tensor(m_rows[:, slot, 0:n], rows[:, B, 0:n], rows[:, U, 0:n], ALU.add).then_inc(row_step, 1)
                if exists(r + 2):
                    all_of(dve, h_turned, r)
                    norm(tile_at(r + 2, slot))
                if exists(j):
                    base = j * FIN_STEPS
                    all_of(dve, num_ps, j)
                    ho = heads_out[0:m, :].rearrange("p (h d) -> p h d", h=HEADS)
                    f = lambda a: fin[0:m, a, :]
                    all_of(dve, squared, j)
                    dve.tensor_tensor(f(0), acc[0:m, :, QK], cols[0:m, 8:12], ALU.max).then_inc(fin_step, 1)
                    dve.wait_ge(fin_step, base + 1)
                    dve.scalar_tensor_tensor(f(1), acc[0:m, :, QK], -1.0, f(0), ALU.mult, ALU.max).then_inc(fin_step, 1)
                    dve.wait_ge(fin_step, base + 2)
                    dve.reciprocal(f(2), f(1)).then_inc(fin_step, 1)
                    dve.wait_ge(fin_step, base + 3)
                    dve.tensor_tensor(f(4), f(3), f(2), ALU.mult).then_inc(fin_step, 1)
                    dve.wait_ge(fin_step, base + 4)
                    dve.scalar_tensor_tensor(f(5), f(4), 1.0 / QK, f(2), ALU.mult, ALU.mult).then_inc(fin_step, 1)
                    dve.wait_ge(fin_step, base + 5)
                    dve.tensor_scalar(f(6), f(5), EPS, None, ALU.add).then_inc(fin_step, 1)
                    all_of(dve, heads_rooted, j)
                    dve.tensor_tensor(f(7), f(3), f(2), ALU.mult).then_inc(fin_step, 1)
                    all_of(dve, o_sb, j)
                    ot = o[0:m, mix.slot, :]
                    dve.tensor_scalar(ot, ot, 1.0, None, ALU.add).then_inc(fin_step, 1)
                    dve.wait_ge(fin_step, base + 8)
                    dve.reciprocal(ot, ot).then_inc(fin_step, 1)
                    all_of(dve, out_done, j - 1, 16)
                    dve.tensor_tensor(ho, acc[0:m, :, 0:QK], f(7).unsqueeze(2).to_broadcast([m, HEADS, QK]), ALU.mult).then_inc(fin_step, 1)
                    dve.wait_ge(fin_step, base + 10)
                    dve.tensor_tensor(heads_out[0:m, :], heads_out[0:m, :], ghead[0:m, :], ALU.mult).then_inc(fin_step, 1)
                    dve.wait_ge(fin_step, base + 11)
                    dve.tensor_tensor(heads_out[0:m, :], heads_out[0:m, :], ot, ALU.mult).then_inc(fin_step, 1)

            rounds(dve, body, NT + 1)


def attention_phase(nc, x_prompt, x_sample, g_mix, w_in, sinks, w_out, cache_k, cache_v, mixed, x_mid,
                    out_k, out_v):
    QKV = AW + 2 * KVW
    PREV, CUR = 0, 1
    SCALE = HD ** -0.5
    with ExitStack() as ctx:
        def sb(name, shape, dt=F32):
            return ctx.enter_context(nc.sbuf_tensor("a_" + name, shape, dt))

        def ps(name, shape):
            return ctx.enter_context(nc.psum_tensor("a_" + name, shape, F32))

        def sem(name):
            return ctx.enter_context(nc.semaphore("a_" + name))

        def sems(names):
            return [sem(n) for n in names.split()]

        wa_hi, wa_lo = sb("wa_hi", [P, KC, QKV], F32R), sb("wa_lo", [P, KC, QKV], F32R)
        wo_hi, wo_lo = sb("wo_hi", [P, KC, D], F32R), sb("wo_lo", [P, KC, D], F32R)
        w_raw = sb("w_raw", [P, 2, D])
        x, x_sum = sb("x", [P, 2, D]), sb("x_sum", [P, 2, D])
        gmix = sb("gmix", [P, D])
        hT_hi, hT_lo = sb("hT_hi", [P, 2, KC, P], F32R), sb("hT_lo", [P, 2, KC, P], F32R)
        mixT_hi, mixT_lo = sb("mixT_hi", [P, KC, P], F32R), sb("mixT_lo", [P, KC, P], F32R)
        heads_in, att = sb("heads_in", [P, 2, MW]), sb("att", [P, 2, AW])
        q, kv = sb("q", [P, AW]), sb("kv", [P, 2, 2 * KVW])
        v_prev = sb("v_prev", [P, KVW])
        ck, cv = sb("ck", [P, KVW]), sb("cv", [P, KVW])
        qT = sb("qT", [P, GRP, P])
        kT, ckT = sb("kT", [P, 2, P]), sb("ckT", [P, P])
        s = sb("s", [P, KVH, GRP, 2 * P])
        sT = sb("sT", [P, KVH, 2, GRP, P])
        bias = sb("bias", [P, AH, 2 * P])
        dist = sb("dist", [P, 2 * P])
        sink = sb("sink", [P, AH])
        mx = sb("mx", [P, KVH, 7, GRP])
        MAX, TOP, NEG, SINK, SUM, SINK_EXP, DEN = range(7)
        ident = sb("ident", [P, P])
        stats, ms, minus_half = sb("stats", [P, 2, 6]), sb("ms", [P, 8]), sb("minus_half", [P, 1])

        proj = [ps("proj0", [P, NB]), ps("proj1", [P, NB])]
        turned = ps("turned", [P, KC, P])
        scores = ps("scores", [P, GRP, 2 * P])
        out_ps = [ps("out0", [P, NB]), ps("out1", [P, NB])]

        made, consts_in, const_sb, cache_turned, cache_out, last_out = sems("made consts_in const_sb cache_turned cache_out last_out")
        w_in_sem, (w_hi_made, w_lo_made) = sems("w_raw0 w_raw1"), sems("w_hi_made w_lo_made")
        x_in, heads_loaded, x_sum_in = sems("x_in0 x_in1"), sems("heads_in0 heads_in1"), sems("x_sum_in0 x_sum_in1")
        normed, rooted, h_turned, h_hi, h_lo = sems("normed rooted h_turned h_hi h_lo")
        q_ps, kv_ps, o0_ps, o1_ps, q_sb, kv_sb, v_kept = sems("q_ps kv_ps o0_ps o1_ps q_sb kv_sb v_kept")
        qk_turned, qT_sb, kT_sb = sems("qk_turned qT_sb kT_sb")
        scores_ps, soft, exps, s_turned, sT_sb, out_done, averaged = sems("scores_ps soft exps s_turned sT_sb out_done averaged")
        mix_turned, mix_hi, mix_lo, added, x_out = sems("mix_turned mix_hi mix_lo added x_out")
        SOFT, AVG, N_CONST = 5, 3, 4
        W_PIECES = 2 * KC

        def keys(t, part):
            return 0 if part == PREV and isinstance(t.i, int) and t.i == 0 else P if part == PREV else t.n

        def parts(t):
            return [p for p in (PREV, CUR) if keys(t, p)]

        def key_span(t):
            return (0 if keys(t, PREV) else P), P + t.n

        block = ctx.enter_context(nc.Block())

        @block.sync
        def _(sp):
            sp.dma_start(x[:, 0, :], x_prompt[0:P, :]).then_inc(x_in[0], 16)
            sp.dma_start(x[:, 1, :], x_prompt[P:2 * P, :]).then_inc(x_in[1], 16)
            sp.dma_start(gmix[:], g_mix.partition_broadcast(P)).then_inc(consts_in, 16)
            sp.dma_start(sink[:], sinks.partition_broadcast(P)).then_inc(consts_in, 16)
            sp.dma_start(ck[:], cache_k).then_inc(consts_in, 16)
            sp.dma_start(cv[:], cache_v).then_inc(consts_in, 16)
            for n in range(W_PIECES):
                c, raw = n % KC, n % 2
                reached(sp, w_lo_made, n - 1)
                width = QKV if n < KC else D
                src = w_in[c * P:(c + 1) * P, Q_COL:Q_COL + QKV] if n < KC else w_out[c * P:(c + 1) * P, :]
                sp.dma_start(w_raw[:, raw, 0:width], src).then_inc(w_in_sem[raw], 16)
            sp.dma_start(out_k[1][0:P - DEC, :], cache_k[DEC:P, :]).then_inc(cache_out, 16)
            sp.dma_start(out_v[1][0:P - DEC, :], cache_v[DEC:P, :]).then_inc(cache_out, 16)

            def body(r, slot):
                if exists(r + 2):
                    nxt = tile_at(r + 2, slot)
                    src = x_sample if nxt.n < P else x_prompt[token_rows(sp, nxt.i, P), :]
                    all_of(sp, h_turned, r)
                    sp.dma_start(x[0:nxt.n, nxt.slot, :], src).then_inc(x_in[slot], 16)
                if exists(r):
                    cur = tile_at(r, slot)
                    all_of(sp, mix_turned, r - 2)
                    sp.dma_start(heads_in[0:cur.n, slot, :], mixed[token_rows(sp, r, cur.n), :]).then_inc(heads_loaded[slot], 16)
                if exists(r - 2):
                    t = tile_at(r - 2, slot)
                    all_of(sp, added, t.i, 2)
                    sp.dma_start(x_mid[token_rows(sp, t.i, t.n), :], x_sum[0:t.n, slot, :]).then_inc(x_out, 16)
                    all_of(sp, x_out, t.i, 16)
                if exists(r):
                    src = x_sample if cur.n < P else x_prompt[token_rows(sp, r, P), :]
                    sp.dma_start(x_sum[0:cur.n, slot, :], src).then_inc(x_sum_in[slot], 16)
                if isinstance(r, int) and NT - 1 <= r <= NT:
                    which, rows = r - (NT - 1), tile_at(r, slot).n
                    all_of(sp, kv_sb, r)
                    sp.dma_start(out_k[which][P - rows:P, :], kv[0:rows, slot, 0:KVW]).then_inc(last_out, 16)
                    sp.dma_start(out_v[which][P - rows:P, :], kv[0:rows, slot, KVW:]).then_inc(last_out, 16)

            rounds(sp, body, NT + 2)
            sp.wait_ge(cache_out, 32)
            sp.wait_ge(last_out, 64)

        @block.gpsimd
        def _(pool):
            make_identity(pool, ident[:], made)
            pool.memset(minus_half[:], -0.5).then_inc(made, 1)
            pool.iota(dist[:], pattern=[[-1, 2 * P]], base=P, channel_multiplier=1,
                      allow_small_or_imprecise_dtypes=True).then_inc(made, 1)
            pool.wait_ge(made, 4)

            def root(t):
                norm_root(pool, normed, rooted, t.i, ms[0:t.n], minus_half[0:t.n])

            root(tile_at(0, 0))
            root(tile_at(1, 1))

            def body(r, slot):
                if exists(r + 2):
                    root(tile_at(r + 2, slot))

            rounds(pool, body, NT - 2)

        @block.scalar
        def _(act):
            def split_h(t):
                all_of(act, h_turned, t.i)
                all_of(act, kv_ps, t.i - 2)
                act.activation(hT_hi[:, t.slot, :, 0:t.n], turned[:, :, 0:t.n], ACT.Copy).then_inc(h_hi, 1)

            split_h(tile_at(0, 0))
            for n in range(W_PIECES):
                c, raw = n % KC, n % 2
                act.wait_ge(w_in_sem[raw], 16 * (n // 2 + 1))
                dst, width = (wa_hi, QKV) if n < KC else (wo_hi, D)
                act.activation(dst[:, c, :], w_raw[:, raw, 0:width], ACT.Copy).then_inc(w_hi_made, 1)

            def exponentials(t, g):
                lo, hi = key_span(t)
                reached(act, soft, (t.i * 2 + g) * SOFT + 4)
                for h in range(GRP):
                    part = s[0:t.n, g, h, lo:hi]
                    ins = act.activation(part, part, ACT.Exp, bias=mx[0:t.n, g, NEG, h:h + 1], accum_out=mx[0:t.n, g, SUM, h:h + 1])
                ins.then_inc(exps, 1)
                reached(act, soft, (t.i * 2 + g) * SOFT + 5)
                act.activation(mx[0:t.n, g, SINK_EXP, :], mx[0:t.n, g, SINK, :], ACT.Exp).then_inc(exps, 1)

            def copy_turned(t, g):
                reached(act, s_turned, t.i * 2 + g + 1)
                for p in parts(t):
                    n = keys(t, p)
                    ins = act.activation(sT[0:n, g, p, :, 0:t.n], turned[0:n, p * GRP:(p + 1) * GRP, 0:t.n], ACT.Copy)
                ins.then_inc(sT_sb, 1)

            def body(r, slot):
                cur, mid, old = tile_at(r, slot), tile_at(r - 1, 1 - slot), tile_at(r - 2, slot)
                if exists(mid.i):
                    exponentials(mid, 0)
                if exists(cur.i):
                    all_of(act, q_ps, r)
                    all_of(act, qk_turned, r - 1)
                    act.activation(q[0:cur.n, :].rearrange("p (h g d) -> p g h d", g=KVH, h=GRP),
                                   proj[0][0:cur.n, :].rearrange("p (g h d) -> p g h d", g=KVH, h=GRP), ACT.Copy).then_inc(q_sb, 1)
                if exists(old.i):
                    all_of(act, mix_turned, old.i)
                    all_of(act, o1_ps, old.i - 1)
                    act.activation(mixT_hi[:, :, 0:old.n], turned[:, :, 0:old.n], ACT.Copy).then_inc(mix_hi, 1)
                if exists(r + 1):
                    split_h(tile_at(r + 1, 1 - slot))
                if exists(mid.i):
                    copy_turned(mid, 0)
                    exponentials(mid, 1)
                if exists(cur.i):
                    all_of(act, qk_turned, r)
                    act.activation(qT[:, :, 0:cur.n], turned[:, 0:GRP, 0:cur.n], ACT.Copy).then_inc(qT_sb, 1)
                if exists(mid.i):
                    copy_turned(mid, 1)

            rounds(act, body, NT + 2)

        @block.tensor
        def _(pe):
            pe.wait_ge(made, 2)

            def turn(t, src, done):
                for c in range(KC):
                    ins = pe.transpose(turned[:, c, 0:t.n], src(c), ident[0:t.n, 0:t.n])
                ins.then_inc(done, 1)

            def turn_h(t):
                all_of(pe, normed, t.i, NORM)
                turn(t, lambda c: x[0:t.n, t.slot, c * P:(c + 1) * P], h_turned)

            def project(out, t, c0, width, chunks):
                return split_product(pe, out, (lambda c: hT_hi[:, t.slot, c, :], lambda c: hT_lo[:, t.slot, c, :]),
                                     (lambda c: wa_hi[:, c, c0:c0 + width], lambda c: wa_lo[:, c, c0:c0 + width]),
                                     chunks, chunks[0] == 0, chunks[-1] == KC - 1)

            def project_out(half, chunks):
                cols = slice(half * NB, (half + 1) * NB)
                return split_product(pe, proj[half][:], (lambda c: mixT_hi[:, c, :], lambda c: mixT_lo[:, c, :]),
                                     (lambda c: wo_hi[:, c, cols], lambda c: wo_lo[:, c, cols]),
                                     chunks, chunks[0] == 0, chunks[-1] == KC - 1)

            def score(t, g):
                head = slice(g * HD, (g + 1) * HD)
                reached(pe, soft, (t.i * 2 + g - 1) * SOFT + 1)
                for h in range(GRP):
                    for p in parts(t):
                        n = keys(t, p)
                        kk = kT[head, t.slot, 0:n] if p == CUR else ckT[head, :] if t.n < P else kT[head, 1 - t.slot, :]
                        ins = pe.matmul(scores[0:t.n, h, p * P:p * P + n], qT[head, h, 0:t.n], kk, start=True, stop=True)
                ins.then_inc(scores_ps, 1)

            def turn_s(t, g):
                reached(pe, exps, (t.i * 2 + g) * 2 + 1)
                for p in parts(t):
                    n = keys(t, p)
                    for h in range(GRP):
                        ins = pe.transpose(turned[0:n, p * GRP + h, 0:t.n], s[0:t.n, g, h, p * P:p * P + n], ident[0:t.n, 0:t.n])
                ins.then_inc(s_turned, 1)

            def average(t, g):
                reached(pe, sT_sb, t.i * 2 + g + 1)
                reached(pe, averaged, ((t.i - 1) * 2 + g + 1) * AVG)
                for h in range(GRP):
                    for p in parts(t):
                        n = keys(t, p)
                        vals = kv[0:n, t.slot, KVW + g * HD:KVW + (g + 1) * HD] if p == CUR else (cv if t.n < P else v_prev)[:, g * HD:(g + 1) * HD]
                        ins = pe.matmul(out_ps[g][0:t.n, h * HD:(h + 1) * HD], sT[0:n, g, p, h, 0:t.n], vals,
                                        start=p == parts(t)[0], stop=p == CUR)
                ins.then_inc(out_done, 1)

            first, second = range(KC // 2), range(KC // 2, KC)
            turn_h(tile_at(0, 0))
            pe.wait_ge(const_sb, 1)
            pe.transpose(scores[:, 0, 0:P], ck[:], ident[:]).then_inc(cache_turned, 1)
            pe.wait_ge(const_sb, 2)

            def body(r, slot):
                cur, mid, old = tile_at(r, slot), tile_at(r - 1, 1 - slot), tile_at(r - 2, slot)
                if exists(mid.i):
                    all_of(pe, qT_sb, mid.i)
                    all_of(pe, kT_sb, mid.i)
                    score(mid, 0)
                if exists(cur.i):
                    if isinstance(r, int) and r == 0:
                        pe.wait_ge(w_lo_made, KC)
                    all_of(pe, h_lo, r)
                    reached(pe, added, (r - 3) * 2 + 1)
                    project(proj[0][:], cur, 0, AW, first)
                if exists(old.i):
                    average(old, 1)
                if exists(cur.i):
                    project(proj[0][:], cur, 0, AW, second).then_inc(q_ps, 1)
                if exists(old.i):
                    reached(pe, averaged, (old.i + 1) * 2 * AVG)
                    slot_loaded(pe, heads_loaded, old)
                    turn(old, lambda c: (heads_in if c < HEADS else att)[0:old.n, old.slot, c % HEADS * P:(c % HEADS + 1) * P], mix_turned)
                if exists(cur.i):
                    all_of(pe, added, r - 3, 2)
                    project(proj[1][:, 0:2 * KVW], cur, AW, 2 * KVW, range(KC)).then_inc(kv_ps, 1)
                if exists(old.i):
                    all_of(pe, mix_lo, old.i)
                if exists(r + 1):
                    turn_h(tile_at(r + 1, 1 - slot))
                if exists(mid.i):
                    score(mid, 1)
                if isinstance(r, int) and r == 2:
                    pe.wait_ge(w_lo_made, W_PIECES)
                if exists(old.i):
                    all_of(pe, q_sb, r if exists(r) else NT)
                    project_out(0, first)
                if exists(mid.i):
                    if exists(r + 1):
                        all_of(pe, h_lo, r + 1)
                    turn_s(mid, 0)
                if exists(old.i):
                    project_out(0, second).then_inc(o0_ps, 1)
                if exists(mid.i):
                    if exists(cur.i):
                        reached(pe, v_kept, r - 1)
                    average(mid, 0)
                if exists(old.i):
                    all_of(pe, kv_sb, r if exists(r) else NT)
                    project_out(1, first)
                if exists(cur.i):
                    all_of(pe, q_sb, r)
                    all_of(pe, kv_sb, r)
                    if exists(mid.i):
                        reached(pe, sT_sb, mid.i * 2 + 1)
                    else:
                        all_of(pe, h_lo, r + 1)
                    for h in range(GRP):
                        pe.transpose(turned[:, h, 0:cur.n], q[0:cur.n, h * P:(h + 1) * P], ident[0:cur.n, 0:cur.n])
                    pe.transpose(turned[:, GRP, 0:cur.n], kv[0:cur.n, slot, 0:KVW], ident[0:cur.n, 0:cur.n]).then_inc(qk_turned, 1)
                if exists(old.i):
                    project_out(1, second).then_inc(o1_ps, 1)
                if exists(mid.i):
                    if exists(cur.i):
                        all_of(pe, qT_sb, r)
                        all_of(pe, kT_sb, r)
                    else:
                        reached(pe, sT_sb, mid.i * 2 + 1)
                    turn_s(mid, 1)

            rounds(pe, body, NT + 2)

        @block.vector
        def _(dve):
            def norm(t):
                slot_loaded(dve, x_in, t)
                xt = x[0:t.n, t.slot, :]
                norm_rows(dve, normed, rooted, t.i, xt, gmix[0:t.n, :], xt, stats[0:t.n], ms[0:t.n])

            def split(i, hi_made, lo, hi, n, lo_made):
                all_of(dve, hi_made, i)
                dve.tensor_tensor(lo, turned[:, :, 0:n], hi, ALU.subtract).then_inc(lo_made, 1)

            def split_h(t):
                split(t.i, h_hi, hT_lo[:, t.slot, :, 0:t.n], hT_hi[:, t.slot, :, 0:t.n], t.n, h_lo)

            def soften(t, g):
                n, (lo, hi) = t.n, key_span(t)
                base = (t.i * 2 + g) * SOFT
                f = lambda a: mx[0:n, g, a, :]
                heads = slice(g * GRP, (g + 1) * GRP)
                reached(dve, scores_ps, t.i * 2 + g + 1)
                reached(dve, s_turned, (t.i - 1) * 2 + g + 1)
                dve.scalar_tensor_tensor(s[0:n, g, :, lo:hi], scores[0:n, :, lo:hi], SCALE, bias[0:n, heads, lo:hi], ALU.mult, ALU.add).then_inc(soft, 1)
                dve.wait_ge(soft, base + 1)
                dve.reduce_max(f(MAX), s[0:n, g, :, lo:hi], AX.X).then_inc(soft, 1)
                dve.wait_ge(soft, base + 2)
                dve.tensor_tensor(f(TOP), f(MAX), sink[0:n, heads], ALU.max).then_inc(soft, 1)
                dve.wait_ge(soft, base + 3)
                reached(dve, exps, ((t.i - 1) * 2 + g + 1) * 2)
                dve.tensor_scalar(f(NEG), f(TOP), -1.0, None, ALU.mult).then_inc(soft, 1)
                dve.tensor_tensor(f(SINK), sink[0:n, heads], f(TOP), ALU.subtract).then_inc(soft, 1)

            def divide(t, g):
                n, base = t.n, (t.i * 2 + g) * AVG
                f = lambda a: mx[0:n, g, a, :]
                reached(dve, exps, (t.i * 2 + g + 1) * 2)
                dve.tensor_tensor(f(DEN), f(SUM), f(SINK_EXP), ALU.add).then_inc(averaged, 1)
                dve.wait_ge(averaged, base + 1)
                dve.reciprocal(f(DEN), f(DEN)).then_inc(averaged, 1)
                dve.wait_ge(averaged, base + 2)
                reached(dve, out_done, t.i * 2 + g + 1)
                all_of(dve, mix_turned, t.i - 2)
                dst = att[0:n, t.slot, g * GRP * HD:(g + 1) * GRP * HD].rearrange("p (h d) -> p h d", h=GRP)
                dve.tensor_tensor(dst, out_ps[g][0:n, 0:GRP * HD].rearrange("p (h d) -> p h d", h=GRP),
                                  f(DEN).unsqueeze(2).to_broadcast([n, GRP, HD]), ALU.mult).then_inc(averaged, 1)

            def add(t, half):
                cols = slice(half * NB, (half + 1) * NB)
                all_of(dve, (o0_ps, o1_ps)[half], t.i)
                dve.tensor_tensor(x_sum[0:t.n, t.slot, cols], x_sum[0:t.n, t.slot, cols], proj[half][0:t.n, :], ALU.add).then_inc(added, 1)

            dve.wait_ge(made, 4)
            dve.wait_ge(consts_in, 16 * N_CONST)
            dve.scalar_tensor_tensor(dist[:], dist[:], -1.0, dist[:], ALU.mult, ALU.max).then_inc(const_sb, 1)
            norm(tile_at(0, 0))
            norm(tile_at(1, 1))
            split_h(tile_at(0, 0))
            dve.wait_ge(cache_turned, 1)
            dve.tensor_copy(ckT[:], scores[:, 0, 0:P]).then_inc(const_sb, 1)
            dve.wait_ge(const_sb, 2)
            for h in range(AH):
                ins = dve.tensor_scalar(bias[:, h, :], dist[:], -(2.0 ** (-(h + 1) * 8.0 / AH)), None, ALU.mult)
            ins.then_inc(const_sb, 1)
            dve.wait_ge(const_sb, 3)
            dve.memset(bias[0:P // 2, :, P + P // 2:], MASKED)
            dve.memset(bias[P // 2:, :, 0:P // 2], MASKED).then_inc(const_sb, 1)
            dve.wait_ge(const_sb, 4)
            for n in range(W_PIECES):
                c, raw = n % KC, n % 2
                hi, lo, width = (wa_hi, wa_lo, QKV) if n < KC else (wo_hi, wo_lo, D)
                dve.wait_ge(w_hi_made, n + 1)
                dve.tensor_tensor(lo[:, c, :], w_raw[:, raw, 0:width], hi[:, c, :], ALU.subtract).then_inc(w_lo_made, 1)

            def body(r, slot):
                cur, mid, old = tile_at(r, slot), tile_at(r - 1, 1 - slot), tile_at(r - 2, slot)
                if exists(mid.i):
                    soften(mid, 0)
                if exists(old.i):
                    divide(old, 1)
                    split(old.i, mix_hi, mixT_lo[:, :, 0:old.n], mixT_hi[:, :, 0:old.n], old.n, mix_lo)
                if exists(cur.i):
                    all_of(dve, kv_ps, r)
                    if exists(old.i):
                        all_of(dve, out_done, old.i, 2)
                        dve.tensor_copy(v_prev[:], kv[:, slot, KVW:]).then_inc(v_kept, 1)
                        all_of(dve, v_kept, old.i)
                    dve.tensor_copy(kv[0:cur.n, slot, :], proj[1][0:cur.n, 0:2 * KVW]).then_inc(kv_sb, 1)
                if exists(r + 1):
                    split_h(tile_at(r + 1, 1 - slot))
                if exists(mid.i):
                    soften(mid, 1)
                if exists(old.i):
                    slot_loaded(dve, x_sum_in, old)
                    add(old, 0)
                if exists(mid.i):
                    divide(mid, 0)
                if exists(cur.i):
                    all_of(dve, qk_turned, r)
                    dve.tensor_copy(kT[:, slot, 0:cur.n], turned[:, GRP, 0:cur.n]).then_inc(kT_sb, 1)
                if exists(old.i):
                    add(old, 1)
                if exists(r + 2):
                    norm(tile_at(r + 2, slot))

            rounds(dve, body, NT + 2)


def mlp_phase(nc, x_mid, g_mlp, w_up, w_down, x_mlp):
    BLOCKS = FF // MLP_BLOCK
    FC = MLP_BLOCK // P
    HALF = NT // 2
    GT = 4
    GW = GT * P
    TOKENS = HALF * P + DEC
    with ExitStack() as ctx:
        def sb(name, shape, dt=F32):
            return ctx.enter_context(nc.sbuf_tensor("f_" + name, shape, dt))

        def ps(name, shape):
            return ctx.enter_context(nc.psum_tensor("f_" + name, shape, F32))

        def sems(names):
            return [ctx.enter_context(nc.semaphore("f_" + n)) for n in names.split()]

        acc = sb("acc", [P, HALF + 1, D])
        h_even = sb("h", [P, D])
        hT_hi, hT_lo = sb("hT_hi", [P, KC, TOKENS], F32R), sb("hT_lo", [P, KC, TOKENS], F32R)
        gmlp = sb("gmlp", [P, D])
        up_hi, up_lo = sb("up_hi", [P, 2, KC, MLP_BLOCK], F32R), sb("up_lo", [P, 2, KC, MLP_BLOCK], F32R)
        down_hi, down_lo = sb("down_hi", [P, 2, FC, D], F32R), sb("down_lo", [P, 2, FC, D], F32R)
        raw = sb("raw", [P, 2, D])
        u = sb("u", [P, FC, GW])
        uT_hi, uT_lo = sb("uT_hi", [P, 2, FC, GW], F32R), sb("uT_lo", [P, 2, FC, GW], F32R)
        us_hi, us_lo = sb("us_hi", [P, FC, P], F32R), sb("us_lo", [P, FC, P], F32R)
        h = [h_even[:], u[:].rearrange("p f t -> p (f t)")]
        ident = sb("ident", [P, P])
        stats, ms, minus_half = sb("stats", [P, 2, 6]), sb("ms", [P, 8]), sb("minus_half", [P, 1])

        up_ps = [ps("up0", [P, FC, GW]), ps("up1", [P, FC, GW])]
        down_ps = [ps("down0", [P, D]), ps("down1", [P, D])]

        raw_in, (w_hi_made, w_lo_made) = sems("raw_in0 raw_in1"), sems("w_hi_made w_lo_made")
        made, gain_in, acc_out, cleared = sems("made gain_in acc_out cleared")
        acc_in = sems(" ".join(f"acc_in{n}" for n in range(HALF + 1)))
        normed, rooted, h_turned, h_hi, h_lo = sems("normed rooted h_turned h_hi h_lo")
        up_done, rectified, squared, u_hi, u_lo, down_done, added = sems("up_done rectified squared u_hi u_lo down_done added")
        PIECES = 8

        def quarter(slot, n, up, down):
            if n < 2:
                return up[:, slot, n * KC // 2:(n + 1) * KC // 2, :].rearrange("p c f -> p (c f)")
            return down[:, slot, n - 2, :]

        def tiles(half):
            return [(n, tile_at(half * HALF + n, n % 2)) for n in range(HALF + half)]

        def groups(half):
            return [(0, GT, GW), (GT, GT, GW)] + ([(HALF, 1, DEC)] if half else [])

        def up_count(half, b, g):
            n = len(groups(half))
            return b * n + (g + 1 - half * BLOCKS * (n - 2))

        def down_count(half, b, n):
            per = HALF + half
            return b * per + (n + 1 - half * BLOCKS)

        def blocks(eng, half, body):
            first, last = half * BLOCKS, (half + 1) * BLOCKS - 1
            body(first, 0, first + 1)
            with eng.Fori(0, (BLOCKS - 2) // 2) as turn:
                body(turn * 2 + (first + 1), 1, turn * 2 + (first + 2))
                body(turn * 2 + (first + 2), 0, turn * 2 + (first + 3))
            body(last, 1, None if half else last + 1)

        block = ctx.enter_context(nc.Block())

        @block.sync
        def _(sp):
            def load_weights(first_col, b):
                up = w_up[:, first_col].rearrange("(n c p) f -> n p c f", n=2, p=P)
                down = w_down[first_col, :].rearrange("(n p) d -> n p d", p=P)
                for n in range(4):
                    dst = raw[:, n % 2, :]
                    reached(sp, w_lo_made, b * PIECES + 2 * (n - 1))
                    sp.dma_start(dst.rearrange("p (c f) -> p c f", f=MLP_BLOCK) if n < 2 else dst,
                                 up[n] if n < 2 else down[n - 2]).then_inc(raw_in[n % 2], 16)

            def load_tile(n, t):
                sp.dma_start(acc[0:t.n, n, :], x_mid[token_rows(sp, t.i, t.n), :]).then_inc(acc_in[n], 16)

            sp.dma_start(gmlp[:], g_mlp.partition_broadcast(P)).then_inc(gain_in, 16)
            load_tile(*tiles(0)[0])
            load_tile(*tiles(0)[1])
            load_weights(slice(0, MLP_BLOCK), 0)
            for n, t in tiles(0)[2:]:
                load_tile(n, t)
            for half in (0, 1):
                def body(b, slot, nxt):
                    if nxt is None:
                        return
                    if isinstance(nxt, int):
                        c = nxt % BLOCKS * MLP_BLOCK
                        load_weights(slice(c, c + MLP_BLOCK), nxt)
                    else:
                        load_weights(bass.ds((nxt - half * BLOCKS) * MLP_BLOCK, MLP_BLOCK), nxt)

                blocks(sp, half, body)
                for n, t in tiles(half):
                    reached(sp, added, down_count(half, (half + 1) * BLOCKS - 1, n))
                    sp.dma_start(x_mlp[token_rows(sp, t.i, t.n), :], acc[0:t.n, n, :]).then_inc(acc_out, 16)
                    if not half:
                        sp.wait_ge(acc_out, 16 * (n + 1))
                        load_tile(*tiles(1)[n])
                if not half:
                    load_tile(*tiles(1)[HALF])
            sp.wait_ge(acc_out, 16 * (NT + 1))

        @block.gpsimd
        def _(pool):
            make_identity(pool, ident[:], made)
            pool.memset(minus_half[:], -0.5).then_inc(made, 1)
            pool.wait_ge(made, 3)
            for i in range(NT + 1):
                n = tile_at(i, 0).n
                norm_root(pool, normed, rooted, i, ms[0:n], minus_half[0:n])

        @block.scalar
        def _(act):
            def weights_hi(b, slot):
                for n in range(4):
                    reached(act, raw_in[n % 2], b * 32 + 16 * (n // 2 + 1))
                    act.activation(quarter(slot, n, up_hi, down_hi), raw[:, n % 2, :], ACT.Copy).then_inc(w_hi_made, 1)

            weights_hi(0, 0)
            for half in (0, 1):
                for n, t in tiles(half):
                    all_of(act, h_turned, t.i)
                    act.activation(hT_hi[:, :, n * P:n * P + t.n], up_ps[n % 2].rearrange("p c (a t) -> p (c a) t", t=P)[:, :, 0:t.n],
                                   ACT.Copy).then_inc(h_hi, 1)

                def body(b, slot, nxt):
                    for g, (n0, places, width) in enumerate(groups(half)):
                        count = up_count(half, b, g)
                        reached(act, up_done, count)
                        reached(act, u_lo, count - 1)
                        act.activation(u[:, :, 0:width], up_ps[g % 2][:, :, 0:width], ACT.Relu).then_inc(rectified, 1)
                        reached(act, squared, count)
                        reached(act, down_done, down_count(half, b - 1, n0 + places - 1))
                        dst = uT_hi[:, g] if g < 2 else us_hi[:, :, 0:DEC]
                        act.activation(dst, u[:, :, 0:width], ACT.Copy).then_inc(u_hi, 1)
                    if nxt is not None:
                        weights_hi(nxt, 1 - slot)

                blocks(act, half, body)

        @block.tensor
        def _(pe):
            pe.wait_ge(made, 2)
            pe.wait_ge(cleared, 1)
            for half in (0, 1):
                for n, t in tiles(half):
                    all_of(pe, normed, t.i, NORM)
                    if n >= 2:
                        all_of(pe, h_lo, t.i - 2)
                    dst = up_ps[n % 2].rearrange("p c (a t) -> p (c a) t", t=P)
                    for c in range(KC):
                        ins = pe.transpose(dst[:, c, 0:t.n], h[t.i % 2][0:t.n, c * P:(c + 1) * P], ident[0:t.n, 0:t.n])
                    ins.then_inc(h_turned, 1)
                all_of(pe, h_lo, tiles(half)[-1][1].i)

                def body(b, slot, nxt):
                    reached(pe, w_lo_made, b * PIECES + 4)
                    for g, (n0, places, width) in enumerate(groups(half)):
                        if g == 2:
                            reached(pe, rectified, up_count(half, b, 0))
                        cols = slice(n0 * P, n0 * P + width)
                        for f in range(FC):
                            fc = slice(f * P, (f + 1) * P)
                            ins = split_product(pe, up_ps[g % 2][:, f, 0:width],
                                                (lambda c: up_hi[:, slot, c, fc], lambda c: up_lo[:, slot, c, fc]),
                                                (lambda c: hT_hi[:, c, cols], lambda c: hT_lo[:, c, cols]), range(KC))
                        ins.then_inc(up_done, 1)
                    reached(pe, w_lo_made, b * PIECES + PIECES)
                    for g, (n0, places, width) in enumerate(groups(half)):
                        reached(pe, u_lo, up_count(half, b, g))
                        for n in range(n0, n0 + places):
                            if n >= 2:
                                reached(pe, added, down_count(half, b, n - 2))
                            else:
                                last = HALF - 2 if not half or n else HALF
                                reached(pe, added, down_count(half, b - 1, last if n == 0 else HALF - 1))
                            for c in range(D // NB):
                                cols = slice(c * NB, (c + 1) * NB)
                                if g < 2:
                                    at = slice((n - n0) * P, (n - n0 + 1) * P)
                                    lhs = (lambda f: uT_hi[:, g, f, at], lambda f: uT_lo[:, g, f, at])
                                else:
                                    lhs = (lambda f: us_hi[:, f, :], lambda f: us_lo[:, f, :])
                                ins = split_product(pe, down_ps[n % 2][:, cols], lhs,
                                                    (lambda f: down_hi[:, slot, f, cols], lambda f: down_lo[:, slot, f, cols]), range(FC))
                            ins.then_inc(down_done, 1)

                blocks(pe, half, body)

        @block.vector
        def _(dve):
            def weights_lo(b, slot, piece):
                n, cols = piece // 2, slice(piece % 2 * NB, (piece % 2 + 1) * NB)
                if piece % 2 == 0:
                    reached(dve, w_hi_made, b * 4 + n + 1)
                dve.tensor_tensor(quarter(slot, n, up_lo, down_lo)[:, cols], raw[:, n % 2, cols],
                                  quarter(slot, n, up_hi, down_hi)[:, cols], ALU.subtract).then_inc(w_lo_made, 1)

            dve.memset(us_hi[:].bitcast(F32), 0.0)
            dve.memset(us_lo[:].bitcast(F32), 0.0).then_inc(cleared, 1)
            dve.wait_ge(gain_in, 16)
            for half in (0, 1):
                def norm(n, t):
                    dve.wait_ge(acc_in[n], 16 * (half + 1) if n < HALF else 16)
                    all_of(dve, h_turned, t.i - 2)
                    norm_rows(dve, normed, rooted, t.i, acc[0:t.n, n, :], gmlp[0:t.n, :], h[t.i % 2][0:t.n, :], stats[0:t.n], ms[0:t.n])

                def split_h(n, t):
                    all_of(dve, h_hi, t.i)
                    dve.tensor_tensor(hT_lo[:, :, n * P:n * P + t.n], up_ps[n % 2].rearrange("p c (a t) -> p (c a) t", t=P)[:, :, 0:t.n],
                                      hT_hi[:, :, n * P:n * P + t.n], ALU.subtract).then_inc(h_lo, 1)

                for k, (n, t) in enumerate(tiles(half)):
                    norm(n, t)
                    if k:
                        split_h(*tiles(half)[k - 1])
                    elif not half:
                        for piece in range(PIECES):
                            weights_lo(0, 0, piece)
                split_h(*tiles(half)[-1])

                def body(b, slot, nxt):
                    for g, (n0, places, width) in enumerate(groups(half)):
                        count = up_count(half, b, g)
                        part = u[:, :, 0:width]
                        reached(dve, rectified, count)
                        dve.tensor_tensor(part, part, part, ALU.mult).then_inc(squared, 1)
                        reached(dve, u_hi, count)
                        hi, lo = (uT_hi[:, g], uT_lo[:, g]) if g < 2 else (us_hi[:, :, 0:DEC], us_lo[:, :, 0:DEC])
                        dve.tensor_tensor(lo, part, hi, ALU.subtract).then_inc(u_lo, 1)
                    for n, t in tiles(half):
                        reached(dve, down_done, down_count(half, b, n))
                        first = isinstance(b, int) and b == half * BLOCKS
                        reached(dve, added, down_count(half, b - 1, n) if not first else 0)
                        if first:
                            all_of(dve, normed, t.i, NORM)
                        dve.tensor_tensor(acc[0:t.n, n, :], acc[0:t.n, n, :], down_ps[n % 2][0:t.n, :], ALU.add).then_inc(added, 1)
                        if nxt is not None and n < PIECES:
                            weights_lo(nxt, 1 - slot, n)

                blocks(dve, half, body)


def ple_phase(nc, x_mlp, p_prompt, p_sample, g_ple, w_gate, w_proj, g_final, y_prompt, y_sample):
    PC = PLE // P
    with ExitStack() as ctx:
        def sb(name, shape, dt=F32):
            return ctx.enter_context(nc.sbuf_tensor("e_" + name, shape, dt))

        def ps(name, shape):
            return ctx.enter_context(nc.psum_tensor("e_" + name, shape, F32))

        def sems(names):
            return [ctx.enter_context(nc.semaphore("e_" + n)) for n in names.split()]

        wg_hi, wg_lo = sb("wg_hi", [P, KC, D], F32R), sb("wg_lo", [P, KC, D], F32R)
        wp_hi, wp_lo = sb("wp_hi", [P, PC, D], F32R), sb("wp_lo", [P, PC, D], F32R)
        w_raw = sb("w_raw", [P, 2, D])
        x, h, y, gate = sb("x", [P, 2, D]), sb("h", [P, 2, D]), sb("y", [P, 2, D]), sb("gate", [P, D])
        p = sb("p", [P, 2, PLE])
        gple, gfinal = sb("gple", [P, D]), sb("gfinal", [P, D])
        hT_hi, hT_lo = sb("hT_hi", [P, 2, KC, P], F32R), sb("hT_lo", [P, 2, KC, P], F32R)
        pT_hi, pT_lo = sb("pT_hi", [P, 2, PC, P], F32R), sb("pT_lo", [P, 2, PC, P], F32R)
        ident = sb("ident", [P, P])
        stats, ms = sb("stats", [P, 2, 2, 6]), sb("ms", [P, 2, 8])
        minus_half = sb("minus_half", [P, 1])

        turned, p_turned_ps = ps("turned", [P, KC, P]), ps("p_turned", [P, 4, P])
        gate_ps, ple_ps = ps("gate_ps", [P, D]), ps("ple_ps", [P, D])

        made, gains_in, w_hi_made, w_lo_made, y_out = sems("made gains_in w_hi_made w_lo_made y_out")
        w_in_sem, x_in, p_in = sems("w_raw0 w_raw1"), sems("x_in0 x_in1"), sems("p_in0 p_in1")
        normed, rooted, finished, final_rooted = sems("normed rooted finished final_rooted")
        h_turned, h_hi, h_lo, p_turned, p_hi, p_lo = sems("h_turned h_hi h_lo p_turned p_hi p_lo")
        gate_done, ple_done, gated, mixed_in, x_new = sems("gate_done ple_done gated mixed_in x_new")
        W_PIECES = KC + PC

        block = ctx.enter_context(nc.Block())

        @block.sync
        def _(sp):
            def load(r, slot):
                t = tile_at(r, slot)
                src = x_mlp[token_rows(sp, r, t.n), :]
                sp.dma_start(x[0:t.n, slot, :], src).then_inc(x_in[slot], 16)
                src = p_sample if t.n < P else p_prompt[token_rows(sp, r, P), :]
                sp.dma_start(p[0:t.n, slot, :], src).then_inc(p_in[slot], 16)

            load(0, 0)
            sp.dma_start(gple[:], g_ple.partition_broadcast(P)).then_inc(gains_in, 16)
            sp.dma_start(gfinal[:], g_final.partition_broadcast(P)).then_inc(gains_in, 16)
            load(1, 1)
            for n in range(W_PIECES):
                raw = n % 2
                reached(sp, w_lo_made, n - 1)
                src = w_gate[n * P:(n + 1) * P, :] if n < KC else w_proj[(n - KC) * P:(n - KC + 1) * P, :]
                sp.dma_start(w_raw[:, raw, :], src).then_inc(w_in_sem[raw], 16)

            def body(r, slot):
                if exists(r - 1):
                    t = tile_at(r - 1, 1 - slot)
                    all_of(sp, finished, t.i, NORM)
                    dst = y_sample if t.n < P else y_prompt[token_rows(sp, t.i, P), :]
                    sp.dma_start(dst, y[0:t.n, t.slot, :]).then_inc(y_out, 16)
                if exists(r - 1) and exists(r + 1):
                    load(r + 1, 1 - slot)

            rounds(sp, body, NT + 1)
            sp.wait_ge(y_out, 16 * (NT + 1))

        @block.gpsimd
        def _(pool):
            make_identity(pool, ident[:], made)
            pool.memset(minus_half[:], -0.5).then_inc(made, 1)
            pool.wait_ge(made, 3)

            def root(t, sem, root_made, which):
                norm_root(pool, sem, root_made, t.i, ms[0:t.n, which], minus_half[0:t.n])

            root(tile_at(0, 0), normed, rooted, 0)

            def body(r, slot):
                if exists(r + 1):
                    root(tile_at(r + 1, 1 - slot), normed, rooted, 0)
                if exists(r):
                    root(tile_at(r, slot), finished, final_rooted, 1)

            rounds(pool, body, NT)

        @block.scalar
        def _(act):
            def split(t):
                all_of(act, h_turned, t.i)
                all_of(act, gate_done, t.i - 2)
                act.activation(hT_hi[:, t.slot, :, 0:t.n], turned[:, :, 0:t.n], ACT.Copy).then_inc(h_hi, 1)
                all_of(act, p_turned, t.i)
                all_of(act, ple_done, t.i - 2)
                act.activation(pT_hi[:, t.slot, :, 0:t.n], p_turned_ps[:, 0:PC, 0:t.n], ACT.Copy).then_inc(p_hi, 1)

            for n in range(W_PIECES):
                raw = n % 2
                act.wait_ge(w_in_sem[raw], 16 * (n // 2 + 1))
                dst, c = (wg_hi, n) if n < KC else (wp_hi, n - KC)
                act.activation(dst[:, c, :], w_raw[:, raw, :], ACT.Copy).then_inc(w_hi_made, 1)
                if n == 1:
                    split(tile_at(0, 0))

            def body(r, slot):
                if exists(r + 1):
                    split(tile_at(r + 1, 1 - slot))
                t = tile_at(r, slot)
                all_of(act, gate_done, r)
                all_of(act, mixed_in, r - 1)
                act.activation(gate[0:t.n, :], gate_ps[0:t.n, :], ACT.Sigmoid).then_inc(gated, 1)

            rounds(act, body, NT)

        @block.tensor
        def _(pe):
            pe.wait_ge(made, 2)

            def turn(t):
                all_of(pe, normed, t.i, NORM)
                all_of(pe, h_lo, t.i - 1)
                for c in range(KC):
                    ins = pe.transpose(turned[:, c, 0:t.n], h[0:t.n, t.slot, c * P:(c + 1) * P], ident[0:t.n, 0:t.n])
                ins.then_inc(h_turned, 1)
                slot_loaded(pe, p_in, t)
                all_of(pe, p_lo, t.i - 1)
                for c in range(PC):
                    ins = pe.transpose(p_turned_ps[:, c, 0:t.n], p[0:t.n, t.slot, c * P:(c + 1) * P], ident[0:t.n, 0:t.n])
                ins.then_inc(p_turned, 1)

            turn(tile_at(0, 0))
            pe.wait_ge(w_lo_made, W_PIECES)

            def body(r, slot):
                all_of(pe, h_lo, r)
                all_of(pe, p_lo, r)
                all_of(pe, gated, r - 1)
                for c in range(D // NB):
                    cols = slice(c * NB, (c + 1) * NB)
                    ins = split_product(pe, gate_ps[:, cols], (lambda k: hT_hi[:, slot, k, :], lambda k: hT_lo[:, slot, k, :]),
                                        (lambda k: wg_hi[:, k, cols], lambda k: wg_lo[:, k, cols]), range(KC))
                    if c == 0 and exists(r + 1):
                        turn(tile_at(r + 1, 1 - slot))
                ins.then_inc(gate_done, 1)
                all_of(pe, mixed_in, r - 1)
                for c in range(D // NB):
                    cols = slice(c * NB, (c + 1) * NB)
                    ins = split_product(pe, ple_ps[:, cols], (lambda k: pT_hi[:, slot, k, :], lambda k: pT_lo[:, slot, k, :]),
                                        (lambda k: wp_hi[:, k, cols], lambda k: wp_lo[:, k, cols]), range(PC))
                ins.then_inc(ple_done, 1)

            rounds(pe, body, NT)

        @block.vector
        def _(dve):
            def norm(t):
                slot_loaded(dve, x_in, t)
                all_of(dve, h_turned, t.i - 2)
                norm_rows(dve, normed, rooted, t.i, x[0:t.n, t.slot, :], gple[0:t.n, :], h[0:t.n, t.slot, :], stats[0:t.n, 0], ms[0:t.n, 0])

            def split(t):
                all_of(dve, h_hi, t.i)
                dve.tensor_tensor(hT_lo[:, t.slot, :, 0:t.n], turned[:, :, 0:t.n], hT_hi[:, t.slot, :, 0:t.n], ALU.subtract).then_inc(h_lo, 1)
                all_of(dve, p_hi, t.i)
                dve.tensor_tensor(pT_lo[:, t.slot, :, 0:t.n], p_turned_ps[:, 0:PC, 0:t.n], pT_hi[:, t.slot, :, 0:t.n], ALU.subtract).then_inc(p_lo, 1)

            dve.wait_ge(gains_in, 32)
            norm(tile_at(0, 0))
            for n in range(W_PIECES):
                raw = n % 2
                hi, lo, c = (wg_hi, wg_lo, n) if n < KC else (wp_hi, wp_lo, n - KC)
                dve.wait_ge(w_hi_made, n + 1)
                dve.tensor_tensor(lo[:, c, :], w_raw[:, raw, :], hi[:, c, :], ALU.subtract).then_inc(w_lo_made, 1)
                if n == 1:
                    split(tile_at(0, 0))
            norm(tile_at(1, 1))

            def body(r, slot):
                if exists(r + 1):
                    split(tile_at(r + 1, 1 - slot))
                t = tile_at(r, slot)
                n = t.n
                all_of(dve, ple_done, r)
                all_of(dve, gated, r)
                dve.tensor_tensor(h[0:n, slot, :], gate[0:n, :], ple_ps[0:n, :], ALU.mult).then_inc(mixed_in, 1)
                all_of(dve, mixed_in, r)
                dve.tensor_tensor(x[0:n, slot, :], x[0:n, slot, :], h[0:n, slot, :], ALU.add).then_inc(x_new, 1)
                all_of(dve, x_new, r)
                reached(dve, y_out, (r - 1) * 16)
                norm_rows(dve, finished, final_rooted, r, x[0:n, slot, :], gfinal[0:n, :], y[0:n, slot, :], stats[0:n, 1], ms[0:n, 1])
                if exists(r + 2):
                    norm(tile_at(r + 2, slot))

            rounds(dve, body, NT)

def build(nc, x_prompt, x_sample, cache_k, cache_v, state_c, state_n, state_m, p_prompt, p_sample,
          g_mix, w_in, b_igate, b_fgate, g_head, sinks, w_out, g_mlp, w_up, w_down, g_ple,
          w_ple_gate, w_ple_proj, g_final, y_prompt, y_sample, pk, pv, pc, pn, pm, sk, sv, sc, sn, sm):
    mixed = nc.dram_tensor("mixed_heads", [TOK, MW], F32, kind="Internal").ap()
    mlstm_phase(nc, x_prompt[0], x_sample[0], g_mix[0], w_in[0], b_igate[0], b_fgate[0], g_head[0],
                state_c[0, 0], state_n[0, 0], state_m[0, 0], mixed,
                (pc[0, 0], sc[0, 0]), (pn[0, 0], sn[0, 0]), (pm[0, 0], sm[0, 0]))
    flat = lambda a: a[0, 0].rearrange("w h d -> w (h d)")
    x_mid = nc.dram_tensor("x_after_mixers", [TOK, D], F32, kind="Internal").ap()
    attention_phase(nc, x_prompt[0], x_sample[0], g_mix[0], w_in[0], sinks[0], w_out[0], flat(cache_k), flat(cache_v),
                    mixed, x_mid, (flat(pk), flat(sk)), (flat(pv), flat(sv)))
    x_mlp = nc.dram_tensor("x_after_mlp", [TOK, D], F32, kind="Internal").ap()
    mlp_phase(nc, x_mid, g_mlp[0], w_up[0], w_down[0], x_mlp)
    ple_phase(nc, x_mlp, p_prompt[0, 0], p_sample[0, 0], g_ple[0], w_ple_gate[0], w_ple_proj[0], g_final, y_prompt[0], y_sample[0])


_INS = ["x_prompt", "x_sample", "cache_swa_k", "cache_swa_v", "state_mlstm_c", "state_mlstm_n", "state_mlstm_m",
        "p_prompt", "p_sample", "g_mix", "w_in", "b_igate", "b_fgate", "g_head", "attn_sinks", "w_out", "g_mlp",
        "w_up", "w_down", "g_ple", "w_ple_gate", "w_ple_proj", "g_final"]
_STATE = [(1, 1, HEADS, QK, QK), (1, 1, HEADS, QK), (1, 1, HEADS)]
_WINDOW = (1, 1, P, KVH, HD)
_OUTS = [(1, SEQ, D), (1, DEC, D), _WINDOW, _WINDOW, *_STATE, _WINDOW, _WINDOW, *_STATE]


def kernel(**inputs):
    import numpy as _np
    import concourse.bacc as _bacc
    from concourse import mybir as _mybir
    from concourse.bass_utils import run_bass_kernel_spmd as _run

    nc = _bacc.Bacc("TRN2", target_bir_lowering=False, num_devices=1)
    arrays, args = {}, []
    for name in _INS:
        a = _np.ascontiguousarray(inputs[name])
        arrays[f"in_{name}"] = a
        args.append(nc.dram_tensor(f"in_{name}", a.shape, _mybir.dt.from_np(a.dtype), kind="ExternalInput").ap())
    for i, shape in enumerate(_OUTS):
        args.append(nc.dram_tensor(f"out_{i}", shape, _mybir.dt.float32, kind="ExternalOutput").ap())
    build(nc, *args)
    r = _run(nc, [arrays], core_ids=[0])
    return tuple(r.results[0][f"out_{i}"] for i in range(len(_OUTS)))
```

```python
from contextlib import ExitStack
from typing import NamedTuple

import concourse.bass as bass
from concourse import mybir

F32 = mybir.dt.float32
F32R = mybir.dt.float32r
ALU = mybir.AluOpType
ACT = mybir.ActivationFunctionType
AX = mybir.AxisListType

P = 128
D = 1024
KC = D // P
SEQ, DEC = 2048, 32
NT = SEQ // P
TOK = SEQ + DEC
HEADS, QK = 4, 128
VA = QK + 1
MW = HEADS * QK
GATE_COL = 4 * MW
Q_COL = GATE_COL + 2 * HEADS
AH, KVH, HD = 8, 2, 64
GRP = AH // KVH
AW = AH * HD
KV_COL = Q_COL + AW
KVW = KVH * HD
FF = 4 * D
PLE = 256
EPS = 1e-6
MASKED = -1e30
MLP_BLOCK = 256
NB = 512


class Tile(NamedTuple):
    i: object
    slot: int
    n: int


def tile_at(i, slot):
    return Tile(i, slot, DEC if isinstance(i, int) and i == NT else P)


def reached(eng, sem, count):
    if isinstance(count, int) and count <= 0:
        return
    eng.wait_ge(sem, count)


def all_of(eng, sem, i, per=1):
    reached(eng, sem, (i + 1) * per)


def slot_loaded(eng, sems, t):
    reached(eng, sems[t.slot], t.i * 8 + 16 - 8 * t.slot)


def rounds(eng, body, last):
    for r in range(3):
        body(r, r % 2)
    with eng.Fori(0, (NT - 6) // 2) as turn:
        body(turn * 2 + 3, 1)
        body(turn * 2 + 4, 0)
    for r in range(NT - 3, last + 1):
        body(r, r % 2)


def exists(i):
    return not isinstance(i, int) or 0 <= i <= NT


def split_product(eng, out, lhs, rhs, chunks, first=True, last=True):
    (lh, ll), (rh, rl) = lhs, rhs
    for k in chunks:
        f, e = first and k == chunks[0], last and k == chunks[-1]
        eng.matmul(out, lh(k), rh(k), start=f, stop=False)
        eng.matmul(out, lh(k), rl(k), start=False, stop=False)
        ins = eng.matmul(out, ll(k), rh(k), start=False, stop=e)
    return ins


def token_rows(eng, i, n):
    return slice(i * P, i * P + n) if isinstance(i, int) else bass.ds(eng.snap(i * P), n)


def norm_rows(dve, sem, rooted, i, x, gain, out, stats, ms):
    base = i * NORM
    groups = 2 * D // NB
    for c in range(D // NB):
        ins = dve.bn_stats(stats[:, c, :], x[:, c * NB:(c + 1) * NB])
    ins.then_inc(sem, 1)
    by_group = stats.rearrange("p c (g s) -> p (c g) s", s=3)
    mean, spread = by_group[:, :, 1], by_group[:, :, 2]
    dve.wait_ge(sem, base + 1)
    dve.tensor_tensor(ms[:, 0:groups], mean, mean, ALU.mult).then_inc(sem, 1)
    dve.wait_ge(sem, base + 2)
    dve.scalar_tensor_tensor(ms[:, 0:groups], ms[:, 0:groups], float(D // groups), spread, ALU.mult, ALU.add).then_inc(sem, 1)
    dve.wait_ge(sem, base + 3)
    dve.reduce_sum(ms[:, 4:5], ms[:, 0:groups], AX.X).then_inc(sem, 1)
    dve.wait_ge(sem, base + 4)
    dve.tensor_scalar(ms[:, 5:6], ms[:, 4:5], 1.0 / D, EPS, ALU.mult, ALU.add).then_inc(sem, 1)
    all_of(dve, rooted, i)
    dve.scalar_tensor_tensor(out, x, ms[:, 6:7], gain, ALU.mult, ALU.mult).then_inc(sem, 1)


def norm_root(pool, sem, rooted, i, ms, minus_half):
    reached(pool, sem, i * NORM + 5)
    pool.tensor_tensor(ms[:, 6:7], ms[:, 5:6], minus_half, ALU.pow).then_inc(rooted, 1)


def sums_root(pool, summed, rooted, i, ms, constants):
    all_of(pool, summed, i)
    pool.tensor_tensor(ms[:, 1:2], ms[:, 0:1], constants[:, 0:1], ALU.add).then_inc(rooted, 1)
    reached(pool, rooted, i * 2 + 1)
    pool.tensor_tensor(ms[:, 2:3], ms[:, 1:2], constants[:, 1:2], ALU.pow).then_inc(rooted, 1)


NORM = 6


def make_identity(pool, ident, made):
    pool.memset(ident, 0.0).then_inc(made, 1)
    pool.wait_ge(made, 1)
    pool.affine_select(out=ident, in_=ident, compare_op=ALU.not_equal, fill=1.0, base=0,
                       pattern=[[-1, P]], channel_multiplier=1).then_inc(made, 1)


def mlstm_phase(nc, x_prompt, x_sample, g_mix, w_in, b_igate, b_fgate, g_head, state_c, state_n, state_m,
                mixed, out_c, out_n, out_m):
    MC = Q_COL
    PIECES = 4
    PC = MC // PIECES
    with ExitStack() as ctx:
        def sb(name, shape, dt=F32):
            return ctx.enter_context(nc.sbuf_tensor("m_" + name, shape, dt))

        def ps(name, shape):
            return ctx.enter_context(nc.psum_tensor("m_" + name, shape, F32))

        def sem(name):
            return ctx.enter_context(nc.semaphore("m_" + name))

        w_hi, w_lo = sb("w_hi", [P, KC, MC], F32R), sb("w_lo", [P, KC, MC], F32R)
        w_raw = sb("w_raw", [P, 2, PC])
        x = sb("x", [P, 2, D])
        hT_hi, hT_lo = sb("hT_hi", [P, 2, KC, P], F32R), sb("hT_lo", [P, 2, KC, P], F32R)
        gmix = sb("gmix", [P, D])
        q, k = sb("q", [P, 2, MW]), sb("k", [P, 2, MW])
        v, o = sb("v", [P, 2, HEADS, VA]), sb("o", [P, 2, MW])
        qT, kT, qsT = sb("qT", [P, HEADS, P]), sb("kT", [P, HEADS, P]), sb("qsT", [P, HEADS, P])
        decay = sb("decay", [P, HEADS, P])
        C, C_new, C_dec = (sb(n, [P, HEADS, VA]) for n in ("C", "C_new", "C_dec"))
        heads_out = sb("heads_out", [P, MW])
        ghead = sb("ghead", [P, MW])
        causal = sb("causal", [P, P])
        ident = sb("ident", [P, P])
        pick = sb("pick", [HEADS, HEADS, P])
        gates = sb("gates", [P, 2 * HEADS])
        gbias = sb("gbias", [HEADS, 2])
        rows = sb("rows", [HEADS, 8, P])
        m_rows = sb("m_rows", [HEADS, 2, P])
        m_dec = sb("m_dec", [HEADS, 1])
        ones_row, zero_row = sb("ones_row", [HEADS, P]), sb("zero_row", [HEADS, P])
        cols = sb("cols", [P, 16])
        stats, ms = sb("stats", [P, 2, 6]), sb("ms", [P, 8])
        minus_half = sb("minus_half", [P, HEADS])
        fin = sb("fin", [P, 8, HEADS])
        I_ROW, F_ROW, F_ABS, F_EXP, B, G, U, W = range(8)
        LOG1P, LF = F_EXP, F_ROW
        E_ROW = F_ABS

        proj = [ps("proj0", [P, NB]), ps("proj1", [P, NB])]
        turned = ps("turned", [P, KC, P])
        wide = ps("wide", [P, HEADS, P])
        small = ps("small", [P, NB])
        acc = ps("acc", [P, HEADS, 256])
        GATES, ROWS, COLS = small[:, 0:2 * HEADS], small[0:HEADS, 128:384], small[:, 16:32]
        junk = wide

        ident_made, consts_in, const_sb, dec_in = sem("ident_made"), sem("consts_in"), sem("const_sb"), sem("dec_in")
        w_in_sem, w_hi_made, w_lo_made = [sem("w_raw0"), sem("w_raw1")], sem("w_hi_made"), sem("w_lo_made")
        x_in, normed, h_turned = [sem("x_in0"), sem("x_in1")], sem("normed"), sem("h_turned")
        h_hi, h_lo, rooted, heads_rooted = sem("h_hi"), sem("h_lo"), sem("rooted"), sem("heads_rooted")
        gates_ps, gates_sb, rows_ps, row_step, row_act = (sem(n) for n in ("gates_ps", "gates_sb", "rows_ps", "row_step", "row_act"))
        q_ps, k_ps, v_ps, o_ps = (sem(n) for n in ("q_ps", "k_ps", "v_ps", "o_ps"))
        q_sb, k_sb, v_sb, o_sb = (sem(n) for n in ("q_sb", "k_sb", "v_sb", "o_sb"))
        cols_ps, cols_sb, masked, decayed = (sem(n) for n in ("cols_ps", "cols_sb", "masked", "decayed"))
        qk_turned, qT_sb, kT_sb, q_scaled, k_scaled = (sem(n) for n in ("qk_turned", "qT_sb", "kT_sb", "q_scaled", "k_scaled"))
        qs_turned, qsT_sb, scores_ps, state_ps = (sem(n) for n in ("qs_turned", "qsT_sb", "scores_ps", "state_ps"))
        weighted, C_made, C_moved, num_ps, squared, fin_step, out_done, state_out = (
            sem(n) for n in ("weighted", "C_made", "C_moved", "num_ps", "squared", "fin_step", "out_done", "state_out"))
        ROW_STEPS, ROW_ACTS, FIN_STEPS = 8, 4, 12
        N_CONST = 7

        block = ctx.enter_context(nc.Block())

        @block.sync
        def _(sp):
            sp.dma_start(x[:, 0, :], x_prompt[0:P, :]).then_inc(x_in[0], 16)
            sp.dma_start(x[:, 1, :], x_prompt[P:2 * P, :]).then_inc(x_in[1], 16)
            sp.dma_start(gmix[:], g_mix.partition_broadcast(P)).then_inc(consts_in, 16)
            sp.dma_start(gbias[:, 0:1], b_igate.rearrange("(h a) -> h a", a=1)).then_inc(consts_in, 16)
            sp.dma_start(gbias[:, 1:2], b_fgate.rearrange("(h a) -> h a", a=1)).then_inc(consts_in, 16)
            sp.dma_start(ghead[:], g_head.partition_broadcast(P)).then_inc(consts_in, 16)
            sp.dma_start(C_dec[:, :, 0:QK], state_c.rearrange("h d v -> d h v")).then_inc(consts_in, 16)
            sp.dma_start(C_dec[:, :, QK], state_n.rearrange("h d -> d h"), allow_slow_non_contiguous=True).then_inc(consts_in, 16)
            sp.dma_start(m_dec[:], state_m.rearrange("(h a) -> h a", a=1)).then_inc(consts_in, 16)
            for n in range(PIECES * KC):
                c, col, raw = n // PIECES, n % PIECES * PC, n % 2
                reached(sp, w_lo_made, n - 1)
                sp.dma_start(w_raw[:, raw, :], w_in[c * P:(c + 1) * P, col:col + PC]).then_inc(w_in_sem[raw], 16)

            def body(r, slot):
                j = r - 1
                if exists(r + 2):
                    nxt = tile_at(r + 2, slot)
                    src = x_sample if nxt.n < P else x_prompt[token_rows(sp, nxt.i, P), :]
                    all_of(sp, h_turned, r)
                    sp.dma_start(x[0:nxt.n, nxt.slot, :], src).then_inc(x_in[nxt.slot], 16)
                if exists(j):
                    t = tile_at(j, 1 - slot)
                    dst = mixed[token_rows(sp, j, t.n), :]
                    all_of(sp, fin_step, j, FIN_STEPS)
                    sp.dma_start(dst, heads_out[0:t.n, :]).then_inc(out_done, 16)
                if isinstance(j, int) and j >= NT - 1:
                    which = j - (NT - 1)
                    all_of(sp, C_made, j)
                    all_of(sp, row_step, j, ROW_STEPS)
                    n = tile_at(j, 0).n
                    sp.dma_start(out_c[which].rearrange("h d v -> d h v"), C_new[:, :, 0:QK]).then_inc(state_out, 16)
                    sp.dma_start(out_n[which].rearrange("h d -> d h"), C_new[:, :, QK], allow_slow_non_contiguous=True).then_inc(state_out, 16)
                    sp.dma_start(out_m[which].rearrange("(h a) -> h a", a=1), m_rows[:, j % 2, n - 1:n]).then_inc(state_out, 16)

            rounds(sp, body, NT + 1)
            sp.wait_ge(out_done, 16 * (NT + 1))
            sp.wait_ge(state_out, 16 * 6)

        @block.gpsimd
        def _(pool):
            make_identity(pool, ident[:], ident_made)
            pool.memset(causal[:], 0.0).then_inc(ident_made, 1)
            pool.wait_ge(ident_made, 3)
            pool.affine_select(out=causal[:], in_=causal[:], compare_op=ALU.is_ge, fill=MASKED, base=0,
                               pattern=[[1, P]], channel_multiplier=-1).then_inc(ident_made, 1)
            pool.memset(minus_half[:], -0.5).then_inc(ident_made, 1)
            pool.wait_ge(ident_made, 5)

            def root(t):
                norm_root(pool, normed, rooted, t.i, ms[0:t.n], minus_half[0:t.n, 0:1])

            root(tile_at(0, 0))
            root(tile_at(1, 1))

            def body(r, slot):
                if exists(r + 2):
                    root(tile_at(r + 2, slot))
                if exists(r - 1):
                    m = tile_at(r - 1, 1 - slot).n
                    reached(pool, fin_step, (r - 1) * FIN_STEPS + 6)
                    pool.tensor_tensor(fin[0:m, 3, :], fin[0:m, 6, :], minus_half[0:m, :], ALU.pow).then_inc(heads_rooted, 1)

            rounds(pool, body, NT + 1)

        @block.scalar
        def _(act):
            def split_h(t):
                all_of(act, h_turned, t.i)
                all_of(act, o_ps, t.i - 2)
                act.activation(hT_hi[:, t.slot, :, 0:t.n], turned[:, :, 0:t.n], ACT.Copy).then_inc(h_hi, 1)

            split_h(tile_at(0, 0))
            for n in range(PIECES * KC):
                c, col, raw = n // PIECES, n % PIECES * PC, n % 2
                act.wait_ge(w_in_sem[raw], 16 * (n // 2 + 1))
                act.activation(w_hi[:, c, col:col + PC], w_raw[:, raw, :], ACT.Copy).then_inc(w_hi_made, 1)

            def body(r, slot):
                i, j = r, r - 1
                cur, mix = tile_at(i, slot), tile_at(j, 1 - slot)
                n = cur.n
                if exists(i):
                    all_of(act, q_ps, i)
                    act.activation(q[0:n, slot, :], proj[0][0:n, :], ACT.Copy).then_inc(q_sb, 1)
                if exists(r + 1):
                    split_h(tile_at(r + 1, 1 - slot))
                if exists(j):
                    all_of(act, masked, j)
                    all_of(act, cols_sb, j, 2)
                    for h in range(HEADS):
                        ins = act.activation(decay[0:mix.n, h, 0:mix.n], decay[0:mix.n, h, 0:mix.n], ACT.Exp, bias=cols[0:mix.n, h:h + 1])
                    ins.then_inc(decayed, 1)
                if exists(i):
                    all_of(act, k_ps, i)
                    act.activation(k[0:n, slot, :], proj[1][0:n, :], ACT.Copy, scale=QK ** -0.5).then_inc(k_sb, 1)
                if exists(j):
                    all_of(act, qk_turned, j)
                    act.activation(qT[:, :, 0:mix.n], turned[:, 0:HEADS, 0:mix.n], ACT.Copy).then_inc(qT_sb, 1)
                if exists(i):
                    reached(act, row_step, i * ROW_STEPS + 2)
                    act.activation(rows[:, F_EXP, 0:n], rows[:, F_ABS, 0:n], ACT.Exp, scale=-1.0).then_inc(row_act, 1)
                    reached(act, row_act, i * ROW_ACTS + 1)
                    act.activation(rows[:, LOG1P, 0:n], rows[:, F_EXP, 0:n], ACT.Ln, bias=1.0).then_inc(row_act, 1)
                if exists(j):
                    all_of(act, qs_turned, j)
                    act.activation(qsT[:, :, 0:mix.n], turned[:, 0:HEADS, 0:mix.n], ACT.Copy).then_inc(qsT_sb, 1)
                if exists(i):
                    all_of(act, o_ps, i)
                    all_of(act, fin_step, i - 2, FIN_STEPS)
                    act.activation(o[0:n, slot, :], proj[1][0:n, :], ACT.Exp, scale=-1.0).then_inc(o_sb, 1)
                    reached(act, row_step, i * ROW_STEPS + 7)
                    m_in = m_dec[:] if n < P else m_rows[:, 1 - slot, P - 1:P]
                    act.activation(rows[:, W, 0:n], rows[:, U, 0:n], ACT.Exp, scale=-1.0, bias=m_in).then_inc(row_act, 1)
                    reached(act, row_step, i * ROW_STEPS + 8)
                    act.activation(rows[:, E_ROW, 0:n], m_rows[:, slot, 0:n], ACT.Exp, scale=-1.0).then_inc(row_act, 1)
                if exists(j):
                    all_of(act, num_ps, j)
                    reached(act, fin_step, (j - 1) * FIN_STEPS + 7)
                    for h in range(HEADS):
                        ins = act.activation(junk[0:mix.n, h, :], acc[0:mix.n, h, 0:QK], ACT.Square, accum_out=fin[0:mix.n, 3, h:h + 1])
                    ins.then_inc(squared, 1)
                    all_of(act, C_made, j)
                    act.activation(C[:], C_new[:], ACT.Copy).then_inc(C_moved, 1)

            rounds(act, body, NT + 1)

        @block.tensor
        def _(pe):
            pe.wait_ge(ident_made, 2)

            def turn_h(t):
                all_of(pe, normed, t.i, NORM)
                all_of(pe, qsT_sb, t.i - 3)
                for c in range(KC):
                    ins = pe.transpose(turned[:, c, 0:t.n], x[0:t.n, t.slot, c * P:(c + 1) * P], ident[0:t.n, 0:t.n])
                ins.then_inc(h_turned, 1)

            def project(out, t, c0, width, done):
                split_product(pe, out, (lambda c: hT_hi[:, t.slot, c, :], lambda c: hT_lo[:, t.slot, c, :]),
                              (lambda c: w_hi[:, c, c0:c0 + width], lambda c: w_lo[:, c, c0:c0 + width]),
                              range(KC)).then_inc(done, 1)

            turn_h(tile_at(0, 0))
            pe.wait_ge(w_hi_made, PIECES * KC)
            pe.wait_ge(w_lo_made, PIECES * KC)
            pe.wait_ge(const_sb, 1)

            def body(r, slot):
                i, j = r, r - 1
                cur, mix = tile_at(i, slot), tile_at(j, 1 - slot)
                n, m = cur.n, mix.n
                if exists(i):
                    all_of(pe, h_hi, i)
                    all_of(pe, h_lo, i)
                    all_of(pe, cols_sb, i - 2, 2)
                    reached(pe, row_step, (i - 1) * ROW_STEPS + 3)
                    project(GATES, cur, GATE_COL, 2 * HEADS, gates_ps)
                    all_of(pe, v_sb, i - 1)
                    project(proj[0][:], cur, 0, MW, q_ps)
                if exists(j):
                    all_of(pe, row_act, j, ROW_ACTS)
                    all_of(pe, row_step, j, ROW_STEPS)
                    all_of(pe, squared, j - 1)
                    all_of(pe, gates_sb, min(i, NT) if isinstance(i, int) else i)
                    for h in range(HEADS):
                        pe.matmul(wide[0:m, h, 0:m], pick[:, h, 0:m], rows[:, U, 0:m], start=True, stop=True)
                    for c, row in enumerate((G, W, E_ROW)):
                        pe.transpose(COLS[0:m, c * HEADS:(c + 1) * HEADS], rows[:, row, 0:m], ident[0:HEADS, 0:HEADS])
                    for h in range(HEADS):
                        ins = pe.matmul(COLS[:, 3 * HEADS + h:3 * HEADS + h + 1], pick[:, h, :], rows[:, W, m - 1:m], start=True, stop=True)
                    ins.then_inc(cols_ps, 1)
                if exists(r + 1):
                    turn_h(tile_at(r + 1, 1 - slot))
                if exists(i):
                    all_of(pe, o_sb, i - 1)
                    project(proj[1][:], cur, MW, MW, k_ps)
                if exists(j):
                    if exists(r + 1):
                        all_of(pe, h_hi, r + 1)
                        all_of(pe, h_lo, r + 1)
                    else:
                        all_of(pe, qsT_sb, j - 1)
                    all_of(pe, q_sb, j)
                    all_of(pe, k_sb, j)
                    for h in range(HEADS):
                        pe.transpose(turned[:, h, 0:m], q[0:m, mix.slot, h * QK:(h + 1) * QK], ident[0:m, 0:m])
                    for h in range(HEADS):
                        ins = pe.transpose(turned[:, HEADS + h, 0:m], k[0:m, mix.slot, h * QK:(h + 1) * QK], ident[0:m, 0:m])
                    ins.then_inc(qk_turned, 1)
                if exists(i):
                    all_of(pe, gates_sb, i)
                    all_of(pe, cols_sb, j, 2)
                    pe.transpose(ROWS[:, 0:n], gates[0:n, 0:HEADS], ident[0:n, 0:n])
                    pe.transpose(ROWS[:, P:P + n], gates[0:n, HEADS:2 * HEADS], ident[0:n, 0:n]).then_inc(rows_ps, 1)
                    all_of(pe, q_sb, i)
                    project(proj[0][:], cur, 2 * MW, MW, v_ps)
                if exists(j):
                    all_of(pe, q_scaled, j)
                    all_of(pe, qT_sb, j)
                    all_of(pe, kT_sb, j)
                    for h in range(HEADS):
                        ins = pe.transpose(turned[:, h, 0:m], q[0:m, mix.slot, h * QK:(h + 1) * QK], ident[0:m, 0:m])
                    ins.then_inc(qs_turned, 1)
                    all_of(pe, masked, j)
                    for h in range(HEADS):
                        ins = pe.matmul(wide[0:m, h, 0:m], kT[:, h, 0:m], qT[:, h, 0:m], start=True, stop=True)
                    ins.then_inc(scores_ps, 1)
                    all_of(pe, k_scaled, j)
                    all_of(pe, v_sb, j)
                    all_of(pe, fin_step, j - 1, FIN_STEPS)
                    for h in range(HEADS):
                        ins = pe.matmul(acc[:, h, 0:VA], k[0:m, mix.slot, h * QK:(h + 1) * QK], v[0:m, mix.slot, h, :], start=True, stop=True)
                    ins.then_inc(state_ps, 1)
                if exists(i):
                    all_of(pe, k_sb, i)
                    project(proj[1][:], cur, 3 * MW, MW, o_ps)
                if exists(j):
                    all_of(pe, qsT_sb, j)
                    all_of(pe, weighted, j)
                    all_of(pe, C_made, j)
                    if m == P:
                        all_of(pe, C_moved, j - 1)
                    state = C if m == P else C_dec
                    for h in range(HEADS):
                        pe.matmul(acc[0:m, h, 0:VA], qsT[:, h, 0:m], state[:, h, :], start=True, stop=False)
                        ins = pe.matmul(acc[0:m, h, 0:VA], decay[0:m, h, 0:m], v[0:m, mix.slot, h, :], start=False, stop=True)
                    ins.then_inc(num_ps, 1)

            rounds(pe, body, NT + 1)

        @block.vector
        def _(dve):
            def norm(t):
                slot_loaded(dve, x_in, t)
                xt = x[0:t.n, t.slot, :]
                norm_rows(dve, normed, rooted, t.i, xt, gmix[0:t.n, :], xt, stats[0:t.n], ms[0:t.n])

            def split_h(t):
                all_of(dve, h_hi, t.i)
                dve.tensor_tensor(hT_lo[:, t.slot, :, 0:t.n], turned[:, :, 0:t.n], hT_hi[:, t.slot, :, 0:t.n], ALU.subtract).then_inc(h_lo, 1)

            dve.memset(C[:], 0.0)
            dve.memset(v[:, :, :, QK:VA], 1.0)
            dve.memset(m_rows[:], 0.0)
            dve.memset(ones_row[:], 1.0)
            dve.memset(zero_row[:], 0.0)
            dve.wait_ge(ident_made, 4)
            dve.wait_ge(consts_in, 16 * N_CONST)
            dve.tensor_copy(pick[:], ident[0:HEADS, 0:HEADS].unsqueeze(2).to_broadcast([HEADS, HEADS, P])).then_inc(const_sb, 1)
            dve.wait_ge(const_sb, 1)
            norm(tile_at(0, 0))
            norm(tile_at(1, 1))
            split_h(tile_at(0, 0))
            for n in range(PIECES * KC):
                c, col, raw = n // PIECES, n % PIECES * PC, n % 2
                dve.wait_ge(w_hi_made, n + 1)
                dve.tensor_tensor(w_lo[:, c, col:col + PC], w_raw[:, raw, :], w_hi[:, c, col:col + PC],
                                  ALU.subtract).then_inc(w_lo_made, 1)

            def body(r, slot):
                i, j = r, r - 1
                cur, mix = tile_at(i, slot), tile_at(j, 1 - slot)
                n, m = cur.n, mix.n
                step = i * ROW_STEPS
                if exists(i):
                    all_of(dve, gates_ps, i)
                    dve.tensor_copy(gates[0:n, :], GATES[0:n, :]).then_inc(gates_sb, 1)
                if exists(j):
                    all_of(dve, cols_ps, j)
                    dve.tensor_copy(cols[0:m, 0:12], COLS[0:m, 0:12]).then_inc(cols_sb, 1)
                    dve.tensor_copy(cols[:, 12:16], COLS[:, 12:16]).then_inc(cols_sb, 1)
                    all_of(dve, num_ps, j - 1)
                    dve.scalar_tensor_tensor(decay[0:m, :, 0:m], wide[0:m, :, 0:m], -1.0,
                                             causal[0:m, 0:m].unsqueeze(1).to_broadcast([m, HEADS, m]), ALU.mult, ALU.add).then_inc(masked, 1)
                if exists(r + 1):
                    split_h(tile_at(r + 1, 1 - slot))
                if exists(j):
                    all_of(dve, qk_turned, j)
                    dve.tensor_copy(kT[:, :, 0:m], turned[:, HEADS:2 * HEADS, 0:m]).then_inc(kT_sb, 1)
                    all_of(dve, cols_sb, j, 2)
                    qv = q[0:m, mix.slot, :].rearrange("p (h d) -> p h d", h=HEADS)
                    dve.tensor_tensor(qv, qv, cols[0:m, 4:8].unsqueeze(2).to_broadcast([m, HEADS, QK]), ALU.mult).then_inc(q_scaled, 1)
                    all_of(dve, decayed, j)
                    kv = k[0:m, mix.slot, :].rearrange("p (h d) -> p h d", h=HEADS)
                    dve.tensor_tensor(kv, kv, decay[0:m, :, m - 1:m].to_broadcast([m, HEADS, QK]), ALU.mult).then_inc(k_scaled, 1)
                if exists(i):
                    all_of(dve, rows_ps, i)
                    all_of(dve, cols_ps, i - 1)
                    dve.tensor_scalar(rows[:, F_ROW, 0:n], ROWS[:, P:P + n], gbias[:, 1:2], None, ALU.add).then_inc(row_step, 1)
                    dve.wait_ge(row_step, step + 1)
                    dve.scalar_tensor_tensor(rows[:, F_ABS, 0:n], rows[:, F_ROW, 0:n], -1.0, rows[:, F_ROW, 0:n], ALU.mult, ALU.max).then_inc(row_step, 1)
                    dve.tensor_scalar(rows[:, I_ROW, 0:n], ROWS[:, 0:n], gbias[:, 0:1], None, ALU.add).then_inc(row_step, 1)
                    all_of(dve, v_ps, i)
                    dve.tensor_copy(v[0:n, slot, :, 0:QK], proj[0][0:n, :].rearrange("p (h d) -> p h d", h=HEADS)).then_inc(v_sb, 1)
                if exists(j):
                    all_of(dve, scores_ps, j)
                    all_of(dve, k_scaled, j)
                    dve.tensor_tensor(decay[0:m, :, 0:m], decay[0:m, :, 0:m], wide[0:m, :, 0:m], ALU.mult).then_inc(weighted, 1)
                    all_of(dve, state_ps, j)
                    all_of(dve, C_moved, j - 1)
                    if isinstance(j, int) and j == NT:
                        dve.wait_ge(state_out, 16 * 3)
                    state = C if m == P else C_dec
                    for h in range(HEADS):
                        ins = dve.scalar_tensor_tensor(C_new[:, h, :], state[:, h, :], cols[:, 12 + h:13 + h], acc[:, h, 0:VA], ALU.mult, ALU.add)
                    ins.then_inc(C_made, 1)
                if exists(i):
                    reached(dve, row_act, i * ROW_ACTS + 2)
                    dve.scalar_tensor_tensor(rows[:, LF, 0:n], rows[:, F_ROW, 0:n], 0.0, rows[:, LOG1P, 0:n], ALU.min, ALU.subtract).then_inc(row_step, 1)
                    dve.wait_ge(row_step, step + 4)
                    dve.tensor_tensor_scan(rows[:, B, 0:n], ones_row[:, 0:n], rows[:, LF, 0:n], 0.0, ALU.mult, ALU.add).then_inc(row_step, 1)
                    dve.wait_ge(row_step, step + 5)
                    dve.tensor_tensor(rows[:, G, 0:n], rows[:, I_ROW, 0:n], rows[:, B, 0:n], ALU.subtract).then_inc(row_step, 1)
                    dve.wait_ge(row_step, step + 6)
                    m_in = m_dec[:] if n < P else m_rows[:, 1 - slot, P - 1:P]
                    dve.tensor_tensor_scan(rows[:, U, 0:n], zero_row[:, 0:n], rows[:, G, 0:n], m_in, ALU.add, ALU.max).then_inc(row_step, 1)
                    dve.wait_ge(row_step, step + 7)
                    dve.tensor_tensor(m_rows[:, slot, 0:n], rows[:, B, 0:n], rows[:, U, 0:n], ALU.add).then_inc(row_step, 1)
                if exists(r + 2):
                    all_of(dve, h_turned, r)
                    norm(tile_at(r + 2, slot))
                if exists(j):
                    base = j * FIN_STEPS
                    all_of(dve, num_ps, j)
                    ho = heads_out[0:m, :].rearrange("p (h d) -> p h d", h=HEADS)
                    f = lambda a: fin[0:m, a, :]
                    all_of(dve, squared, j)
                    dve.tensor_tensor(f(0), acc[0:m, :, QK], cols[0:m, 8:12], ALU.max).then_inc(fin_step, 1)
                    dve.wait_ge(fin_step, base + 1)
                    dve.scalar_tensor_tensor(f(1), acc[0:m, :, QK], -1.0, f(0), ALU.mult, ALU.max).then_inc(fin_step, 1)
                    dve.wait_ge(fin_step, base + 2)
                    dve.reciprocal(f(2), f(1)).then_inc(fin_step, 1)
                    dve.wait_ge(fin_step, base + 3)
                    dve.tensor_tensor(f(4), f(3), f(2), ALU.mult).then_inc(fin_step, 1)
                    dve.wait_ge(fin_step, base + 4)
                    dve.scalar_tensor_tensor(f(5), f(4), 1.0 / QK, f(2), ALU.mult, ALU.mult).then_inc(fin_step, 1)
                    dve.wait_ge(fin_step, base + 5)
                    dve.tensor_scalar(f(6), f(5), EPS, None, ALU.add).then_inc(fin_step, 1)
                    all_of(dve, heads_rooted, j)
                    dve.tensor_tensor(f(7), f(3), f(2), ALU.mult).then_inc(fin_step, 1)
                    all_of(dve, o_sb, j)
                    ot = o[0:m, mix.slot, :]
                    dve.tensor_scalar(ot, ot, 1.0, None, ALU.add).then_inc(fin_step, 1)
                    dve.wait_ge(fin_step, base + 8)
                    dve.reciprocal(ot, ot).then_inc(fin_step, 1)
                    all_of(dve, out_done, j - 1, 16)
                    dve.tensor_tensor(ho, acc[0:m, :, 0:QK], f(7).unsqueeze(2).to_broadcast([m, HEADS, QK]), ALU.mult).then_inc(fin_step, 1)
                    dve.wait_ge(fin_step, base + 10)
                    dve.tensor_tensor(heads_out[0:m, :], heads_out[0:m, :], ghead[0:m, :], ALU.mult).then_inc(fin_step, 1)
                    dve.wait_ge(fin_step, base + 11)
                    dve.tensor_tensor(heads_out[0:m, :], heads_out[0:m, :], ot, ALU.mult).then_inc(fin_step, 1)

            rounds(dve, body, NT + 1)


def attention_phase(nc, x_prompt, x_sample, g_mix, w_in, sinks, w_out, cache_k, cache_v, mixed, x_mid,
                    out_k, out_v):
    QKV = AW + 2 * KVW
    PREV, CUR = 0, 1
    SCALE = HD ** -0.5
    with ExitStack() as ctx:
        def sb(name, shape, dt=F32):
            return ctx.enter_context(nc.sbuf_tensor("a_" + name, shape, dt))

        def ps(name, shape):
            return ctx.enter_context(nc.psum_tensor("a_" + name, shape, F32))

        def sem(name):
            return ctx.enter_context(nc.semaphore("a_" + name))

        def sems(names):
            return [sem(n) for n in names.split()]

        wa_hi, wa_lo = sb("wa_hi", [P, KC, QKV], F32R), sb("wa_lo", [P, KC, QKV], F32R)
        wo_hi, wo_lo = sb("wo_hi", [P, KC, D], F32R), sb("wo_lo", [P, KC, D], F32R)
        w_raw = sb("w_raw", [P, 2, D])
        x, x_sum = sb("x", [P, 2, D]), sb("x_sum", [P, 2, D])
        gmix = sb("gmix", [P, D])
        hT_hi, hT_lo = sb("hT_hi", [P, 2, KC, P], F32R), sb("hT_lo", [P, 2, KC, P], F32R)
        mixT_hi, mixT_lo = sb("mixT_hi", [P, KC, P], F32R), sb("mixT_lo", [P, KC, P], F32R)
        heads_in, att = sb("heads_in", [P, 2, MW]), sb("att", [P, 2, AW])
        q, kv = sb("q", [P, AW]), sb("kv", [P, 2, 2 * KVW])
        v_prev = sb("v_prev", [P, KVW])
        ck, cv = sb("ck", [P, KVW]), sb("cv", [P, KVW])
        qT = sb("qT", [P, GRP, P])
        kT, ckT = sb("kT", [P, 2, P]), sb("ckT", [P, P])
        s = sb("s", [P, KVH, GRP, 2 * P])
        sT = sb("sT", [P, KVH, 2, GRP, P])
        bias = sb("bias", [P, AH, 2 * P])
        dist = sb("dist", [P, 2 * P])
        sink = sb("sink", [P, AH])
        mx = sb("mx", [P, KVH, 7, GRP])
        MAX, TOP, NEG, SINK, SUM, SINK_EXP, DEN = range(7)
        ident = sb("ident", [P, P])
        stats, ms, minus_half = sb("stats", [P, 2, 6]), sb("ms", [P, 8]), sb("minus_half", [P, 1])

        proj = [ps("proj0", [P, NB]), ps("proj1", [P, NB])]
        turned = ps("turned", [P, KC, P])
        scores = ps("scores", [P, GRP, 2 * P])
        out_ps = [ps("out0", [P, NB]), ps("out1", [P, NB])]

        made, consts_in, const_sb, cache_turned, cache_out, last_out = sems("made consts_in const_sb cache_turned cache_out last_out")
        w_in_sem, (w_hi_made, w_lo_made) = sems("w_raw0 w_raw1"), sems("w_hi_made w_lo_made")
        x_in, heads_loaded, x_sum_in = sems("x_in0 x_in1"), sems("heads_in0 heads_in1"), sems("x_sum_in0 x_sum_in1")
        normed, rooted, h_turned, h_hi, h_lo = sems("normed rooted h_turned h_hi h_lo")
        q_ps, kv_ps, o0_ps, o1_ps, q_sb, kv_sb, v_kept = sems("q_ps kv_ps o0_ps o1_ps q_sb kv_sb v_kept")
        qk_turned, qT_sb, kT_sb = sems("qk_turned qT_sb kT_sb")
        scores_ps, soft, exps, s_turned, sT_sb, out_done, averaged = sems("scores_ps soft exps s_turned sT_sb out_done averaged")
        mix_turned, mix_hi, mix_lo, added, x_out = sems("mix_turned mix_hi mix_lo added x_out")
        SOFT, AVG, N_CONST = 5, 3, 4
        W_PIECES = 2 * KC

        def keys(t, part):
            return 0 if part == PREV and isinstance(t.i, int) and t.i == 0 else P if part == PREV else t.n

        def parts(t):
            return [p for p in (PREV, CUR) if keys(t, p)]

        def key_span(t):
            return (0 if keys(t, PREV) else P), P + t.n

        block = ctx.enter_context(nc.Block())

        @block.sync
        def _(sp):
            sp.dma_start(x[:, 0, :], x_prompt[0:P, :]).then_inc(x_in[0], 16)
            sp.dma_start(x[:, 1, :], x_prompt[P:2 * P, :]).then_inc(x_in[1], 16)
            sp.dma_start(gmix[:], g_mix.partition_broadcast(P)).then_inc(consts_in, 16)
            sp.dma_start(sink[:], sinks.partition_broadcast(P)).then_inc(consts_in, 16)
            sp.dma_start(ck[:], cache_k).then_inc(consts_in, 16)
            sp.dma_start(cv[:], cache_v).then_inc(consts_in, 16)
            for n in range(W_PIECES):
                c, raw = n % KC, n % 2
                reached(sp, w_lo_made, n - 1)
                width = QKV if n < KC else D
                src = w_in[c * P:(c + 1) * P, Q_COL:Q_COL + QKV] if n < KC else w_out[c * P:(c + 1) * P, :]
                sp.dma_start(w_raw[:, raw, 0:width], src).then_inc(w_in_sem[raw], 16)
            sp.dma_start(out_k[1][0:P - DEC, :], cache_k[DEC:P, :]).then_inc(cache_out, 16)
            sp.dma_start(out_v[1][0:P - DEC, :], cache_v[DEC:P, :]).then_inc(cache_out, 16)

            def body(r, slot):
                if exists(r + 2):
                    nxt = tile_at(r + 2, slot)
                    src = x_sample if nxt.n < P else x_prompt[token_rows(sp, nxt.i, P), :]
                    all_of(sp, h_turned, r)
                    sp.dma_start(x[0:nxt.n, nxt.slot, :], src).then_inc(x_in[slot], 16)
                if exists(r):
                    cur = tile_at(r, slot)
                    all_of(sp, mix_turned, r - 2)
                    sp.dma_start(heads_in[0:cur.n, slot, :], mixed[token_rows(sp, r, cur.n), :]).then_inc(heads_loaded[slot], 16)
                if exists(r - 2):
                    t = tile_at(r - 2, slot)
                    all_of(sp, added, t.i, 2)
                    sp.dma_start(x_mid[token_rows(sp, t.i, t.n), :], x_sum[0:t.n, slot, :]).then_inc(x_out, 16)
                    all_of(sp, x_out, t.i, 16)
                if exists(r):
                    src = x_sample if cur.n < P else x_prompt[token_rows(sp, r, P), :]
                    sp.dma_start(x_sum[0:cur.n, slot, :], src).then_inc(x_sum_in[slot], 16)
                if isinstance(r, int) and NT - 1 <= r <= NT:
                    which, rows = r - (NT - 1), tile_at(r, slot).n
                    all_of(sp, kv_sb, r)
                    sp.dma_start(out_k[which][P - rows:P, :], kv[0:rows, slot, 0:KVW]).then_inc(last_out, 16)
                    sp.dma_start(out_v[which][P - rows:P, :], kv[0:rows, slot, KVW:]).then_inc(last_out, 16)

            rounds(sp, body, NT + 2)
            sp.wait_ge(cache_out, 32)
            sp.wait_ge(last_out, 64)

        @block.gpsimd
        def _(pool):
            make_identity(pool, ident[:], made)
            pool.memset(minus_half[:], -0.5).then_inc(made, 1)
            pool.iota(dist[:], pattern=[[-1, 2 * P]], base=P, channel_multiplier=1,
                      allow_small_or_imprecise_dtypes=True).then_inc(made, 1)
            pool.wait_ge(made, 4)

            def root(t):
                norm_root(pool, normed, rooted, t.i, ms[0:t.n], minus_half[0:t.n])

            root(tile_at(0, 0))
            root(tile_at(1, 1))

            def body(r, slot):
                if exists(r + 2):
                    root(tile_at(r + 2, slot))

            rounds(pool, body, NT - 2)

        @block.scalar
        def _(act):
            def split_h(t):
                all_of(act, h_turned, t.i)
                all_of(act, kv_ps, t.i - 2)
                act.activation(hT_hi[:, t.slot, :, 0:t.n], turned[:, :, 0:t.n], ACT.Copy).then_inc(h_hi, 1)

            split_h(tile_at(0, 0))
            for n in range(W_PIECES):
                c, raw = n % KC, n % 2
                act.wait_ge(w_in_sem[raw], 16 * (n // 2 + 1))
                dst, width = (wa_hi, QKV) if n < KC else (wo_hi, D)
                act.activation(dst[:, c, :], w_raw[:, raw, 0:width], ACT.Copy).then_inc(w_hi_made, 1)

            def exponentials(t, g):
                lo, hi = key_span(t)
                reached(act, soft, (t.i * 2 + g) * SOFT + 4)
                for h in range(GRP):
                    part = s[0:t.n, g, h, lo:hi]
                    ins = act.activation(part, part, ACT.Exp, bias=mx[0:t.n, g, NEG, h:h + 1], accum_out=mx[0:t.n, g, SUM, h:h + 1])
                ins.then_inc(exps, 1)
                reached(act, soft, (t.i * 2 + g) * SOFT + 5)
                act.activation(mx[0:t.n, g, SINK_EXP, :], mx[0:t.n, g, SINK, :], ACT.Exp).then_inc(exps, 1)

            def copy_turned(t, g):
                reached(act, s_turned, t.i * 2 + g + 1)
                for p in parts(t):
                    n = keys(t, p)
                    ins = act.activation(sT[0:n, g, p, :, 0:t.n], turned[0:n, p * GRP:(p + 1) * GRP, 0:t.n], ACT.Copy)
                ins.then_inc(sT_sb, 1)

            def body(r, slot):
                cur, mid, old = tile_at(r, slot), tile_at(r - 1, 1 - slot), tile_at(r - 2, slot)
                if exists(mid.i):
                    exponentials(mid, 0)
                if exists(cur.i):
                    all_of(act, q_ps, r)
                    all_of(act, qk_turned, r - 1)
                    act.activation(q[0:cur.n, :].rearrange("p (h g d) -> p g h d", g=KVH, h=GRP),
                                   proj[0][0:cur.n, :].rearrange("p (g h d) -> p g h d", g=KVH, h=GRP), ACT.Copy).then_inc(q_sb, 1)
                if exists(old.i):
                    all_of(act, mix_turned, old.i)
                    all_of(act, o1_ps, old.i - 1)
                    act.activation(mixT_hi[:, :, 0:old.n], turned[:, :, 0:old.n], ACT.Copy).then_inc(mix_hi, 1)
                if exists(r + 1):
                    split_h(tile_at(r + 1, 1 - slot))
                if exists(mid.i):
                    copy_turned(mid, 0)
                    exponentials(mid, 1)
                if exists(cur.i):
                    all_of(act, qk_turned, r)
                    act.activation(qT[:, :, 0:cur.n], turned[:, 0:GRP, 0:cur.n], ACT.Copy).then_inc(qT_sb, 1)
                if exists(mid.i):
                    copy_turned(mid, 1)

            rounds(act, body, NT + 2)

        @block.tensor
        def _(pe):
            pe.wait_ge(made, 2)

            def turn(t, src, done):
                for c in range(KC):
                    ins = pe.transpose(turned[:, c, 0:t.n], src(c), ident[0:t.n, 0:t.n])
                ins.then_inc(done, 1)

            def turn_h(t):
                all_of(pe, normed, t.i, NORM)
                turn(t, lambda c: x[0:t.n, t.slot, c * P:(c + 1) * P], h_turned)

            def project(out, t, c0, width, chunks):
                return split_product(pe, out, (lambda c: hT_hi[:, t.slot, c, :], lambda c: hT_lo[:, t.slot, c, :]),
                                     (lambda c: wa_hi[:, c, c0:c0 + width], lambda c: wa_lo[:, c, c0:c0 + width]),
                                     chunks, chunks[0] == 0, chunks[-1] == KC - 1)

            def project_out(half, chunks):
                cols = slice(half * NB, (half + 1) * NB)
                return split_product(pe, proj[half][:], (lambda c: mixT_hi[:, c, :], lambda c: mixT_lo[:, c, :]),
                                     (lambda c: wo_hi[:, c, cols], lambda c: wo_lo[:, c, cols]),
                                     chunks, chunks[0] == 0, chunks[-1] == KC - 1)

            def score(t, g):
                head = slice(g * HD, (g + 1) * HD)
                reached(pe, soft, (t.i * 2 + g - 1) * SOFT + 1)
                for h in range(GRP):
                    for p in parts(t):
                        n = keys(t, p)
                        kk = kT[head, t.slot, 0:n] if p == CUR else ckT[head, :] if t.n < P else kT[head, 1 - t.slot, :]
                        ins = pe.matmul(scores[0:t.n, h, p * P:p * P + n], qT[head, h, 0:t.n], kk, start=True, stop=True)
                ins.then_inc(scores_ps, 1)

            def turn_s(t, g):
                reached(pe, exps, (t.i * 2 + g) * 2 + 1)
                for p in parts(t):
                    n = keys(t, p)
                    for h in range(GRP):
                        ins = pe.transpose(turned[0:n, p * GRP + h, 0:t.n], s[0:t.n, g, h, p * P:p * P + n], ident[0:t.n, 0:t.n])
                ins.then_inc(s_turned, 1)

            def average(t, g):
                reached(pe, sT_sb, t.i * 2 + g + 1)
                reached(pe, averaged, ((t.i - 1) * 2 + g + 1) * AVG)
                for h in range(GRP):
                    for p in parts(t):
                        n = keys(t, p)
                        vals = kv[0:n, t.slot, KVW + g * HD:KVW + (g + 1) * HD] if p == CUR else (cv if t.n < P else v_prev)[:, g * HD:(g + 1) * HD]
                        ins = pe.matmul(out_ps[g][0:t.n, h * HD:(h + 1) * HD], sT[0:n, g, p, h, 0:t.n], vals,
                                        start=p == parts(t)[0], stop=p == CUR)
                ins.then_inc(out_done, 1)

            first, second = range(KC // 2), range(KC // 2, KC)
            turn_h(tile_at(0, 0))
            pe.wait_ge(const_sb, 1)
            pe.transpose(scores[:, 0, 0:P], ck[:], ident[:]).then_inc(cache_turned, 1)
            pe.wait_ge(const_sb, 2)

            def body(r, slot):
                cur, mid, old = tile_at(r, slot), tile_at(r - 1, 1 - slot), tile_at(r - 2, slot)
                if exists(mid.i):
                    all_of(pe, qT_sb, mid.i)
                    all_of(pe, kT_sb, mid.i)
                    score(mid, 0)
                if exists(cur.i):
                    if isinstance(r, int) and r == 0:
                        pe.wait_ge(w_lo_made, KC)
                    all_of(pe, h_lo, r)
                    reached(pe, added, (r - 3) * 2 + 1)
                    project(proj[0][:], cur, 0, AW, first)
                if exists(old.i):
                    average(old, 1)
                if exists(cur.i):
                    project(proj[0][:], cur, 0, AW, second).then_inc(q_ps, 1)
                if exists(old.i):
                    reached(pe, averaged, (old.i + 1) * 2 * AVG)
                    slot_loaded(pe, heads_loaded, old)
                    turn(old, lambda c: (heads_in if c < HEADS else att)[0:old.n, old.slot, c % HEADS * P:(c % HEADS + 1) * P], mix_turned)
                if exists(cur.i):
                    all_of(pe, added, r - 3, 2)
                    project(proj[1][:, 0:2 * KVW], cur, AW, 2 * KVW, range(KC)).then_inc(kv_ps, 1)
                if exists(old.i):
                    all_of(pe, mix_lo, old.i)
                if exists(r + 1):
                    turn_h(tile_at(r + 1, 1 - slot))
                if exists(mid.i):
                    score(mid, 1)
                if isinstance(r, int) and r == 2:
                    pe.wait_ge(w_lo_made, W_PIECES)
                if exists(old.i):
                    all_of(pe, q_sb, r if exists(r) else NT)
                    project_out(0, first)
                if exists(mid.i):
                    if exists(r + 1):
                        all_of(pe, h_lo, r + 1)
                    turn_s(mid, 0)
                if exists(old.i):
                    project_out(0, second).then_inc(o0_ps, 1)
                if exists(mid.i):
                    if exists(cur.i):
                        reached(pe, v_kept, r - 1)
                    average(mid, 0)
                if exists(old.i):
                    all_of(pe, kv_sb, r if exists(r) else NT)
                    project_out(1, first)
                if exists(cur.i):
                    all_of(pe, q_sb, r)
                    all_of(pe, kv_sb, r)
                    if exists(mid.i):
                        reached(pe, sT_sb, mid.i * 2 + 1)
                    else:
                        all_of(pe, h_lo, r + 1)
                    for h in range(GRP):
                        pe.transpose(turned[:, h, 0:cur.n], q[0:cur.n, h * P:(h + 1) * P], ident[0:cur.n, 0:cur.n])
                    pe.transpose(turned[:, GRP, 0:cur.n], kv[0:cur.n, slot, 0:KVW], ident[0:cur.n, 0:cur.n]).then_inc(qk_turned, 1)
                if exists(old.i):
                    project_out(1, second).then_inc(o1_ps, 1)
                if exists(mid.i):
                    if exists(cur.i):
                        all_of(pe, qT_sb, r)
                        all_of(pe, kT_sb, r)
                    else:
                        reached(pe, sT_sb, mid.i * 2 + 1)
                    turn_s(mid, 1)

            rounds(pe, body, NT + 2)

        @block.vector
        def _(dve):
            def norm(t):
                slot_loaded(dve, x_in, t)
                xt = x[0:t.n, t.slot, :]
                norm_rows(dve, normed, rooted, t.i, xt, gmix[0:t.n, :], xt, stats[0:t.n], ms[0:t.n])

            def split(i, hi_made, lo, hi, n, lo_made):
                all_of(dve, hi_made, i)
                dve.tensor_tensor(lo, turned[:, :, 0:n], hi, ALU.subtract).then_inc(lo_made, 1)

            def split_h(t):
                split(t.i, h_hi, hT_lo[:, t.slot, :, 0:t.n], hT_hi[:, t.slot, :, 0:t.n], t.n, h_lo)

            def soften(t, g):
                n, (lo, hi) = t.n, key_span(t)
                base = (t.i * 2 + g) * SOFT
                f = lambda a: mx[0:n, g, a, :]
                heads = slice(g * GRP, (g + 1) * GRP)
                reached(dve, scores_ps, t.i * 2 + g + 1)
                reached(dve, s_turned, (t.i - 1) * 2 + g + 1)
                dve.scalar_tensor_tensor(s[0:n, g, :, lo:hi], scores[0:n, :, lo:hi], SCALE, bias[0:n, heads, lo:hi], ALU.mult, ALU.add).then_inc(soft, 1)
                dve.wait_ge(soft, base + 1)
                dve.reduce_max(f(MAX), s[0:n, g, :, lo:hi], AX.X).then_inc(soft, 1)
                dve.wait_ge(soft, base + 2)
                dve.tensor_tensor(f(TOP), f(MAX), sink[0:n, heads], ALU.max).then_inc(soft, 1)
                dve.wait_ge(soft, base + 3)
                reached(dve, exps, ((t.i - 1) * 2 + g + 1) * 2)
                dve.tensor_scalar(f(NEG), f(TOP), -1.0, None, ALU.mult).then_inc(soft, 1)
                dve.tensor_tensor(f(SINK), sink[0:n, heads], f(TOP), ALU.subtract).then_inc(soft, 1)

            def divide(t, g):
                n, base = t.n, (t.i * 2 + g) * AVG
                f = lambda a: mx[0:n, g, a, :]
                reached(dve, exps, (t.i * 2 + g + 1) * 2)
                dve.tensor_tensor(f(DEN), f(SUM), f(SINK_EXP), ALU.add).then_inc(averaged, 1)
                dve.wait_ge(averaged, base + 1)
                dve.reciprocal(f(DEN), f(DEN)).then_inc(averaged, 1)
                dve.wait_ge(averaged, base + 2)
                reached(dve, out_done, t.i * 2 + g + 1)
                all_of(dve, mix_turned, t.i - 2)
                dst = att[0:n, t.slot, g * GRP * HD:(g + 1) * GRP * HD].rearrange("p (h d) -> p h d", h=GRP)
                dve.tensor_tensor(dst, out_ps[g][0:n, 0:GRP * HD].rearrange("p (h d) -> p h d", h=GRP),
                                  f(DEN).unsqueeze(2).to_broadcast([n, GRP, HD]), ALU.mult).then_inc(averaged, 1)

            def add(t, half):
                cols = slice(half * NB, (half + 1) * NB)
                all_of(dve, (o0_ps, o1_ps)[half], t.i)
                dve.tensor_tensor(x_sum[0:t.n, t.slot, cols], x_sum[0:t.n, t.slot, cols], proj[half][0:t.n, :], ALU.add).then_inc(added, 1)

            dve.wait_ge(made, 4)
            dve.wait_ge(consts_in, 16 * N_CONST)
            dve.scalar_tensor_tensor(dist[:], dist[:], -1.0, dist[:], ALU.mult, ALU.max).then_inc(const_sb, 1)
            norm(tile_at(0, 0))
            norm(tile_at(1, 1))
            split_h(tile_at(0, 0))
            dve.wait_ge(cache_turned, 1)
            dve.tensor_copy(ckT[:], scores[:, 0, 0:P]).then_inc(const_sb, 1)
            dve.wait_ge(const_sb, 2)
            for h in range(AH):
                ins = dve.tensor_scalar(bias[:, h, :], dist[:], -(2.0 ** (-(h + 1) * 8.0 / AH)), None, ALU.mult)
            ins.then_inc(const_sb, 1)
            dve.wait_ge(const_sb, 3)
            dve.memset(bias[0:P // 2, :, P + P // 2:], MASKED)
            dve.memset(bias[P // 2:, :, 0:P // 2], MASKED).then_inc(const_sb, 1)
            dve.wait_ge(const_sb, 4)
            for n in range(W_PIECES):
                c, raw = n % KC, n % 2
                hi, lo, width = (wa_hi, wa_lo, QKV) if n < KC else (wo_hi, wo_lo, D)
                dve.wait_ge(w_hi_made, n + 1)
                dve.tensor_tensor(lo[:, c, :], w_raw[:, raw, 0:width], hi[:, c, :], ALU.subtract).then_inc(w_lo_made, 1)

            def body(r, slot):
                cur, mid, old = tile_at(r, slot), tile_at(r - 1, 1 - slot), tile_at(r - 2, slot)
                if exists(mid.i):
                    soften(mid, 0)
                if exists(old.i):
                    divide(old, 1)
                    split(old.i, mix_hi, mixT_lo[:, :, 0:old.n], mixT_hi[:, :, 0:old.n], old.n, mix_lo)
                if exists(cur.i):
                    all_of(dve, kv_ps, r)
                    if exists(old.i):
                        all_of(dve, out_done, old.i, 2)
                        dve.tensor_copy(v_prev[:], kv[:, slot, KVW:]).then_inc(v_kept, 1)
                        all_of(dve, v_kept, old.i)
                    dve.tensor_copy(kv[0:cur.n, slot, :], proj[1][0:cur.n, 0:2 * KVW]).then_inc(kv_sb, 1)
                if exists(r + 1):
                    split_h(tile_at(r + 1, 1 - slot))
                if exists(mid.i):
                    soften(mid, 1)
                if exists(old.i):
                    slot_loaded(dve, x_sum_in, old)
                    add(old, 0)
                if exists(mid.i):
                    divide(mid, 0)
                if exists(cur.i):
                    all_of(dve, qk_turned, r)
                    dve.tensor_copy(kT[:, slot, 0:cur.n], turned[:, GRP, 0:cur.n]).then_inc(kT_sb, 1)
                if exists(old.i):
                    add(old, 1)
                if exists(r + 2):
                    norm(tile_at(r + 2, slot))

            rounds(dve, body, NT + 2)


def mlp_phase(nc, x_mid, g_mlp, w_up, w_down, x_mlp):
    BLOCKS = FF // MLP_BLOCK
    FC = MLP_BLOCK // P
    HALF = NT // 2
    TOKENS = HALF * P + DEC
    with ExitStack() as ctx:
        def sb(name, shape, dt=F32):
            return ctx.enter_context(nc.sbuf_tensor("f_" + name, shape, dt))

        def ps(name, shape):
            return ctx.enter_context(nc.psum_tensor("f_" + name, shape, F32))

        def sems(names):
            return [ctx.enter_context(nc.semaphore("f_" + n)) for n in names.split()]

        acc = sb("acc", [P, HALF + 1, D])
        h_buf = sb("h", [P, D])
        hT_hi, hT_lo = sb("hT_hi", [P, KC, TOKENS], F32R), sb("hT_lo", [P, KC, TOKENS], F32R)
        gmlp = sb("gmlp", [P, D])
        up_hi, up_lo = sb("up_hi", [P, 2, KC, MLP_BLOCK], F32R), sb("up_lo", [P, 2, KC, MLP_BLOCK], F32R)
        down_hi, down_lo = sb("down_hi", [P, 2, FC, D], F32R), sb("down_lo", [P, 2, FC, D], F32R)
        raw = sb("raw", [P, 2, D])
        u = sb("u", [P, FC, NB])
        uT_hi, uT_lo = sb("uT_hi", [P, FC, (HALF + 1) * P], F32R), sb("uT_lo", [P, FC, (HALF + 1) * P], F32R)
        h = [h_buf[:], u[:].rearrange("p f t -> p (f t)"), acc[:, HALF, :]]
        H_SLOT = [0, 1, 2, 0, 1, 2, 0, 2, 0]
        H_BEFORE = [None, None, None, 0, 1, 2, 3, 5, 6]
        ident = sb("ident", [P, P])
        ms, constants = sb("ms", [P, HALF + 1, 3]), sb("constants", [P, 2])

        up_ps = [ps("up0", [P, FC, NB]), ps("up1", [P, FC, NB])]
        down_ps = [ps("down0", [P, D]), ps("down1", [P, D])]

        raw_in, (w_hi_made, w_lo_made) = sems("raw_in0 raw_in1"), sems("w_hi_made w_lo_made")
        made, gain_in, acc_out, cleared = sems("made gain_in acc_out cleared")
        acc_in = sems(" ".join(f"acc_in{n}" for n in range(HALF + 1)))
        h_in = sems("h_in0 h_in1 h_in2")
        summed, normed, rooted, h_turned, h_hi, h_lo = sems("summed normed rooted h_turned h_hi h_lo")
        up_done, rectified, squared, u_hi, u_lo, down_done, added = sems("up_done rectified squared u_hi u_lo down_done added")
        PIECES = 8

        def quarter(slot, n, up, down):
            if n < 2:
                return up[:, slot, n * KC // 2:(n + 1) * KC // 2, :].rearrange("p c f -> p (c f)")
            return down[:, slot, n - 2, :]

        def tiles(half):
            return [(n, tile_at(half * HALF + n, n % 2)) for n in range(HALF + half)]

        def groups(half):
            cols = TOKENS // 3 if half else NB
            return [slice(c, c + cols) for c in range(0, HALF * P + half * DEC, cols)]

        def last_place(cols):
            return (cols.stop - 1) // P

        def up_count(half, b, g):
            n = len(groups(half))
            return b * n + (g + 1 - half * BLOCKS * (n - 2))

        def turned_at(half, n):
            banks = up_ps if half and n < 4 else down_ps
            t = banks[n % 2]
            return t.rearrange("p c (a t) -> p (c a) t", t=P) if banks is up_ps else t.rearrange("p (c t) -> p c t", t=P)

        def turned_free(eng, half, n):
            if half and n < 2:
                eng.wait_ge(rectified, up_count(0, BLOCKS - 1, 1))
            elif half and 4 <= n < 6:
                eng.wait_ge(added, down_count(0, BLOCKS - 1, HALF - 1))
            elif n >= 2:
                all_of(eng, h_lo, half * HALF + n - 2)

        TURNED_AFTER = [{(0, 0): [4, 5], (0, 1): [6, 7]}, {(0, 0): [4, 5], (1, 0): [6], (1, 1): [7, 8]}]
        TURNED_AHEAD = {2: 0, 3: 1, 5: 2, 6: 3}

        def turned_in(half, g):
            return [n for (at, _), places in TURNED_AFTER[half].items() if at == g for n in places]

        def down_count(half, b, n):
            per = HALF + half
            return b * per + (n + 1 - half * BLOCKS)

        def blocks(eng, half, body):
            first, last = half * BLOCKS, (half + 1) * BLOCKS - 1
            body(first, 0, first + 1)
            with eng.Fori(0, (BLOCKS - 2) // 2) as turn:
                body(turn * 2 + (first + 1), 1, turn * 2 + (first + 2))
                body(turn * 2 + (first + 2), 0, turn * 2 + (first + 3))
            body(last, 1, None if half else last + 1)

        block = ctx.enter_context(nc.Block())

        @block.sync
        def _(sp):
            def load_weights(first_col, b, between=None):
                up = w_up[:, first_col].rearrange("(n c p) f -> n p c f", n=2, p=P)
                down = w_down[first_col, :].rearrange("(n p) d -> n p d", p=P)
                for n in range(4):
                    dst = raw[:, n % 2, :]
                    reached(sp, w_lo_made, b * PIECES + 2 * (n - 1))
                    sp.dma_start(dst.rearrange("p (c f) -> p c f", f=MLP_BLOCK) if n < 2 else dst,
                                 up[n] if n < 2 else down[n - 2]).then_inc(raw_in[n % 2], 16)
                    if between:
                        between(n)

            def load_tile(n, t):
                sp.dma_start(acc[0:t.n, n, :], x_mid[token_rows(sp, t.i, t.n), :]).then_inc(acc_in[n], 16)

            sp.dma_start(gmlp[:], g_mlp.partition_broadcast(P)).then_inc(gain_in, 16)
            for n, t in tiles(0)[:2]:
                load_tile(n, t)
            load_weights(slice(0, MLP_BLOCK), 0, lambda n: load_tile(*tiles(0)[n + 2]))
            for n, t in tiles(0)[6:]:
                load_tile(n, t)
            for half in (0, 1):
                def body(b, slot, nxt):
                    if nxt is None:
                        return
                    if isinstance(nxt, int):
                        c = nxt % BLOCKS * MLP_BLOCK
                        load_weights(slice(c, c + MLP_BLOCK), nxt)
                    else:
                        load_weights(bass.ds((nxt - half * BLOCKS) * MLP_BLOCK, MLP_BLOCK), nxt)

                blocks(sp, half, body)
                for n, t in tiles(half):
                    reached(sp, added, down_count(half, (half + 1) * BLOCKS - 1, n))
                    sp.dma_start(x_mlp[token_rows(sp, t.i, t.n), :], acc[0:t.n, n, :]).then_inc(acc_out, 16)
                    if not half:
                        sp.wait_ge(acc_out, 16 * (n + 1))
                        load_tile(*tiles(1)[n])
                if not half:
                    all_of(sp, h_turned, HALF + HALF - 1)
                    load_tile(*tiles(1)[HALF])
            sp.wait_ge(acc_out, 16 * (NT + 1))

        @block.gpsimd
        def _(pool):
            make_identity(pool, ident[:], made)
            pool.memset(constants[:, 0:1], EPS).then_inc(made, 1)
            pool.memset(constants[:, 1:2], -0.5).then_inc(made, 1)
            pool.wait_ge(made, 4)

            def load_h(n):
                t = tiles(1)[n][1]
                slot = H_SLOT[n]
                pool.dma_start(h[slot][0:t.n, :], x_mid[token_rows(pool, t.i, t.n), :]).then_inc(h_in[slot], 16)

            for half in (0, 1):
                if half:
                    all_of(pool, h_turned, HALF - 1)
                    all_of(pool, normed, HALF - 1)
                    load_h(0)
                    load_h(2)
                    pool.wait_ge(u_lo, up_count(0, BLOCKS - 1, 1))
                    load_h(1)
                for n, t in tiles(half):
                    sums_root(pool, summed, rooted, t.i, ms[0:t.n, n], constants[0:t.n])
                    if half:
                        for later in range(HALF + 1):
                            if n and H_BEFORE[later] == n - 1:
                                all_of(pool, h_turned, HALF + n - 1)
                                load_h(later)

        @block.scalar
        def _(act):
            def weights_hi(b, slot, quarters=range(4)):
                for n in quarters:
                    reached(act, raw_in[n % 2], b * 32 + 16 * (n // 2 + 1))
                    act.activation(quarter(slot, n, up_hi, down_hi), raw[:, n % 2, :], ACT.Copy).then_inc(w_hi_made, 1)

            def sum_h(half, n):
                if n >= len(tiles(half)):
                    return
                t = tiles(half)[n][1]
                slot = H_SLOT[n]
                if half:
                    turned_free(act, half, n)
                    act.wait_ge(h_in[slot], 16 * (H_SLOT[:n].count(slot) + 1))
                    src, squares = h[slot][0:t.n, :].rearrange("p (c t) -> p c t", t=P), turned_at(half, n)[0:t.n]
                else:
                    if H_BEFORE[n] is not None:
                        all_of(act, h_turned, H_BEFORE[n])
                    act.wait_ge(acc_in[n], 16)
                    src, squares = acc[0:t.n, n, :], h[slot][0:t.n, :]
                act.activation(squares, src, ACT.Square, scale=D ** -0.5, accum_out=ms[0:t.n, n, 0:1]).then_inc(summed, 1)

            def split_h(half, n):
                t = tiles(half)[n][1]
                all_of(act, h_turned, t.i)
                if half:
                    act.wait_ge(up_done, up_count(0, BLOCKS - 1, 1))
                act.activation(hT_hi[:, :, n * P:n * P + t.n], turned_at(half, n)[:, :, 0:t.n], ACT.Copy).then_inc(h_hi, 1)
                sum_h(half, n + 2)

            sum_h(0, 0)
            sum_h(0, 1)
            weights_hi(0, 0, range(0, 2))
            split_h(0, 0)
            split_h(0, 1)
            weights_hi(0, 0, range(2, 3))
            split_h(0, 2)
            weights_hi(0, 0, range(3, 4))
            split_h(0, 3)
            for half in (0, 1):
                def body(b, slot, nxt):
                    for g, cols in enumerate(groups(half)):
                        if isinstance(b, int) and b == half * BLOCKS:
                            for n in turned_in(half, g):
                                split_h(half, n)
                        width = cols.stop - cols.start
                        count = up_count(half, b, g)
                        reached(act, up_done, count)
                        reached(act, u_lo, count - 1)
                        act.activation(u[:, :, 0:width], up_ps[g % 2][:, :, 0:width], ACT.Relu).then_inc(rectified, 1)
                        reached(act, squared, count)
                        reached(act, down_done, down_count(half, b - 1, last_place(cols)))
                        act.activation(uT_hi[:, :, cols], u[:, :, 0:width], ACT.Copy).then_inc(u_hi, 1)
                    if isinstance(nxt, int) and nxt == BLOCKS:
                        weights_hi(nxt, 1 - slot, range(0, 2))
                        sum_h(1, 0)
                        sum_h(1, 1)
                        weights_hi(nxt, 1 - slot, range(2, 3))
                        split_h(1, 0)
                        weights_hi(nxt, 1 - slot, range(3, 4))
                        for n in range(1, 4):
                            split_h(1, n)
                    elif nxt is not None:
                        weights_hi(nxt, 1 - slot)

                blocks(act, half, body)

        @block.tensor
        def _(pe):
            pe.wait_ge(made, 2)
            pe.wait_ge(cleared, 1)

            def turn_h(half, n):
                t = tiles(half)[n][1]
                turned_free(pe, half, n)
                all_of(pe, normed, t.i)
                for c in range(KC):
                    ins = pe.transpose(turned_at(half, n)[:, c, 0:t.n], h[H_SLOT[n]][0:t.n, c * P:(c + 1) * P], ident[0:t.n, 0:t.n])
                ins.then_inc(h_turned, 1)

            for n in range(4):
                turn_h(0, n)
            for half in (0, 1):
                def body(b, slot, nxt):
                    first = isinstance(b, int) and b == half * BLOCKS
                    reached(pe, w_lo_made, b * PIECES + 4)
                    for g, cols in enumerate(groups(half)):
                        if first:
                            all_of(pe, h_lo, half * HALF + last_place(cols))
                        if g == 2:
                            reached(pe, rectified, up_count(half, b, 0))
                        for f in range(FC):
                            fc = slice(f * P, (f + 1) * P)
                            ins = split_product(pe, up_ps[g % 2][:, f, 0:cols.stop - cols.start],
                                                (lambda c: up_hi[:, slot, c, fc], lambda c: up_lo[:, slot, c, fc]),
                                                (lambda c: hT_hi[:, c, cols], lambda c: hT_lo[:, c, cols]), range(KC))
                            if f == FC - 1:
                                ins.then_inc(up_done, 1)
                            if first:
                                for n in TURNED_AFTER[half].get((g, f), []):
                                    turn_h(half, n)
                    reached(pe, w_lo_made, b * PIECES + PIECES)
                    for n in range(HALF + half):
                        for g, cols in enumerate(groups(half)):
                            if cols.start <= n * P < cols.stop or n * P < cols.start < (n + 1) * P:
                                reached(pe, u_lo, up_count(half, b, g))
                        if n >= 2:
                            reached(pe, added, down_count(half, b, n - 2))
                        else:
                            last = HALF - 2 if not half or n else HALF
                            reached(pe, added, down_count(half, b - 1, last if n == 0 else HALF - 1))
                        at = slice(n * P, (n + 1) * P)
                        for c in range(D // NB):
                            cols = slice(c * NB, (c + 1) * NB)
                            ins = split_product(pe, down_ps[n % 2][:, cols], (lambda f: uT_hi[:, f, at], lambda f: uT_lo[:, f, at]),
                                                (lambda f: down_hi[:, slot, f, cols], lambda f: down_lo[:, slot, f, cols]), range(FC))
                        ins.then_inc(down_done, 1)
                        if isinstance(nxt, int) and nxt == BLOCKS and n in TURNED_AHEAD:
                            turn_h(1, TURNED_AHEAD[n])

                blocks(pe, half, body)

        @block.vector
        def _(dve):
            def weights_lo(b, slot, piece):
                n, cols = piece // 2, slice(piece % 2 * NB, (piece % 2 + 1) * NB)
                if piece % 2 == 0:
                    reached(dve, w_hi_made, b * 4 + n + 1)
                dve.tensor_tensor(quarter(slot, n, up_lo, down_lo)[:, cols], raw[:, n % 2, cols],
                                  quarter(slot, n, up_hi, down_hi)[:, cols], ALU.subtract).then_inc(w_lo_made, 1)

            dve.memset(uT_hi[:].bitcast(F32), 0.0)
            dve.memset(uT_lo[:].bitcast(F32), 0.0).then_inc(cleared, 1)
            dve.wait_ge(gain_in, 16)

            def scale_h(half, n):
                if n >= len(tiles(half)):
                    return
                t = tiles(half)[n][1]
                at = h[H_SLOT[n]][0:t.n, :]
                all_of(dve, rooted, t.i, 2)
                dve.scalar_tensor_tensor(at, at if half else acc[0:t.n, n, :], ms[0:t.n, n, 2:3], gmlp[0:t.n, :],
                                         ALU.mult, ALU.mult).then_inc(normed, 1)

            def low_h(half, n):
                t = tiles(half)[n][1]
                all_of(dve, h_hi, t.i)
                dve.tensor_tensor(hT_lo[:, :, n * P:n * P + t.n], turned_at(half, n)[:, :, 0:t.n], hT_hi[:, :, n * P:n * P + t.n],
                                  ALU.subtract).then_inc(h_lo, 1)

            scale_h(0, 0)
            scale_h(0, 1)
            for n in range(4):
                for piece in ((0, 1, 2, 3), (), (4, 5), (6, 7))[n]:
                    weights_lo(0, 0, piece)
                low_h(0, n)
                scale_h(0, n + 2)
            AHEAD = {1: [(scale_h, 0)], 2: [(scale_h, 1)], 3: [(low_h, 0)], 4: [(low_h, 1)], 5: [(scale_h, 2)],
                     6: [(scale_h, 3), (low_h, 2)], 7: [(low_h, 3), (scale_h, 4), (scale_h, 5)]}
            for half in (0, 1):
                def add(b, n, t):
                    first = isinstance(b, int) and b == half * BLOCKS
                    reached(dve, down_done, down_count(half, b, n))
                    if first:
                        dve.wait_ge(acc_in[n], 16 * (half + 1) if n < HALF else 16)
                        all_of(dve, normed, t.i)
                    else:
                        reached(dve, added, down_count(half, b - 1, n))
                    dve.tensor_tensor(acc[0:t.n, n, :], acc[0:t.n, n, :], down_ps[n % 2][0:t.n, :], ALU.add).then_inc(added, 1)

                def body(b, slot, nxt):
                    for g, cols in enumerate(groups(half)):
                        if isinstance(b, int) and b == half * BLOCKS:
                            for n in turned_in(half, g):
                                low_h(half, n)
                                scale_h(half, n + 2)
                        count = up_count(half, b, g)
                        part = u[:, :, 0:cols.stop - cols.start]
                        reached(dve, rectified, count)
                        dve.tensor_tensor(part, part, part, ALU.mult).then_inc(squared, 1)
                        if g == len(groups(half)) - 1:
                            add(b, *tiles(half)[0])
                        reached(dve, u_hi, count)
                        dve.tensor_tensor(uT_lo[:, :, cols], part, uT_hi[:, :, cols], ALU.subtract).then_inc(u_lo, 1)
                    for n, t in tiles(half):
                        if n:
                            add(b, n, t)
                        if nxt is not None and n < PIECES:
                            weights_lo(nxt, 1 - slot, n)
                        if isinstance(nxt, int) and nxt == BLOCKS:
                            for step, place in AHEAD.get(n, []):
                                step(1, place)

                blocks(dve, half, body)


def ple_phase(nc, x_mlp, p_prompt, p_sample, g_ple, w_gate, w_proj, g_final, y_prompt, y_sample):
    PC = PLE // P
    W_PIECES = KC + PC
    SLOTS = 4
    with ExitStack() as ctx:
        def sb(name, shape, dt=F32):
            return ctx.enter_context(nc.sbuf_tensor("e_" + name, shape, dt))

        def ps(name, shape):
            return ctx.enter_context(nc.psum_tensor("e_" + name, shape, F32))

        def sems(names):
            return [ctx.enter_context(nc.semaphore("e_" + n)) for n in names.split()]

        wg_hi, wg_lo = sb("wg_hi", [P, KC, D], F32R), sb("wg_lo", [P, KC, D], F32R)
        wp_hi, wp_lo = sb("wp_hi", [P, PC, D], F32R), sb("wp_lo", [P, PC, D], F32R)
        w_raw = sb("w_raw", [P, W_PIECES, D])
        x, p = sb("x", [P, SLOTS, D]), sb("p", [P, SLOTS, PLE])
        h, y, gate = sb("h", [P, 2, D]), sb("y", [P, 2, D]), sb("gate", [P, D])
        gple, gfinal = sb("gple", [P, D]), sb("gfinal", [P, D])
        hT_hi, hT_lo = sb("hT_hi", [P, 2, KC, P], F32R), sb("hT_lo", [P, 2, KC, P], F32R)
        pT_hi, pT_lo = sb("pT_hi", [P, 2, PC, P], F32R), sb("pT_lo", [P, 2, PC, P], F32R)
        ident = sb("ident", [P, P])
        ms, ms_final = sb("ms", [P, 2, 3]), sb("ms_final", [P, 2, 3])
        constants = sb("constants", [P, 2])

        turned, p_turned_ps = ps("turned", [P, KC, P]), ps("p_turned", [P, 4, P])
        gate_ps, ple_ps = ps("gate_ps", [P, D]), ps("ple_ps", [P, D])

        made, gple_in, gfinal_in, w_hi_made, w_lo_made = sems("made gple_in gfinal_in w_hi_made w_lo_made")
        y_out = sems("y_out0 y_out1")
        w_in_sem = sems("w_in0 w_in1 w_in2 w_in3 w_in4")
        tile_in = sems("tile_in0 tile_in1 tile_in2 tile_in3")
        summed, rooted, normed = sems("summed rooted normed")
        final_summed, final_rooted, finished = sems("final_summed final_rooted finished")
        hp_turned, hp_hi, hp_lo = sems("hp_turned hp_hi hp_lo")
        gate_done, ple_done, gated, mixed_in, x_new = sems("gate_done ple_done gated mixed_in x_new")

        def rounds_of_four(eng, body, last):
            first, turns = 3, (NT - 6) // 4
            for r in range(first):
                body(r, r % SLOTS)
            with eng.Fori(0, turns) as turn:
                for k in range(SLOTS):
                    body(turn * SLOTS + (first + k), (first + k) % SLOTS)
            for r in range(first + turns * SLOTS, last + 1):
                body(r, r % SLOTS)

        def h_part(eng, sem, r):
            reached(eng, sem, r * 2 + 1)

        def p_part(eng, sem, r):
            reached(eng, sem, r * 2 + 2)

        def in_slot(eng, r, slot):
            reached(eng, tile_in[slot], r * 8 + 8 * (4 - slot))

        block = ctx.enter_context(nc.Block())

        @block.sync
        def _(sp):
            def load(r, slot):
                t = tile_at(r, slot)
                sp.dma_start(x[0:t.n, slot, :], x_mlp[token_rows(sp, r, t.n), :]).then_inc(tile_in[slot], 16)
                src = p_sample if t.n < P else p_prompt[token_rows(sp, r, P), :]
                sp.dma_start(p[0:t.n, slot, :], src).then_inc(tile_in[slot], 16)

            load(0, 0)
            sp.dma_start(gple[:], g_ple.partition_broadcast(P)).then_inc(gple_in, 16)
            for n in range(0, W_PIECES, 2):
                src = w_gate[n * P:(n + 2) * P, :] if n < KC else w_proj
                sp.dma_start(w_raw[:, n:n + 2, :], src.rearrange("(c p) d -> p c d", p=P)).then_inc(w_in_sem[n // 2], 16)
                if n == 2:
                    load(1, 1)
            sp.dma_start(gfinal[:], g_final.partition_broadcast(P)).then_inc(gfinal_in, 16)

            def body(r, slot):
                if exists(r - 2):
                    t = tile_at(r - 2, slot % 2)
                    dst = y_sample if t.n < P else y_prompt[token_rows(sp, t.i, P), :]
                    all_of(sp, finished, t.i)
                    sp.dma_start(dst, y[0:t.n, t.slot, :]).then_inc(y_out[t.slot], 16)
                if exists(r + 2):
                    load(r + 2, (slot + 2) % SLOTS)

            rounds_of_four(sp, body, NT + 2)
            for slot in (0, 1):
                sp.wait_ge(y_out[slot], 16 * (NT // 2 + 1 - slot))

        @block.gpsimd
        def _(pool):
            make_identity(pool, ident[:], made)
            pool.memset(constants[:, 0:1], EPS).then_inc(made, 1)
            pool.memset(constants[:, 1:2], -0.5).then_inc(made, 1)
            pool.wait_ge(made, 4)

            def body(r, slot):
                if exists(r + 1):
                    t = tile_at(r + 1, (slot + 1) % 2)
                    sums_root(pool, summed, rooted, t.i, ms[0:t.n, t.slot], constants[0:t.n])
                if exists(r - 1):
                    t = tile_at(r - 1, (slot + 1) % 2)
                    sums_root(pool, final_summed, final_rooted, t.i, ms_final[0:t.n, t.slot], constants[0:t.n])

            body(-1, SLOTS - 1)
            rounds_of_four(pool, body, NT + 1)

        @block.scalar
        def _(act):
            def sum_x(r, slot):
                t = tile_at(r, slot % 2)
                in_slot(act, r, slot)
                h_part(act, hp_turned, r - 2)
                all_of(act, rooted, r - 2, 2)
                act.activation(h[0:t.n, t.slot, :], x[0:t.n, slot, :], ACT.Square, scale=D ** -0.5,
                               accum_out=ms[0:t.n, t.slot, 0:1]).then_inc(summed, 1)

            def split(r, slot):
                t = tile_at(r, slot % 2)
                h_part(act, hp_turned, r)
                all_of(act, gate_done, r - 2)
                act.activation(hT_hi[:, t.slot, :, 0:t.n], turned[:, :, 0:t.n], ACT.Copy).then_inc(hp_hi, 1)
                p_part(act, hp_turned, r)
                all_of(act, ple_done, r - 2)
                act.activation(pT_hi[:, t.slot, :, 0:t.n], p_turned_ps[:, 0:PC, 0:t.n], ACT.Copy).then_inc(hp_hi, 1)

            sum_x(0, 0)
            for n in range(W_PIECES):
                act.wait_ge(w_in_sem[n // 2], 16)
                dst, c = (wg_hi, n) if n < KC else (wp_hi, n - KC)
                act.activation(dst[:, c, :], w_raw[:, n, :], ACT.Copy).then_inc(w_hi_made, 1)
                if n == 0:
                    split(0, 0)

            def body(r, slot):
                before = tile_at(r - 1, (slot + 1) % 2)
                m = before.n
                if exists(r - 1):
                    all_of(act, gate_done, r - 1)
                    all_of(act, x_new, r - 2)
                    act.activation(gate[0:m, :], gate_ps[0:m, :], ACT.Sigmoid).then_inc(gated, 1)
                if exists(r + 1):
                    sum_x(r + 1, (slot + 1) % SLOTS)
                if exists(r - 1):
                    all_of(act, x_new, r - 1)
                    all_of(act, final_rooted, r - 3, 2)
                    slot_loaded(act, y_out, tile_at(r - 3, before.slot))
                    act.activation(y[0:m, before.slot, :], x[0:m, (slot + 3) % SLOTS, :], ACT.Square, scale=D ** -0.5,
                                   accum_out=ms_final[0:m, before.slot, 0:1]).then_inc(final_summed, 1)
                if exists(r + 1):
                    split(r + 1, (slot + 1) % SLOTS)

            rounds_of_four(act, body, NT + 1)

        @block.tensor
        def _(pe):
            pe.wait_ge(made, 2)

            def turn(r, slot):
                t = tile_at(r, slot % 2)
                all_of(pe, normed, r)
                h_part(pe, hp_lo, r - 1)
                for c in range(KC):
                    ins = pe.transpose(turned[:, c, 0:t.n], h[0:t.n, t.slot, c * P:(c + 1) * P], ident[0:t.n, 0:t.n])
                ins.then_inc(hp_turned, 1)
                in_slot(pe, r, slot)
                p_part(pe, hp_lo, r - 1)
                for c in range(PC):
                    ins = pe.transpose(p_turned_ps[:, c, 0:t.n], p[0:t.n, slot, c * P:(c + 1) * P], ident[0:t.n, 0:t.n])
                ins.then_inc(hp_turned, 1)

            turn(0, 0)

            def body(r, slot):
                s = slot % 2
                h_part(pe, hp_lo, r)
                all_of(pe, gated, r - 1)
                for c in range(D // NB):
                    cols = slice(c * NB, (c + 1) * NB)
                    for n in range(KC):
                        if isinstance(r, int) and r == 0 and c == 0:
                            pe.wait_ge(w_lo_made, n + 1)
                        ins = split_product(pe, gate_ps[:, cols], (lambda k: hT_hi[:, s, k, :], lambda k: hT_lo[:, s, k, :]),
                                            (lambda k: wg_hi[:, k, cols], lambda k: wg_lo[:, k, cols]), [n], n == 0, n == KC - 1)
                    if c == 0 and exists(r + 1):
                        turn(r + 1, (slot + 1) % SLOTS)
                ins.then_inc(gate_done, 1)
                p_part(pe, hp_lo, r)
                all_of(pe, mixed_in, r - 1)
                if isinstance(r, int) and r == 0:
                    pe.wait_ge(w_lo_made, W_PIECES)
                for c in range(D // NB):
                    cols = slice(c * NB, (c + 1) * NB)
                    ins = split_product(pe, ple_ps[:, cols], (lambda k: pT_hi[:, s, k, :], lambda k: pT_lo[:, s, k, :]),
                                        (lambda k: wp_hi[:, k, cols], lambda k: wp_lo[:, k, cols]), range(PC))
                ins.then_inc(ple_done, 1)

            rounds_of_four(pe, body, NT)

        @block.vector
        def _(dve):
            def norm(r, slot):
                t = tile_at(r, slot % 2)
                all_of(dve, rooted, r, 2)
                dve.scalar_tensor_tensor(h[0:t.n, t.slot, :], x[0:t.n, slot, :], ms[0:t.n, t.slot, 2:3],
                                         gple[0:t.n, :], ALU.mult, ALU.mult).then_inc(normed, 1)

            def split(r, slot):
                t = tile_at(r, slot % 2)
                h_part(dve, hp_hi, r)
                dve.tensor_tensor(hT_lo[:, t.slot, :, 0:t.n], turned[:, :, 0:t.n], hT_hi[:, t.slot, :, 0:t.n], ALU.subtract).then_inc(hp_lo, 1)
                p_part(dve, hp_hi, r)
                dve.tensor_tensor(pT_lo[:, t.slot, :, 0:t.n], p_turned_ps[:, 0:PC, 0:t.n], pT_hi[:, t.slot, :, 0:t.n], ALU.subtract).then_inc(hp_lo, 1)

            dve.wait_ge(gple_in, 16)
            norm(0, 0)
            for n in range(W_PIECES):
                hi, lo, c = (wg_hi, wg_lo, n) if n < KC else (wp_hi, wp_lo, n - KC)
                dve.wait_ge(w_hi_made, n + 1)
                dve.tensor_tensor(lo[:, c, :], w_raw[:, n, :], hi[:, c, :], ALU.subtract).then_inc(w_lo_made, 1)
                if n == 0:
                    split(0, 0)
            dve.wait_ge(gfinal_in, 16)

            def body(r, slot):
                before = tile_at(r - 1, (slot + 1) % 2)
                m, s = before.n, before.slot
                xb = x[0:m, (slot + 3) % SLOTS, :]
                if exists(r - 1):
                    all_of(dve, ple_done, r - 1)
                    all_of(dve, gated, r - 1)
                    dve.tensor_tensor(gate[0:m, :], gate[0:m, :], ple_ps[0:m, :], ALU.mult).then_inc(mixed_in, 1)
                    all_of(dve, mixed_in, r - 1)
                    dve.tensor_tensor(xb, xb, gate[0:m, :], ALU.add).then_inc(x_new, 1)
                if exists(r + 1):
                    norm(r + 1, (slot + 1) % SLOTS)
                if exists(r - 1):
                    all_of(dve, final_rooted, r - 1, 2)
                    dve.scalar_tensor_tensor(y[0:m, s, :], xb, ms_final[0:m, s, 2:3], gfinal[0:m, :], ALU.mult, ALU.mult).then_inc(finished, 1)
                if exists(r + 1):
                    split(r + 1, (slot + 1) % SLOTS)

            rounds_of_four(dve, body, NT + 1)

def build(nc, x_prompt, x_sample, cache_k, cache_v, state_c, state_n, state_m, p_prompt, p_sample,
          g_mix, w_in, b_igate, b_fgate, g_head, sinks, w_out, g_mlp, w_up, w_down, g_ple,
          w_ple_gate, w_ple_proj, g_final, y_prompt, y_sample, pk, pv, pc, pn, pm, sk, sv, sc, sn, sm):
    mixed = nc.dram_tensor("mixed_heads", [TOK, MW], F32, kind="Internal").ap()
    mlstm_phase(nc, x_prompt[0], x_sample[0], g_mix[0], w_in[0], b_igate[0], b_fgate[0], g_head[0],
                state_c[0, 0], state_n[0, 0], state_m[0, 0], mixed,
                (pc[0, 0], sc[0, 0]), (pn[0, 0], sn[0, 0]), (pm[0, 0], sm[0, 0]))
    flat = lambda a: a[0, 0].rearrange("w h d -> w (h d)")
    x_mid = nc.dram_tensor("x_after_mixers", [TOK, D], F32, kind="Internal").ap()
    attention_phase(nc, x_prompt[0], x_sample[0], g_mix[0], w_in[0], sinks[0], w_out[0], flat(cache_k), flat(cache_v),
                    mixed, x_mid, (flat(pk), flat(sk)), (flat(pv), flat(sv)))
    x_mlp = nc.dram_tensor("x_after_mlp", [TOK, D], F32, kind="Internal").ap()
    mlp_phase(nc, x_mid, g_mlp[0], w_up[0], w_down[0], x_mlp)
    ple_phase(nc, x_mlp, p_prompt[0, 0], p_sample[0, 0], g_ple[0], w_ple_gate[0], w_ple_proj[0], g_final, y_prompt[0], y_sample[0])


_INS = ["x_prompt", "x_sample", "cache_swa_k", "cache_swa_v", "state_mlstm_c", "state_mlstm_n", "state_mlstm_m",
        "p_prompt", "p_sample", "g_mix", "w_in", "b_igate", "b_fgate", "g_head", "attn_sinks", "w_out", "g_mlp",
        "w_up", "w_down", "g_ple", "w_ple_gate", "w_ple_proj", "g_final"]
_STATE = [(1, 1, HEADS, QK, QK), (1, 1, HEADS, QK), (1, 1, HEADS)]
_WINDOW = (1, 1, P, KVH, HD)
_OUTS = [(1, SEQ, D), (1, DEC, D), _WINDOW, _WINDOW, *_STATE, _WINDOW, _WINDOW, *_STATE]


def kernel(**inputs):
    import numpy as _np
    import concourse.bacc as _bacc
    from concourse import mybir as _mybir
    from concourse.bass_utils import run_bass_kernel_spmd as _run

    nc = _bacc.Bacc("TRN2", target_bir_lowering=False, num_devices=1)
    arrays, args = {}, []
    for name in _INS:
        a = _np.ascontiguousarray(inputs[name])
        arrays[f"in_{name}"] = a
        args.append(nc.dram_tensor(f"in_{name}", a.shape, _mybir.dt.from_np(a.dtype), kind="ExternalInput").ap())
    for i, shape in enumerate(_OUTS):
        args.append(nc.dram_tensor(f"out_{i}", shape, _mybir.dt.float32, kind="ExternalOutput").ap())
    build(nc, *args)
    r = _run(nc, [arrays], core_ids=[0])
    return tuple(r.results[0][f"out_{i}"] for i in range(len(_OUTS)))
```

```python
from contextlib import ExitStack
from typing import NamedTuple

import concourse.bass as bass
from concourse import mybir

F32 = mybir.dt.float32
F32R = mybir.dt.float32r
ALU = mybir.AluOpType
ACT = mybir.ActivationFunctionType
AX = mybir.AxisListType

P = 128
D = 1024
KC = D // P
SEQ, DEC = 2048, 32
NT = SEQ // P
TOK = SEQ + DEC
HEADS, QK = 4, 128
VA = QK + 1
MW = HEADS * QK
GATE_COL = 4 * MW
Q_COL = GATE_COL + 2 * HEADS
AH, KVH, HD = 8, 2, 64
GRP = AH // KVH
AW = AH * HD
KV_COL = Q_COL + AW
KVW = KVH * HD
FF = 4 * D
PLE = 256
EPS = 1e-6
MASKED = -1e30
MLP_BLOCK = 256
NB = 512


class Tile(NamedTuple):
    i: object
    slot: int
    n: int


def tile_at(i, slot):
    return Tile(i, slot, DEC if isinstance(i, int) and i == NT else P)


def reached(eng, sem, count):
    if isinstance(count, int) and count <= 0:
        return
    eng.wait_ge(sem, count)


def all_of(eng, sem, i, per=1):
    reached(eng, sem, (i + 1) * per)


def slot_loaded(eng, sems, t):
    reached(eng, sems[t.slot], t.i * 8 + 16 - 8 * t.slot)


def rounds(eng, body, last):
    for r in range(3):
        body(r, r % 2)
    with eng.Fori(0, (NT - 6) // 2) as turn:
        body(turn * 2 + 3, 1)
        body(turn * 2 + 4, 0)
    for r in range(NT - 3, last + 1):
        body(r, r % 2)


def exists(i):
    return not isinstance(i, int) or 0 <= i <= NT


def split_product(eng, out, lhs, rhs, chunks, first=True, last=True):
    (lh, ll), (rh, rl) = lhs, rhs
    for k in chunks:
        f, e = first and k == chunks[0], last and k == chunks[-1]
        eng.matmul(out, lh(k), rh(k), start=f, stop=False)
        eng.matmul(out, lh(k), rl(k), start=False, stop=False)
        ins = eng.matmul(out, ll(k), rh(k), start=False, stop=e)
    return ins


def token_rows(eng, i, n):
    return slice(i * P, i * P + n) if isinstance(i, int) else bass.ds(eng.snap(i * P), n)


def norm_rows(dve, sem, rooted, i, x, gain, out, stats, ms):
    base = i * NORM
    groups = 2 * D // NB
    for c in range(D // NB):
        ins = dve.bn_stats(stats[:, c, :], x[:, c * NB:(c + 1) * NB])
    ins.then_inc(sem, 1)
    by_group = stats.rearrange("p c (g s) -> p (c g) s", s=3)
    mean, spread = by_group[:, :, 1], by_group[:, :, 2]
    dve.wait_ge(sem, base + 1)
    dve.tensor_tensor(ms[:, 0:groups], mean, mean, ALU.mult).then_inc(sem, 1)
    dve.wait_ge(sem, base + 2)
    dve.scalar_tensor_tensor(ms[:, 0:groups], ms[:, 0:groups], float(D // groups), spread, ALU.mult, ALU.add).then_inc(sem, 1)
    dve.wait_ge(sem, base + 3)
    dve.reduce_sum(ms[:, 4:5], ms[:, 0:groups], AX.X).then_inc(sem, 1)
    dve.wait_ge(sem, base + 4)
    dve.tensor_scalar(ms[:, 5:6], ms[:, 4:5], 1.0 / D, EPS, ALU.mult, ALU.add).then_inc(sem, 1)
    all_of(dve, rooted, i)
    dve.scalar_tensor_tensor(out, x, ms[:, 6:7], gain, ALU.mult, ALU.mult).then_inc(sem, 1)


def norm_root(pool, sem, rooted, i, ms, minus_half):
    reached(pool, sem, i * NORM + 5)
    pool.tensor_tensor(ms[:, 6:7], ms[:, 5:6], minus_half, ALU.pow).then_inc(rooted, 1)


def sums_root(pool, summed, rooted, i, ms, constants):
    all_of(pool, summed, i)
    pool.tensor_tensor(ms[:, 1:2], ms[:, 0:1], constants[:, 0:1], ALU.add).then_inc(rooted, 1)
    reached(pool, rooted, i * 2 + 1)
    pool.tensor_tensor(ms[:, 2:3], ms[:, 1:2], constants[:, 1:2], ALU.pow).then_inc(rooted, 1)


NORM = 6


def make_identity(pool, ident, made):
    pool.memset(ident, 0.0).then_inc(made, 1)
    pool.wait_ge(made, 1)
    pool.affine_select(out=ident, in_=ident, compare_op=ALU.not_equal, fill=1.0, base=0,
                       pattern=[[-1, P]], channel_multiplier=1).then_inc(made, 1)


def mlstm_phase(nc, x_prompt, x_sample, g_mix, w_in, b_igate, b_fgate, g_head, state_c, state_n, state_m,
                mixed, out_c, out_n, out_m, x, gmix):
    AHEAD = NT + 2
    MC = Q_COL
    PC = D
    PIECES = [(c, col) for col in (PC, 0) for c in range(KC)]
    OG = 2 * HEADS + MW // 2
    with ExitStack() as ctx:
        def sb(name, shape, dt=F32):
            return ctx.enter_context(nc.sbuf_tensor("m_" + name, shape, dt))

        def ps(name, shape):
            return ctx.enter_context(nc.psum_tensor("m_" + name, shape, F32))

        def sem(name):
            return ctx.enter_context(nc.semaphore("m_" + name))

        w_hi, w_lo = sb("w_hi", [P, KC, MC], F32R), sb("w_lo", [P, KC, MC], F32R)
        w_raw = sb("w_raw", [P, PC])
        hT_hi, hT_lo = sb("hT_hi", [P, 2, KC, P], F32R), sb("hT_lo", [P, 2, KC, P], F32R)
        q, k = sb("q", [P, 2, MW]), sb("k", [P, 2, MW])
        v, o = sb("v", [P, 2, HEADS, VA]), sb("o", [P, 2, MW])
        qkT, qsT = sb("qkT", [P, 2, HEADS, P]), sb("qsT", [P, HEADS, P])
        qT, kT = qkT[:, 0], qkT[:, 1]
        decay = sb("decay", [P, HEADS, P])
        C, C_new, C_dec = (sb(n, [P, HEADS, VA]) for n in ("C", "C_new", "C_dec"))
        heads_out = sb("heads_out", [P, MW])
        ghead = sb("ghead", [P, MW])
        causal = sb("causal", [P, P])
        ident = sb("ident", [P, P])
        pick = sb("pick", [HEADS, HEADS, P])
        gates = sb("gates", [P, 2 * HEADS])
        gbias = sb("gbias", [HEADS, 2])
        rows = sb("rows", [HEADS, 8, P])
        m_rows = sb("m_rows", [HEADS, 2, P])
        m_dec = sb("m_dec", [HEADS, 1])
        ones_row, zero_row = sb("ones_row", [HEADS, P]), sb("zero_row", [HEADS, P])
        cols = sb("cols", [P, 16])
        stats, ms = sb("stats", [P, 2, 6]), sb("ms", [P, 8])
        minus_half = sb("minus_half", [P, HEADS])
        fin = sb("fin", [P, 8, HEADS])
        raw = [w_raw[:]] + [b.rearrange("p a b -> p (a b)") for b in (q, k, o)]
        raw += [b.rearrange("p a h d -> p (a h d)")[:, 0:PC] for b in (v, qkT)]
        gates_raw = decay[:, 0, 0:KC * 2 * HEADS].rearrange("p (c g) -> p c g", c=KC)
        WAVE = 3
        I_ROW, F_ROW, F_ABS, F_EXP, B, G, U, W = range(8)
        LOG1P, LF = F_EXP, F_ROW
        E_ROW = F_ABS

        proj = [ps("proj0", [P, NB]), ps("proj1", [P, NB])]
        turned = ps("turned", [P, KC, P])
        wide = ps("wide", [P, HEADS, P])
        small = ps("small", [P, NB])
        acc = ps("acc", [P, HEADS, 256])
        O_GATES, ROWS, COLS = small[:, 0:OG], small[0:HEADS, 0:2 * P], small[:, OG + 8:OG + 24]
        first_q, first_k = (acc[:, 2 * n:2 * n + 2, :].rearrange("p a b -> p (a b)") for n in (0, 1))
        junk = qsT

        ident_made, consts_in, const_sb = sem("ident_made"), sem("consts_in"), sem("const_sb")
        w_in_sem, w_hi_made, w_lo_made = [sem("w_raw0"), sem("w_raw1")], sem("w_hi_made"), sem("w_lo_made")
        x_in, normed, h_turned = [sem("x_in0"), sem("x_in1")], sem("normed"), sem("h_turned")
        h_hi, h_lo, rooted, heads_rooted = sem("h_hi"), sem("h_lo"), sem("rooted"), sem("heads_rooted")
        og_ps, gates_sb, rows_ps, row_step, row_act = (sem(n) for n in ("og_ps", "gates_sb", "rows_ps", "row_step", "row_act"))
        q_ps, k_ps, v_ps, o_ps = (sem(n) for n in ("q_ps", "k_ps", "v_ps", "o_ps"))
        q_sb, k_sb, v_sb, o_sb = (sem(n) for n in ("q_sb", "k_sb", "v_sb", "o_sb"))
        cols_ps, cols_sb, masked, decayed = (sem(n) for n in ("cols_ps", "cols_sb", "masked", "decayed"))
        qk_turned, qT_sb, kT_sb, q_scaled, k_scaled = (sem(n) for n in ("qk_turned", "qT_sb", "kT_sb", "q_scaled", "k_scaled"))
        qs_turned, qsT_sb, scores_ps, state_ps = (sem(n) for n in ("qs_turned", "qsT_sb", "scores_ps", "state_ps"))
        weighted, C_made, C_moved, num_ps, squared, fin_step, out_done, state_out = (
            sem(n) for n in ("weighted", "C_made", "C_moved", "num_ps", "squared", "fin_step", "out_done", "state_out"))
        ROW_STEPS, ROW_ACTS, FIN_STEPS = 8, 4, 11
        N_CONST = 8

        def first_round(r):
            return isinstance(r, int) and r == 0

        def wanted(i):
            return not isinstance(i, int) or i <= AHEAD

        block = ctx.enter_context(nc.Block())

        @block.sync
        def _(sp):
            def load_weights(pieces):
                for n in pieces:
                    (c, col), slot = PIECES[n], n % len(raw)
                    before = n - len(raw)
                    reached(sp, w_lo_made, before + 1 + (before >= KC))
                    sp.dma_start(raw[slot], w_in[c * P:(c + 1) * P, col:col + PC]).then_inc(w_in_sem[slot // WAVE], 16)

            sp.dma_start(x[:, 0, :], x_prompt[0:P, :]).then_inc(x_in[0], 16)
            sp.dma_start(gmix[:], g_mix.partition_broadcast(P)).then_inc(consts_in, 16)
            load_weights(range(WAVE))
            sp.wait_ge(consts_in, 16)
            sp.dma_start(x[:, 1, :], x_prompt[P:2 * P, :]).then_inc(x_in[1], 16)
            sp.dma_start(gbias[:, 0:1], b_igate.rearrange("(h a) -> h a", a=1)).then_inc(consts_in, 16)
            sp.dma_start(gbias[:, 1:2], b_fgate.rearrange("(h a) -> h a", a=1)).then_inc(consts_in, 16)
            sp.dma_start(ghead[:], g_head.partition_broadcast(P)).then_inc(consts_in, 16)
            sp.dma_start(m_dec[:], state_m.rearrange("(h a) -> h a", a=1)).then_inc(consts_in, 16)
            sp.dma_start(C_dec[:, :, 0:QK], state_c.rearrange("h d v -> d h v")).then_inc(consts_in, 16)
            sp.dma_start(C_dec[:, :, QK], state_n.rearrange("h d -> d h"), allow_slow_non_contiguous=True).then_inc(consts_in, 16)
            gate_cols = w_in[:, GATE_COL:MC].rearrange("(c p) g -> p c g", p=P)
            sp.dma_start(gates_raw, gate_cols, allow_slow_non_contiguous=True).then_inc(consts_in, 16)
            load_weights(range(WAVE, len(PIECES)))

            def body(r, slot):
                j = r - 1
                if wanted(r + 2):
                    nxt = tile_at(r + 2, slot)
                    first = (r + 2) % (NT + 1) if isinstance(r, int) else nxt.i
                    src = x_sample if nxt.n < P else x_prompt[token_rows(sp, first, P), :]
                    all_of(sp, h_turned, r)
                    sp.dma_start(x[0:nxt.n, nxt.slot, :], src).then_inc(x_in[nxt.slot], 16)
                if exists(j):
                    t = tile_at(j, 1 - slot)
                    dst = mixed[token_rows(sp, j, t.n), :]
                    all_of(sp, fin_step, j, FIN_STEPS)
                    sp.dma_start(dst, heads_out[0:t.n, :]).then_inc(out_done, 16)
                if isinstance(j, int) and j >= NT - 1:
                    which = j - (NT - 1)
                    all_of(sp, C_made, j)
                    all_of(sp, row_step, j, ROW_STEPS)
                    n = tile_at(j, 0).n
                    sp.dma_start(out_c[which].rearrange("h d v -> d h v"), C_new[:, :, 0:QK]).then_inc(state_out, 16)
                    sp.dma_start(out_n[which].rearrange("h d -> d h"), C_new[:, :, QK], allow_slow_non_contiguous=True).then_inc(state_out, 16)
                    sp.dma_start(out_m[which].rearrange("(h a) -> h a", a=1), m_rows[:, j % 2, n - 1:n]).then_inc(state_out, 16)

            rounds(sp, body, NT + 1)
            sp.wait_ge(out_done, 16 * (NT + 1))
            sp.wait_ge(state_out, 16 * 6)

        @block.gpsimd
        def _(pool):
            make_identity(pool, ident[:], ident_made)
            pool.memset(causal[:], 0.0).then_inc(ident_made, 1)
            pool.wait_ge(ident_made, 3)
            pool.affine_select(out=causal[:], in_=causal[:], compare_op=ALU.is_ge, fill=MASKED, base=0,
                               pattern=[[1, P]], channel_multiplier=-1).then_inc(ident_made, 1)
            pool.memset(minus_half[:], -0.5).then_inc(ident_made, 1)
            pool.wait_ge(ident_made, 5)

            def root(t):
                norm_root(pool, normed, rooted, t.i, ms[0:t.n], minus_half[0:t.n, 0:1])

            root(tile_at(0, 0))
            root(tile_at(1, 1))

            def body(r, slot):
                if wanted(r + 2):
                    root(tile_at(r + 2, slot))
                if exists(r - 1):
                    m = tile_at(r - 1, 1 - slot).n
                    reached(pool, fin_step, (r - 1) * FIN_STEPS + 9)
                    pool.tensor_tensor(fin[0:m, 3, :], fin[0:m, 6, :], minus_half[0:m, :], ALU.pow).then_inc(heads_rooted, 1)

            rounds(pool, body, NT + 1)

        @block.scalar
        def _(act):
            def split_h(t):
                all_of(act, h_turned, t.i)
                all_of(act, o_ps, t.i - 2)
                act.activation(hT_hi[:, t.slot, :, 0:t.n], turned[:, :, 0:t.n], ACT.Copy).then_inc(h_hi, 1)

            for n, (c, col) in enumerate(PIECES):
                slot = n % len(raw)
                first = n - slot % WAVE
                last = min(first + WAVE, len(PIECES))
                loaded = sum(1 for m in range(last) if m % len(raw) // WAVE == slot // WAVE)
                act.wait_ge(w_in_sem[slot // WAVE], 16 * loaded)
                act.activation(w_hi[:, c, col:col + PC], raw[slot], ACT.Copy).then_inc(w_hi_made, 1)
                if n == WAVE - 1:
                    split_h(tile_at(0, 0))
                if n == KC - 1:
                    act.wait_ge(consts_in, 16 * N_CONST)
                    act.activation(w_hi[:, :, GATE_COL:MC], gates_raw, ACT.Copy).then_inc(w_hi_made, 1)

            act.wait_ge(w_lo_made, len(PIECES) + 1)

            def take_q(t):
                all_of(act, q_ps, t.i)
                src = first_q if first_round(t.i) else proj[0]
                act.activation(q[0:t.n, t.slot, :], src[0:t.n, :], ACT.Copy).then_inc(q_sb, 1)

            def take_k(t):
                all_of(act, k_ps, t.i)
                src = first_k if first_round(t.i) else proj[1]
                act.activation(k[0:t.n, t.slot, :], src[0:t.n, :], ACT.Copy, scale=QK ** -0.5).then_inc(k_sb, 1)

            def body(r, slot):
                i, j = r, r - 1
                cur, mix = tile_at(i, slot), tile_at(j, 1 - slot)
                n = cur.n
                if exists(i):
                    all_of(act, og_ps, i)
                    all_of(act, fin_step, i - 2, FIN_STEPS)
                    act.activation(gates[0:n, :], O_GATES[0:n, MW // 2:OG], ACT.Copy)
                    act.activation(o[0:n, slot, MW // 2:MW], O_GATES[0:n, 0:MW // 2], ACT.Exp, scale=-1.0).then_inc(gates_sb, 1)
                    if not first_round(r):
                        take_q(cur)
                if exists(r + 1):
                    split_h(tile_at(r + 1, 1 - slot))
                if exists(j):
                    all_of(act, masked, j)
                    all_of(act, cols_sb, j, 2)
                    for h in range(HEADS):
                        ins = act.activation(decay[0:mix.n, h, 0:mix.n], decay[0:mix.n, h, 0:mix.n], ACT.Exp, bias=cols[0:mix.n, h:h + 1])
                    ins.then_inc(decayed, 1)
                if exists(i) and not first_round(r):
                    take_k(cur)
                if exists(j):
                    all_of(act, qk_turned, j)
                    act.activation(qT[:, :, 0:mix.n], turned[:, 0:HEADS, 0:mix.n], ACT.Copy).then_inc(qT_sb, 1)
                if exists(i):
                    reached(act, row_step, i * ROW_STEPS + 2)
                    act.activation(rows[:, F_EXP, 0:n], rows[:, F_ABS, 0:n], ACT.Exp, scale=-1.0).then_inc(row_act, 1)
                    reached(act, row_act, i * ROW_ACTS + 1)
                    act.activation(rows[:, LOG1P, 0:n], rows[:, F_EXP, 0:n], ACT.Ln, bias=1.0).then_inc(row_act, 1)
                if exists(j):
                    all_of(act, qs_turned, j)
                    all_of(act, squared, j - 1)
                    act.activation(qsT[:, :, 0:mix.n], turned[:, 0:HEADS, 0:mix.n], ACT.Copy).then_inc(qsT_sb, 1)
                if exists(i):
                    all_of(act, o_ps, i)
                    act.activation(o[0:n, slot, 0:MW // 2], proj[1][0:n, 0:MW // 2], ACT.Exp, scale=-1.0).then_inc(o_sb, 1)
                    reached(act, row_step, i * ROW_STEPS + 7)
                    m_in = m_dec[:] if n < P else m_rows[:, 1 - slot, P - 1:P]
                    act.activation(rows[:, W, 0:n], rows[:, U, 0:n], ACT.Exp, scale=-1.0, bias=m_in).then_inc(row_act, 1)
                    reached(act, row_step, i * ROW_STEPS + 8)
                    act.activation(rows[:, E_ROW, 0:n], m_rows[:, slot, 0:n], ACT.Exp, scale=-1.0).then_inc(row_act, 1)
                if first_round(r):
                    take_q(cur)
                    take_k(cur)
                if exists(j):
                    all_of(act, num_ps, j)
                    reached(act, fin_step, (j - 1) * FIN_STEPS + 10)
                    for h in range(HEADS):
                        ins = act.activation(junk[0:mix.n, h, :], acc[0:mix.n, h, 0:QK], ACT.Square, accum_out=fin[0:mix.n, 3, h:h + 1])
                    ins.then_inc(squared, 1)
                    all_of(act, C_made, j)
                    act.activation(C[:], C_new[:], ACT.Copy).then_inc(C_moved, 1)

            rounds(act, body, NT + 1)

        @block.tensor
        def _(pe):
            pe.wait_ge(ident_made, 2)

            def turn_h(t):
                all_of(pe, normed, t.i, NORM)
                all_of(pe, qsT_sb, t.i - 3)
                for c in range(KC):
                    ins = pe.transpose(turned[:, c, 0:t.n], x[0:t.n, t.slot, c * P:(c + 1) * P], ident[0:t.n, 0:t.n])
                ins.then_inc(h_turned, 1)

            def project(out, t, c0, width, done):
                split_product(pe, out, (lambda c: hT_hi[:, t.slot, c, :], lambda c: hT_lo[:, t.slot, c, :]),
                              (lambda c: w_hi[:, c, c0:c0 + width], lambda c: w_lo[:, c, c0:c0 + width]),
                              range(KC)).then_inc(done, 1)

            def turn_gates(t):
                all_of(pe, gates_sb, t.i)
                all_of(pe, cols_sb, t.i - 1, 2)
                pe.transpose(ROWS[:, 0:t.n], gates[0:t.n, 0:HEADS], ident[0:t.n, 0:t.n])
                pe.transpose(ROWS[:, P:P + t.n], gates[0:t.n, HEADS:2 * HEADS], ident[0:t.n, 0:t.n]).then_inc(rows_ps, 1)

            def project_by_chunk(t, targets, made_before):
                for c in range(KC):
                    pe.wait_ge(w_lo_made, made_before + c + 1)
                    for out, c0, width, done in targets:
                        ins = split_product(pe, out, (lambda c: hT_hi[:, t.slot, c, :], lambda c: hT_lo[:, t.slot, c, :]),
                                            (lambda c: w_hi[:, c, c0:c0 + width], lambda c: w_lo[:, c, c0:c0 + width]),
                                            [c], c == 0, c == KC - 1)
                        if c == KC - 1:
                            ins.then_inc(done, 1)

            turn_h(tile_at(0, 0))

            def body(r, slot):
                i, j = r, r - 1
                cur, mix = tile_at(i, slot), tile_at(j, 1 - slot)
                n, m = cur.n, mix.n
                if exists(i):
                    all_of(pe, h_hi, i)
                    all_of(pe, h_lo, i)
                    all_of(pe, cols_sb, i - 2, 2)
                    reached(pe, row_step, (i - 1) * ROW_STEPS + 3)
                    if first_round(r):
                        project_by_chunk(cur, [(proj[0][:], 2 * MW, MW, v_ps), (proj[1][:, 0:MW // 2], 3 * MW, MW // 2, o_ps)], 0)
                        pe.wait_ge(w_lo_made, KC + 1)
                    project(O_GATES, cur, MC - OG, OG, og_ps)
                    if not first_round(r):
                        all_of(pe, v_sb, i - 1)
                        project(proj[0][:], cur, 0, MW, q_ps)
                if exists(j):
                    all_of(pe, row_act, j, ROW_ACTS)
                    all_of(pe, row_step, j, ROW_STEPS)
                    all_of(pe, weighted, j - 1)
                    all_of(pe, gates_sb, min(i, NT) if isinstance(i, int) else i)
                    for h in range(HEADS):
                        pe.matmul(wide[0:m, h, 0:m], pick[:, h, 0:m], rows[:, U, 0:m], start=True, stop=True)
                    for c, row in enumerate((G, W, E_ROW)):
                        pe.transpose(COLS[0:m, c * HEADS:(c + 1) * HEADS], rows[:, row, 0:m], ident[0:HEADS, 0:HEADS])
                    for h in range(HEADS):
                        ins = pe.matmul(COLS[:, 3 * HEADS + h:3 * HEADS + h + 1], pick[:, h, :], rows[:, W, m - 1:m], start=True, stop=True)
                    ins.then_inc(cols_ps, 1)
                if exists(r + 1):
                    turn_h(tile_at(r + 1, 1 - slot))
                if exists(i) and not first_round(r):
                    all_of(pe, o_sb, i - 1)
                    project(proj[1][:], cur, MW, MW, k_ps)
                if exists(j):
                    if exists(r + 1):
                        all_of(pe, h_hi, r + 1)
                        all_of(pe, h_lo, r + 1)
                    else:
                        all_of(pe, qsT_sb, j - 1)
                    all_of(pe, q_sb, j)
                    all_of(pe, k_sb, j)
                    for h in range(HEADS):
                        pe.transpose(turned[:, h, 0:m], q[0:m, mix.slot, h * QK:(h + 1) * QK], ident[0:m, 0:m])
                    for h in range(HEADS):
                        ins = pe.transpose(turned[:, HEADS + h, 0:m], k[0:m, mix.slot, h * QK:(h + 1) * QK], ident[0:m, 0:m])
                    ins.then_inc(qk_turned, 1)
                if exists(i):
                    if not first_round(r):
                        turn_gates(cur)
                        all_of(pe, q_sb, i)
                        project(proj[0][:], cur, 2 * MW, MW, v_ps)
                if exists(j):
                    all_of(pe, q_scaled, j)
                    all_of(pe, qT_sb, j)
                    all_of(pe, kT_sb, j)
                    for h in range(HEADS):
                        ins = pe.transpose(turned[:, h, 0:m], q[0:m, mix.slot, h * QK:(h + 1) * QK], ident[0:m, 0:m])
                    ins.then_inc(qs_turned, 1)
                    all_of(pe, masked, j)
                    for h in range(HEADS):
                        ins = pe.matmul(wide[0:m, h, 0:m], kT[:, h, 0:m], qT[:, h, 0:m], start=True, stop=True)
                    ins.then_inc(scores_ps, 1)
                    all_of(pe, k_scaled, j)
                    all_of(pe, v_sb, j)
                    all_of(pe, fin_step, j - 1, FIN_STEPS)
                    for h in range(HEADS):
                        ins = pe.matmul(acc[:, h, 0:VA], k[0:m, mix.slot, h * QK:(h + 1) * QK], v[0:m, mix.slot, h, :], start=True, stop=True)
                    ins.then_inc(state_ps, 1)
                if exists(i):
                    if not first_round(r):
                        all_of(pe, k_sb, i)
                        project(proj[1][:, 0:MW // 2], cur, 3 * MW, MW // 2, o_ps)
                if first_round(r):
                    project_by_chunk(cur, [(first_q, 0, MW, q_ps), (first_k, MW, MW, k_ps)], KC + 1)
                    turn_gates(cur)
                    pe.wait_ge(const_sb, 1)
                if exists(j):
                    all_of(pe, qsT_sb, j)
                    all_of(pe, weighted, j)
                    all_of(pe, C_made, j)
                    if m == P:
                        all_of(pe, C_moved, j - 1)
                    state = C if m == P else C_dec
                    for h in range(HEADS):
                        pe.matmul(acc[0:m, h, 0:VA], qsT[:, h, 0:m], state[:, h, :], start=True, stop=False)
                        ins = pe.matmul(acc[0:m, h, 0:VA], decay[0:m, h, 0:m], v[0:m, mix.slot, h, :], start=False, stop=True)
                    ins.then_inc(num_ps, 1)

            rounds(pe, body, NT + 1)

        @block.vector
        def _(dve):
            def norm(t):
                slot_loaded(dve, x_in, t)
                xt = x[0:t.n, t.slot, :]
                norm_rows(dve, normed, rooted, t.i, xt, gmix[0:t.n, :], xt, stats[0:t.n], ms[0:t.n])

            def split_h(t):
                all_of(dve, h_hi, t.i)
                dve.tensor_tensor(hT_lo[:, t.slot, :, 0:t.n], turned[:, :, 0:t.n], hT_hi[:, t.slot, :, 0:t.n], ALU.subtract).then_inc(h_lo, 1)

            def output_gate(t):
                all_of(dve, o_sb, t.i)
                ot = o[0:t.n, t.slot, :]
                dve.tensor_scalar(ot, ot, 1.0, None, ALU.add).then_inc(fin_step, 1)
                dve.wait_ge(fin_step, t.i * FIN_STEPS + 1)
                dve.reciprocal(ot, ot).then_inc(fin_step, 1)
                dve.wait_ge(fin_step, t.i * FIN_STEPS + 2)
                dve.tensor_tensor(ot, ot, ghead[0:t.n, :], ALU.mult).then_inc(fin_step, 1)

            dve.wait_ge(consts_in, 16)
            norm(tile_at(0, 0))
            for n, (c, col) in enumerate(PIECES):
                cols_of = slice(col, col + PC)
                dve.wait_ge(w_hi_made, n + 1 + (n >= KC))
                dve.tensor_tensor(w_lo[:, c, cols_of], raw[n % len(raw)], w_hi[:, c, cols_of], ALU.subtract).then_inc(w_lo_made, 1)
                if n == WAVE - 1:
                    split_h(tile_at(0, 0))
                if n == KC - 1:
                    dve.wait_ge(w_hi_made, n + 2)
                    dve.tensor_tensor(w_lo[:, :, GATE_COL:MC], gates_raw, w_hi[:, :, GATE_COL:MC], ALU.subtract).then_inc(w_lo_made, 1)
                    norm(tile_at(1, 1))
                if n == KC:
                    dve.memset(C[:], 0.0)
                    dve.memset(m_rows[:], 0.0)
                    dve.memset(ones_row[:], 1.0)
                    dve.memset(zero_row[:], 0.0)
                    dve.wait_ge(ident_made, 4)
                    dve.wait_ge(consts_in, 16 * N_CONST)
                    dve.tensor_copy(pick[:], ident[0:HEADS, 0:HEADS].unsqueeze(2).to_broadcast([HEADS, HEADS, P])).then_inc(const_sb, 1)
                    dve.wait_ge(const_sb, 1)
            dve.wait_ge(w_lo_made, len(PIECES) + 1)
            dve.memset(v[:, :, :, QK:VA], 1.0)

            def body(r, slot):
                i, j = r, r - 1
                cur, mix = tile_at(i, slot), tile_at(j, 1 - slot)
                n, m = cur.n, mix.n
                step = i * ROW_STEPS
                if exists(j):
                    all_of(dve, cols_ps, j)
                    dve.tensor_copy(cols[0:m, 0:12], COLS[0:m, 0:12]).then_inc(cols_sb, 1)
                    dve.tensor_copy(cols[:, 12:16], COLS[:, 12:16]).then_inc(cols_sb, 1)
                    all_of(dve, num_ps, j - 1)
                    dve.scalar_tensor_tensor(decay[0:m, :, 0:m], wide[0:m, :, 0:m], -1.0,
                                             causal[0:m, 0:m].unsqueeze(1).to_broadcast([m, HEADS, m]), ALU.mult, ALU.add).then_inc(masked, 1)
                if exists(r + 1):
                    split_h(tile_at(r + 1, 1 - slot))
                if exists(j):
                    if exists(i):
                        output_gate(mix)
                    all_of(dve, qk_turned, j)
                    dve.tensor_copy(kT[:, :, 0:m], turned[:, HEADS:2 * HEADS, 0:m]).then_inc(kT_sb, 1)
                    all_of(dve, cols_sb, j, 2)
                    qv = q[0:m, mix.slot, :].rearrange("p (h d) -> p h d", h=HEADS)
                    dve.tensor_tensor(qv, qv, cols[0:m, 4:8].unsqueeze(2).to_broadcast([m, HEADS, QK]), ALU.mult).then_inc(q_scaled, 1)
                    all_of(dve, decayed, j)
                    kv = k[0:m, mix.slot, :].rearrange("p (h d) -> p h d", h=HEADS)
                    dve.tensor_tensor(kv, kv, decay[0:m, :, m - 1:m].to_broadcast([m, HEADS, QK]), ALU.mult).then_inc(k_scaled, 1)
                    if not exists(i):
                        output_gate(mix)
                if exists(i):
                    all_of(dve, rows_ps, i)
                    all_of(dve, cols_ps, i - 1)
                    dve.tensor_scalar(rows[:, F_ROW, 0:n], ROWS[:, P:P + n], gbias[:, 1:2], None, ALU.add).then_inc(row_step, 1)
                    dve.wait_ge(row_step, step + 1)
                    dve.scalar_tensor_tensor(rows[:, F_ABS, 0:n], rows[:, F_ROW, 0:n], -1.0, rows[:, F_ROW, 0:n], ALU.mult, ALU.max).then_inc(row_step, 1)
                    dve.tensor_scalar(rows[:, I_ROW, 0:n], ROWS[:, 0:n], gbias[:, 0:1], None, ALU.add).then_inc(row_step, 1)
                    all_of(dve, v_ps, i)
                    dve.tensor_copy(v[0:n, slot, :, 0:QK], proj[0][0:n, :].rearrange("p (h d) -> p h d", h=HEADS)).then_inc(v_sb, 1)
                if exists(j):
                    all_of(dve, scores_ps, j)
                    all_of(dve, k_scaled, j)
                    dve.tensor_tensor(decay[0:m, :, 0:m], decay[0:m, :, 0:m], wide[0:m, :, 0:m], ALU.mult).then_inc(weighted, 1)
                    all_of(dve, state_ps, j)
                    all_of(dve, C_moved, j - 1)
                    if isinstance(j, int) and j == NT:
                        dve.wait_ge(state_out, 16 * 3)
                    state = C if m == P else C_dec
                    for h in range(HEADS):
                        ins = dve.scalar_tensor_tensor(C_new[:, h, :], state[:, h, :], cols[:, 12 + h:13 + h], acc[:, h, 0:VA], ALU.mult, ALU.add)
                    ins.then_inc(C_made, 1)
                if exists(i):
                    reached(dve, row_act, i * ROW_ACTS + 2)
                    dve.scalar_tensor_tensor(rows[:, LF, 0:n], rows[:, F_ROW, 0:n], 0.0, rows[:, LOG1P, 0:n], ALU.min, ALU.subtract).then_inc(row_step, 1)
                    dve.wait_ge(row_step, step + 4)
                    dve.tensor_tensor_scan(rows[:, B, 0:n], ones_row[:, 0:n], rows[:, LF, 0:n], 0.0, ALU.mult, ALU.add).then_inc(row_step, 1)
                    dve.wait_ge(row_step, step + 5)
                    dve.tensor_tensor(rows[:, G, 0:n], rows[:, I_ROW, 0:n], rows[:, B, 0:n], ALU.subtract).then_inc(row_step, 1)
                    dve.wait_ge(row_step, step + 6)
                    m_in = m_dec[:] if n < P else m_rows[:, 1 - slot, P - 1:P]
                    dve.tensor_tensor_scan(rows[:, U, 0:n], zero_row[:, 0:n], rows[:, G, 0:n], m_in, ALU.add, ALU.max).then_inc(row_step, 1)
                    dve.wait_ge(row_step, step + 7)
                    dve.tensor_tensor(m_rows[:, slot, 0:n], rows[:, B, 0:n], rows[:, U, 0:n], ALU.add).then_inc(row_step, 1)
                if wanted(r + 2):
                    all_of(dve, h_turned, r)
                    norm(tile_at(r + 2, slot))
                if exists(j):
                    base = j * FIN_STEPS
                    all_of(dve, num_ps, j)
                    f = lambda a: fin[0:m, a, :]
                    all_of(dve, squared, j)
                    dve.tensor_tensor(f(0), acc[0:m, :, QK], cols[0:m, 8:12], ALU.max).then_inc(fin_step, 1)
                    dve.wait_ge(fin_step, base + 4)
                    dve.scalar_tensor_tensor(f(1), acc[0:m, :, QK], -1.0, f(0), ALU.mult, ALU.max).then_inc(fin_step, 1)
                    dve.wait_ge(fin_step, base + 5)
                    dve.reciprocal(f(2), f(1)).then_inc(fin_step, 1)
                    dve.wait_ge(fin_step, base + 6)
                    dve.tensor_tensor(f(4), f(3), f(2), ALU.mult).then_inc(fin_step, 1)
                    dve.wait_ge(fin_step, base + 7)
                    dve.scalar_tensor_tensor(f(5), f(4), 1.0 / QK, f(2), ALU.mult, ALU.mult).then_inc(fin_step, 1)
                    dve.wait_ge(fin_step, base + 8)
                    dve.tensor_scalar(f(6), f(5), EPS, None, ALU.add).then_inc(fin_step, 1)
                    all_of(dve, heads_rooted, j)
                    dve.tensor_tensor(f(7), f(3), f(2), ALU.mult).then_inc(fin_step, 1)
                    dve.wait_ge(fin_step, base + 10)
                    all_of(dve, out_done, j - 1, 16)
                    for h in range(HEADS):
                        at = slice(h * QK, (h + 1) * QK)
                        ins = dve.scalar_tensor_tensor(heads_out[0:m, at], acc[0:m, h, 0:QK], fin[0:m, 7, h:h + 1], o[0:m, mix.slot, at],
                                                       ALU.mult, ALU.mult)
                    ins.then_inc(fin_step, 1)

            rounds(dve, body, NT + 1)


def attention_phase(nc, x_prompt, x_sample, w_in, sinks, w_out, cache_k, cache_v, mixed, x_mid,
                    out_k, out_v, x, gmix):
    QKV = AW + 2 * KVW
    PREV, CUR = 0, 1
    SCALE = HD ** -0.5
    with ExitStack() as ctx:
        def sb(name, shape, dt=F32):
            return ctx.enter_context(nc.sbuf_tensor("a_" + name, shape, dt))

        def ps(name, shape):
            return ctx.enter_context(nc.psum_tensor("a_" + name, shape, F32))

        def sem(name):
            return ctx.enter_context(nc.semaphore("a_" + name))

        def sems(names):
            return [sem(n) for n in names.split()]

        wa_hi, wa_lo = sb("wa_hi", [P, KC, QKV], F32R), sb("wa_lo", [P, KC, QKV], F32R)
        wo_hi, wo_lo = sb("wo_hi", [P, KC, D], F32R), sb("wo_lo", [P, KC, D], F32R)
        w_raw = sb("w_raw", [P, 2 * D])
        x_sum = sb("x_sum", [P, 2, D])
        hT_hi, hT_lo = sb("hT_hi", [P, 2, KC, P], F32R), sb("hT_lo", [P, 2, KC, P], F32R)
        mixT_hi, mixT_lo = sb("mixT_hi", [P, KC, P], F32R), sb("mixT_lo", [P, KC, P], F32R)
        heads_in, att = sb("heads_in", [P, 2, MW]), sb("att", [P, 2, AW])
        q, kv = sb("q", [P, AW]), sb("kv", [P, 2, 2 * KVW])
        v_prev = sb("v_prev", [P, KVW])
        ck, cv = sb("ck", [P, KVW]), sb("cv", [P, KVW])
        qT = sb("qT", [P, GRP, P])
        kT, ckT = sb("kT", [P, 2, P]), sb("ckT", [P, P])
        s = sb("s", [P, KVH, GRP, 2 * P])
        sT = sb("sT", [P, KVH, 2, GRP, P])
        bias = sb("bias", [P, AH, 2 * P])
        raw = [b[:, n * D:(n + 1) * D] for b in (w_raw, s.rearrange("p g h k -> p (g h k)"), sT.rearrange("p g a h t -> p (g a h t)")) for n in (0, 1)]
        WAVE = 3
        dist = sb("dist", [P, 2 * P])
        sink = sb("sink", [P, AH])
        mx = sb("mx", [P, KVH, 7, GRP])
        MAX, TOP, NEG, SINK, SUM, SINK_EXP, DEN = range(7)
        ident = sb("ident", [P, P])
        stats, ms, minus_half = sb("stats", [P, 2, 6]), sb("ms", [P, 8]), sb("minus_half", [P, 1])

        proj = [ps("proj0", [P, NB]), ps("proj1", [P, NB])]
        turned = ps("turned", [P, KC, P])
        scores = ps("scores", [P, GRP, 2 * P])
        out_ps = [ps("out0", [P, NB]), ps("out1", [P, NB])]

        def x_of(t):
            return x[0:t.n, 1 - t.slot, :]

        DONE = 2

        made, consts_in, const_sb, cache_turned, cache_out, last_out = sems("made consts_in const_sb cache_turned cache_out last_out")
        w_in_sem, (w_hi_made, w_lo_made) = sems("w_raw0 w_raw1"), sems("w_hi_made w_lo_made")
        x_in, heads_loaded, x_sum_in = sems("x_in0 x_in1"), sems("heads_in0 heads_in1"), sems("x_sum_in0 x_sum_in1")
        normed, rooted, h_turned, h_hi, h_lo = sems("normed rooted h_turned h_hi h_lo")
        q_ps, kv_ps, o0_ps, o1_ps, q_sb, kv_sb, v_kept = sems("q_ps kv_ps o0_ps o1_ps q_sb kv_sb v_kept")
        qk_turned, qT_sb, kT_sb = sems("qk_turned qT_sb kT_sb")
        scores_ps, soft, exps, s_turned, sT_sb, out_done, averaged = sems("scores_ps soft exps s_turned sT_sb out_done averaged")
        mix_turned, mix_hi, mix_lo, added, x_out = sems("mix_turned mix_hi mix_lo added x_out")
        SOFT, AVG, N_CONST = 5, 3, 3
        W_PIECES = 2 * KC

        def keys(t, part):
            return 0 if part == PREV and isinstance(t.i, int) and t.i == 0 else P if part == PREV else t.n

        def parts(t):
            return [p for p in (PREV, CUR) if keys(t, p)]

        def key_span(t):
            return (0 if keys(t, PREV) else P), P + t.n

        block = ctx.enter_context(nc.Block())

        @block.sync
        def _(sp):
            def load_weights(pieces):
                for n in pieces:
                    c, slot = n % KC, n % len(raw)
                    reached(sp, w_lo_made, n - len(raw) + 1)
                    width = QKV if n < KC else D
                    src = w_in[c * P:(c + 1) * P, Q_COL:Q_COL + QKV] if n < KC else w_out[c * P:(c + 1) * P, :]
                    sp.dma_start(raw[slot][:, 0:width], src).then_inc(w_in_sem[slot // WAVE], 16)

            load_weights(range(WAVE))
            sp.dma_start(sink[:], sinks.partition_broadcast(P)).then_inc(consts_in, 16)
            sp.dma_start(ck[:], cache_k).then_inc(consts_in, 16)
            sp.dma_start(cv[:], cache_v).then_inc(consts_in, 16)
            load_weights(range(WAVE, W_PIECES))
            sp.dma_start(out_k[1][0:P - DEC, :], cache_k[DEC:P, :]).then_inc(cache_out, 16)
            sp.dma_start(out_v[1][0:P - DEC, :], cache_v[DEC:P, :]).then_inc(cache_out, 16)

            def body(r, slot):
                if exists(r + 2):
                    nxt = tile_at(r + 2, slot)
                    src = x_sample if nxt.n < P else x_prompt[token_rows(sp, nxt.i, P), :]
                    all_of(sp, h_turned, r)
                    sp.dma_start(x_of(nxt), src).then_inc(x_in[slot], 16)
                if exists(r):
                    cur = tile_at(r, slot)
                    all_of(sp, mix_turned, r - 2)
                    sp.dma_start(heads_in[0:cur.n, slot, :], mixed[token_rows(sp, r, cur.n), :]).then_inc(heads_loaded[slot], 16)
                if exists(r - 2):
                    t = tile_at(r - 2, slot)
                    all_of(sp, added, t.i, 2)
                    sp.dma_start(x_mid[token_rows(sp, t.i, t.n), :], x_sum[0:t.n, slot, :]).then_inc(x_out, 16)
                    all_of(sp, x_out, t.i, 16)
                if exists(r):
                    src = x_sample if cur.n < P else x_prompt[token_rows(sp, r, P), :]
                    sp.dma_start(x_sum[0:cur.n, slot, :], src).then_inc(x_sum_in[slot], 16)
                if isinstance(r, int) and NT - 1 <= r <= NT:
                    which, rows = r - (NT - 1), tile_at(r, slot).n
                    all_of(sp, kv_sb, r)
                    sp.dma_start(out_k[which][P - rows:P, :], kv[0:rows, slot, 0:KVW]).then_inc(last_out, 16)
                    sp.dma_start(out_v[which][P - rows:P, :], kv[0:rows, slot, KVW:]).then_inc(last_out, 16)

            rounds(sp, body, NT + 2)
            sp.wait_ge(cache_out, 32)
            sp.wait_ge(last_out, 64)

        @block.gpsimd
        def _(pool):
            make_identity(pool, ident[:], made)
            pool.memset(minus_half[:], -0.5).then_inc(made, 1)
            pool.iota(dist[:], pattern=[[-1, 2 * P]], base=P, channel_multiplier=1,
                      allow_small_or_imprecise_dtypes=True).then_inc(made, 1)
            pool.wait_ge(made, 4)

            def root(t):
                norm_root(pool, normed, rooted, t.i - DONE, ms[0:t.n], minus_half[0:t.n])

            def body(r, slot):
                if exists(r + 2):
                    root(tile_at(r + 2, slot))

            rounds(pool, body, NT - 2)

        @block.scalar
        def _(act):
            def split_h(t):
                all_of(act, h_turned, t.i)
                all_of(act, kv_ps, t.i - 2)
                act.activation(hT_hi[:, t.slot, :, 0:t.n], turned[:, :, 0:t.n], ACT.Copy).then_inc(h_hi, 1)

            def weights_hi(pieces):
                for n in pieces:
                    c, slot = n % KC, n % len(raw)
                    last = min(n - slot % WAVE + WAVE, W_PIECES)
                    loaded = sum(1 for k in range(last) if k % len(raw) // WAVE == slot // WAVE)
                    act.wait_ge(w_in_sem[slot // WAVE], 16 * loaded)
                    dst, width = (wa_hi, QKV) if n < KC else (wo_hi, D)
                    act.activation(dst[:, c, :], raw[slot][:, 0:width], ACT.Copy).then_inc(w_hi_made, 1)

            split_h(tile_at(0, 0))
            weights_hi(range(KC))

            def exponentials(t, g):
                lo, hi = key_span(t)
                reached(act, soft, (t.i * 2 + g) * SOFT + 4)
                for h in range(GRP):
                    part = s[0:t.n, g, h, lo:hi]
                    ins = act.activation(part, part, ACT.Exp, bias=mx[0:t.n, g, NEG, h:h + 1], accum_out=mx[0:t.n, g, SUM, h:h + 1])
                ins.then_inc(exps, 1)
                reached(act, soft, (t.i * 2 + g) * SOFT + 5)
                act.activation(mx[0:t.n, g, SINK_EXP, :], mx[0:t.n, g, SINK, :], ACT.Exp).then_inc(exps, 1)

            def copy_turned(t, g):
                reached(act, s_turned, t.i * 2 + g + 1)
                for p in parts(t):
                    n = keys(t, p)
                    ins = act.activation(sT[0:n, g, p, :, 0:t.n], turned[0:n, p * GRP:(p + 1) * GRP, 0:t.n], ACT.Copy)
                ins.then_inc(sT_sb, 1)

            def body(r, slot):
                cur, mid, old = tile_at(r, slot), tile_at(r - 1, 1 - slot), tile_at(r - 2, slot)
                if exists(mid.i):
                    exponentials(mid, 0)
                if exists(cur.i):
                    all_of(act, q_ps, r)
                    all_of(act, qk_turned, r - 1)
                    act.activation(q[0:cur.n, :].rearrange("p (h g d) -> p g h d", g=KVH, h=GRP),
                                   proj[0][0:cur.n, :].rearrange("p (g h d) -> p g h d", g=KVH, h=GRP), ACT.Copy).then_inc(q_sb, 1)
                if exists(old.i):
                    all_of(act, mix_turned, old.i)
                    all_of(act, o1_ps, old.i - 1)
                    act.activation(mixT_hi[:, :, 0:old.n], turned[:, :, 0:old.n], ACT.Copy).then_inc(mix_hi, 1)
                if exists(r + 1):
                    split_h(tile_at(r + 1, 1 - slot))
                if exists(mid.i):
                    copy_turned(mid, 0)
                    exponentials(mid, 1)
                if exists(cur.i):
                    all_of(act, qk_turned, r)
                    act.activation(qT[:, :, 0:cur.n], turned[:, 0:GRP, 0:cur.n], ACT.Copy).then_inc(qT_sb, 1)
                if exists(mid.i):
                    copy_turned(mid, 1)
                if isinstance(r, int) and r == 0:
                    weights_hi(range(KC, W_PIECES))

            rounds(act, body, NT + 2)

        @block.tensor
        def _(pe):
            pe.wait_ge(made, 2)

            def turn(t, src, done):
                for c in range(KC):
                    ins = pe.transpose(turned[:, c, 0:t.n], src(c), ident[0:t.n, 0:t.n])
                ins.then_inc(done, 1)

            def turn_h(t):
                all_of(pe, normed, t.i - DONE, NORM)
                turn(t, lambda c: x_of(t)[:, c * P:(c + 1) * P], h_turned)

            def project(out, t, c0, width, chunks):
                for c in chunks:
                    if isinstance(t.i, int) and t.i == 0 and c0 == 0:
                        pe.wait_ge(w_lo_made, c + 1)
                    ins = split_product(pe, out, (lambda c: hT_hi[:, t.slot, c, :], lambda c: hT_lo[:, t.slot, c, :]),
                                        (lambda c: wa_hi[:, c, c0:c0 + width], lambda c: wa_lo[:, c, c0:c0 + width]),
                                        [c], c == 0, c == KC - 1)
                return ins

            def project_out(half, chunks):
                cols = slice(half * NB, (half + 1) * NB)
                return split_product(pe, proj[half][:], (lambda c: mixT_hi[:, c, :], lambda c: mixT_lo[:, c, :]),
                                     (lambda c: wo_hi[:, c, cols], lambda c: wo_lo[:, c, cols]),
                                     chunks, chunks[0] == 0, chunks[-1] == KC - 1)

            def score(t, g):
                head = slice(g * HD, (g + 1) * HD)
                reached(pe, soft, (t.i * 2 + g - 1) * SOFT + 1)
                for h in range(GRP):
                    for p in parts(t):
                        n = keys(t, p)
                        kk = kT[head, t.slot, 0:n] if p == CUR else ckT[head, :] if t.n < P else kT[head, 1 - t.slot, :]
                        ins = pe.matmul(scores[0:t.n, h, p * P:p * P + n], qT[head, h, 0:t.n], kk, start=True, stop=True)
                ins.then_inc(scores_ps, 1)

            def turn_s(t, g):
                reached(pe, exps, (t.i * 2 + g) * 2 + 1)
                for p in parts(t):
                    n = keys(t, p)
                    for h in range(GRP):
                        ins = pe.transpose(turned[0:n, p * GRP + h, 0:t.n], s[0:t.n, g, h, p * P:p * P + n], ident[0:t.n, 0:t.n])
                ins.then_inc(s_turned, 1)

            def average(t, g):
                reached(pe, sT_sb, t.i * 2 + g + 1)
                reached(pe, averaged, ((t.i - 1) * 2 + g + 1) * AVG)
                for h in range(GRP):
                    for p in parts(t):
                        n = keys(t, p)
                        vals = kv[0:n, t.slot, KVW + g * HD:KVW + (g + 1) * HD] if p == CUR else (cv if t.n < P else v_prev)[:, g * HD:(g + 1) * HD]
                        ins = pe.matmul(out_ps[g][0:t.n, h * HD:(h + 1) * HD], sT[0:n, g, p, h, 0:t.n], vals,
                                        start=p == parts(t)[0], stop=p == CUR)
                ins.then_inc(out_done, 1)

            first, second = range(KC // 2), range(KC // 2, KC)
            turn_h(tile_at(0, 0))
            pe.wait_ge(consts_in, 16 * N_CONST)
            pe.transpose(scores[:, 0, 0:P], ck[:], ident[:]).then_inc(cache_turned, 1)
            pe.wait_ge(const_sb, 2)

            def body(r, slot):
                cur, mid, old = tile_at(r, slot), tile_at(r - 1, 1 - slot), tile_at(r - 2, slot)
                if exists(mid.i):
                    all_of(pe, qT_sb, mid.i)
                    all_of(pe, kT_sb, mid.i)
                    score(mid, 0)
                if exists(cur.i):
                    all_of(pe, h_lo, r)
                    reached(pe, added, (r - 3) * 2 + 1)
                    project(proj[0][:], cur, 0, AW, first)
                if exists(old.i):
                    average(old, 1)
                if exists(cur.i):
                    project(proj[0][:], cur, 0, AW, second).then_inc(q_ps, 1)
                if exists(old.i):
                    reached(pe, averaged, (old.i + 1) * 2 * AVG)
                    slot_loaded(pe, heads_loaded, old)
                    turn(old, lambda c: (heads_in if c < HEADS else att)[0:old.n, old.slot, c % HEADS * P:(c % HEADS + 1) * P], mix_turned)
                if exists(cur.i):
                    all_of(pe, added, r - 3, 2)
                    project(proj[1][:, 0:2 * KVW], cur, AW, 2 * KVW, range(KC)).then_inc(kv_ps, 1)
                if exists(old.i):
                    all_of(pe, mix_lo, old.i)
                if exists(r + 1):
                    turn_h(tile_at(r + 1, 1 - slot))
                if exists(mid.i):
                    score(mid, 1)
                if isinstance(r, int) and r == 2:
                    pe.wait_ge(w_lo_made, W_PIECES)
                if exists(old.i):
                    all_of(pe, q_sb, r if exists(r) else NT)
                    project_out(0, first)
                if exists(mid.i):
                    if exists(r + 1):
                        all_of(pe, h_lo, r + 1)
                    turn_s(mid, 0)
                if exists(old.i):
                    project_out(0, second).then_inc(o0_ps, 1)
                if exists(mid.i):
                    if exists(cur.i):
                        reached(pe, v_kept, r - 1)
                    average(mid, 0)
                if exists(old.i):
                    all_of(pe, kv_sb, r if exists(r) else NT)
                    project_out(1, first)
                if exists(cur.i):
                    all_of(pe, q_sb, r)
                    all_of(pe, kv_sb, r)
                    if exists(mid.i):
                        reached(pe, sT_sb, mid.i * 2 + 1)
                    else:
                        all_of(pe, h_lo, r + 1)
                    for h in range(GRP):
                        pe.transpose(turned[:, h, 0:cur.n], q[0:cur.n, h * P:(h + 1) * P], ident[0:cur.n, 0:cur.n])
                    pe.transpose(turned[:, GRP, 0:cur.n], kv[0:cur.n, slot, 0:KVW], ident[0:cur.n, 0:cur.n]).then_inc(qk_turned, 1)
                if exists(old.i):
                    project_out(1, second).then_inc(o1_ps, 1)
                if exists(mid.i):
                    if exists(cur.i):
                        all_of(pe, qT_sb, r)
                        all_of(pe, kT_sb, r)
                    else:
                        reached(pe, sT_sb, mid.i * 2 + 1)
                    turn_s(mid, 1)

            rounds(pe, body, NT + 2)

        @block.vector
        def _(dve):
            def norm(t):
                slot_loaded(dve, x_in, Tile(t.i - DONE, t.slot, t.n))
                xt = x_of(t)
                norm_rows(dve, normed, rooted, t.i - DONE, xt, gmix[0:t.n, :], xt, stats[0:t.n], ms[0:t.n])

            def split(i, hi_made, lo, hi, n, lo_made):
                all_of(dve, hi_made, i)
                dve.tensor_tensor(lo, turned[:, :, 0:n], hi, ALU.subtract).then_inc(lo_made, 1)

            def split_h(t):
                split(t.i, h_hi, hT_lo[:, t.slot, :, 0:t.n], hT_hi[:, t.slot, :, 0:t.n], t.n, h_lo)

            def soften(t, g):
                n, (lo, hi) = t.n, key_span(t)
                base = (t.i * 2 + g) * SOFT
                f = lambda a: mx[0:n, g, a, :]
                heads = slice(g * GRP, (g + 1) * GRP)
                reached(dve, scores_ps, t.i * 2 + g + 1)
                reached(dve, s_turned, (t.i - 1) * 2 + g + 1)
                dve.scalar_tensor_tensor(s[0:n, g, :, lo:hi], scores[0:n, :, lo:hi], SCALE, bias[0:n, heads, lo:hi], ALU.mult, ALU.add).then_inc(soft, 1)
                dve.wait_ge(soft, base + 1)
                dve.reduce_max(f(MAX), s[0:n, g, :, lo:hi], AX.X).then_inc(soft, 1)
                dve.wait_ge(soft, base + 2)
                dve.tensor_tensor(f(TOP), f(MAX), sink[0:n, heads], ALU.max).then_inc(soft, 1)
                dve.wait_ge(soft, base + 3)
                reached(dve, exps, ((t.i - 1) * 2 + g + 1) * 2)
                dve.tensor_scalar(f(NEG), f(TOP), -1.0, None, ALU.mult).then_inc(soft, 1)
                dve.tensor_tensor(f(SINK), sink[0:n, heads], f(TOP), ALU.subtract).then_inc(soft, 1)

            def divide(t, g):
                n, base = t.n, (t.i * 2 + g) * AVG
                f = lambda a: mx[0:n, g, a, :]
                reached(dve, exps, (t.i * 2 + g + 1) * 2)
                dve.tensor_tensor(f(DEN), f(SUM), f(SINK_EXP), ALU.add).then_inc(averaged, 1)
                dve.wait_ge(averaged, base + 1)
                dve.reciprocal(f(DEN), f(DEN)).then_inc(averaged, 1)
                dve.wait_ge(averaged, base + 2)
                reached(dve, out_done, t.i * 2 + g + 1)
                all_of(dve, mix_turned, t.i - 2)
                dst = att[0:n, t.slot, g * GRP * HD:(g + 1) * GRP * HD].rearrange("p (h d) -> p h d", h=GRP)
                dve.tensor_tensor(dst, out_ps[g][0:n, 0:GRP * HD].rearrange("p (h d) -> p h d", h=GRP),
                                  f(DEN).unsqueeze(2).to_broadcast([n, GRP, HD]), ALU.mult).then_inc(averaged, 1)

            def add(t, half):
                cols = slice(half * NB, (half + 1) * NB)
                all_of(dve, (o0_ps, o1_ps)[half], t.i)
                dve.tensor_tensor(x_sum[0:t.n, t.slot, cols], x_sum[0:t.n, t.slot, cols], proj[half][0:t.n, :], ALU.add).then_inc(added, 1)

            def weights_lo(pieces):
                for n in pieces:
                    c, slot = n % KC, n % len(raw)
                    hi, lo, width = (wa_hi, wa_lo, QKV) if n < KC else (wo_hi, wo_lo, D)
                    dve.wait_ge(w_hi_made, n + 1)
                    dve.tensor_tensor(lo[:, c, :], raw[slot][:, 0:width], hi[:, c, :], ALU.subtract).then_inc(w_lo_made, 1)

            split_h(tile_at(0, 0))
            weights_lo(range(WAVE))
            dve.wait_ge(made, 4)
            dve.wait_ge(consts_in, 16 * N_CONST)
            dve.scalar_tensor_tensor(dist[:], dist[:], -1.0, dist[:], ALU.mult, ALU.max).then_inc(const_sb, 1)
            dve.wait_ge(cache_turned, 1)
            dve.tensor_copy(ckT[:], scores[:, 0, 0:P]).then_inc(const_sb, 1)
            weights_lo(range(WAVE, KC))
            dve.wait_ge(const_sb, 2)
            for h in range(AH):
                ins = dve.tensor_scalar(bias[:, h, :], dist[:], -(2.0 ** (-(h + 1) * 8.0 / AH)), None, ALU.mult)
            ins.then_inc(const_sb, 1)
            dve.wait_ge(const_sb, 3)
            dve.memset(bias[0:P // 2, :, P + P // 2:], MASKED)
            dve.memset(bias[P // 2:, :, 0:P // 2], MASKED).then_inc(const_sb, 1)
            dve.wait_ge(const_sb, 4)

            def body(r, slot):
                cur, mid, old = tile_at(r, slot), tile_at(r - 1, 1 - slot), tile_at(r - 2, slot)
                if exists(mid.i):
                    soften(mid, 0)
                if exists(old.i):
                    divide(old, 1)
                    split(old.i, mix_hi, mixT_lo[:, :, 0:old.n], mixT_hi[:, :, 0:old.n], old.n, mix_lo)
                if exists(cur.i):
                    all_of(dve, kv_ps, r)
                    if exists(old.i):
                        all_of(dve, out_done, old.i, 2)
                        dve.tensor_copy(v_prev[:], kv[:, slot, KVW:]).then_inc(v_kept, 1)
                        all_of(dve, v_kept, old.i)
                    dve.tensor_copy(kv[0:cur.n, slot, :], proj[1][0:cur.n, 0:2 * KVW]).then_inc(kv_sb, 1)
                if exists(r + 1):
                    split_h(tile_at(r + 1, 1 - slot))
                if exists(mid.i):
                    soften(mid, 1)
                if exists(old.i):
                    slot_loaded(dve, x_sum_in, old)
                    add(old, 0)
                if exists(mid.i):
                    divide(mid, 0)
                if exists(cur.i):
                    all_of(dve, qk_turned, r)
                    dve.tensor_copy(kT[:, slot, 0:cur.n], turned[:, GRP, 0:cur.n]).then_inc(kT_sb, 1)
                if exists(old.i):
                    add(old, 1)
                if isinstance(r, int) and r == 0:
                    weights_lo(range(KC, W_PIECES))
                    dve.wait_ge(w_lo_made, W_PIECES)
                if exists(r + 2):
                    norm(tile_at(r + 2, slot))

            rounds(dve, body, NT + 2)


def mlp_phase(nc, x_mid, g_mlp, w_up, w_down, x_mlp):
    BLOCKS = FF // MLP_BLOCK
    FC = MLP_BLOCK // P
    HALF = NT // 2
    TOKENS = HALF * P + DEC
    with ExitStack() as ctx:
        def sb(name, shape, dt=F32):
            return ctx.enter_context(nc.sbuf_tensor("f_" + name, shape, dt))

        def ps(name, shape):
            return ctx.enter_context(nc.psum_tensor("f_" + name, shape, F32))

        def sems(names):
            return [ctx.enter_context(nc.semaphore("f_" + n)) for n in names.split()]

        acc = sb("acc", [P, HALF + 1, D])
        h_buf = sb("h", [P, D])
        hT_hi, hT_lo = sb("hT_hi", [P, KC, TOKENS], F32R), sb("hT_lo", [P, KC, TOKENS], F32R)
        gmlp = sb("gmlp", [P, D])
        up_hi, up_lo = sb("up_hi", [P, 2, KC, MLP_BLOCK], F32R), sb("up_lo", [P, 2, KC, MLP_BLOCK], F32R)
        down_hi, down_lo = sb("down_hi", [P, 2, FC, D], F32R), sb("down_lo", [P, 2, FC, D], F32R)
        raw = sb("raw", [P, 2, D])
        u = sb("u", [P, FC, NB])
        uT_hi, uT_lo = sb("uT_hi", [P, FC, (HALF + 1) * P], F32R), sb("uT_lo", [P, FC, (HALF + 1) * P], F32R)
        h = [h_buf[:], u[:].rearrange("p f t -> p (f t)"), acc[:, HALF, :]]
        H_SLOT = [0, 1, 2, 0, 1, 2, 0, 2, 0]
        H_BEFORE = [None, None, None, 0, 1, 2, 3, 5, 6]
        ident = sb("ident", [P, P])
        ms, constants = sb("ms", [P, HALF + 1, 3]), sb("constants", [P, 2])

        up_ps = [ps("up0", [P, FC, NB]), ps("up1", [P, FC, NB])]
        down_ps = [ps("down0", [P, D]), ps("down1", [P, D])]

        raw_in, (w_hi_made, w_lo_made) = sems("raw_in0 raw_in1"), sems("w_hi_made w_lo_made")
        made, gain_in, acc_out, cleared = sems("made gain_in acc_out cleared")
        acc_in = sems(" ".join(f"acc_in{n}" for n in range(HALF + 1)))
        h_in = sems("h_in0 h_in1 h_in2")
        summed, normed, rooted, h_turned, h_hi, h_lo = sems("summed normed rooted h_turned h_hi h_lo")
        up_done, rectified, squared, u_hi, u_lo, down_done, added = sems("up_done rectified squared u_hi u_lo down_done added")
        PIECES = 8

        def quarter(slot, n, up, down):
            if n < 2:
                return up[:, slot, n * KC // 2:(n + 1) * KC // 2, :].rearrange("p c f -> p (c f)")
            return down[:, slot, n - 2, :]

        def tiles(half):
            return [(n, tile_at(half * HALF + n, n % 2)) for n in range(HALF + half)]

        def groups(half):
            cols = TOKENS // 3 if half else NB
            return [slice(c, c + cols) for c in range(0, HALF * P + half * DEC, cols)]

        def last_place(cols):
            return (cols.stop - 1) // P

        def up_count(half, b, g):
            n = len(groups(half))
            return b * n + (g + 1 - half * BLOCKS * (n - 2))

        LEAD = (3, 2)

        def turned_at(half, n):
            banks = up_ps if half and n < 4 else down_ps
            t = banks[n % 2]
            return t.rearrange("p c (a t) -> p (c a) t", t=P) if banks is up_ps else t.rearrange("p (c t) -> p c t", t=P)

        def turned_free(eng, half, n):
            if half and n < 2:
                eng.wait_ge(rectified, up_count(0, BLOCKS - 1, 1))
            elif half and 4 <= n < 6:
                eng.wait_ge(added, down_count(0, BLOCKS - 1, HALF - 1))
            elif n >= 2:
                all_of(eng, h_lo, half * HALF + n - 2)

        TURNED_AFTER = [{(0, 0): [4, 5], (0, 1): [6, 7]}, {(0, 0): [4, 5], (1, 0): [6], (1, 1): [7, 8]}]
        TURNED_AHEAD = {2: 0, 3: 1, 5: 2, 6: 3}

        def turned_in(half, g):
            return [n for (at, _), places in TURNED_AFTER[half].items() if at == g for n in places]

        def down_count(half, b, n):
            per = HALF + half
            return b * per + (n + 1 - half * BLOCKS)

        def blocks(eng, half, body):
            first, last = half * BLOCKS, (half + 1) * BLOCKS - 1
            body(first, 0, first + 1)
            with eng.Fori(0, (BLOCKS - 2) // 2) as turn:
                body(turn * 2 + (first + 1), 1, turn * 2 + (first + 2))
                body(turn * 2 + (first + 2), 0, turn * 2 + (first + 3))
            body(last, 1, None if half else last + 1)

        block = ctx.enter_context(nc.Block())

        @block.sync
        def _(sp):
            def load_weights(first_col, b, between=None):
                up = w_up[:, first_col].rearrange("(n c p) f -> n p c f", n=2, p=P)
                down = w_down[first_col, :].rearrange("(n p) d -> n p d", p=P)
                for n in range(4):
                    dst = raw[:, n % 2, :]
                    reached(sp, w_lo_made, b * PIECES + 2 * (n - 1))
                    sp.dma_start(dst.rearrange("p (c f) -> p c f", f=MLP_BLOCK) if n < 2 else dst,
                                 up[n] if n < 2 else down[n - 2]).then_inc(raw_in[n % 2], 16)
                    if between:
                        between(n)

            def load_tile(n, t):
                sp.dma_start(acc[0:t.n, n, :], x_mid[token_rows(sp, t.i, t.n), :]).then_inc(acc_in[n], 16)

            load_tile(*tiles(0)[0])
            sp.dma_start(gmlp[:], g_mlp.partition_broadcast(P)).then_inc(gain_in, 16)
            for n, t in tiles(0)[1:3]:
                load_tile(n, t)
            load_weights(slice(0, MLP_BLOCK), 0, lambda n: load_tile(*tiles(0)[n + 3]))
            for n, t in tiles(0)[7:]:
                load_tile(n, t)
            for half in (0, 1):
                def body(b, slot, nxt):
                    if nxt is None:
                        return
                    if isinstance(nxt, int):
                        c = nxt % BLOCKS * MLP_BLOCK
                        load_weights(slice(c, c + MLP_BLOCK), nxt)
                    else:
                        load_weights(bass.ds((nxt - half * BLOCKS) * MLP_BLOCK, MLP_BLOCK), nxt)

                blocks(sp, half, body)
                for n, t in tiles(half):
                    reached(sp, added, down_count(half, (half + 1) * BLOCKS - 1, n))
                    sp.dma_start(x_mlp[token_rows(sp, t.i, t.n), :], acc[0:t.n, n, :]).then_inc(acc_out, 16)
                    if not half:
                        sp.wait_ge(acc_out, 16 * (n + 1))
                        load_tile(*tiles(1)[n])
                if not half:
                    all_of(sp, h_turned, HALF + HALF - 1)
                    load_tile(*tiles(1)[HALF])
            sp.wait_ge(acc_out, 16 * (NT + 1))

        @block.gpsimd
        def _(pool):
            make_identity(pool, ident[:], made)
            pool.memset(constants[:, 0:1], EPS).then_inc(made, 1)
            pool.memset(constants[:, 1:2], -0.5).then_inc(made, 1)
            pool.wait_ge(made, 4)

            def load_h(n):
                t = tiles(1)[n][1]
                slot = H_SLOT[n]
                pool.dma_start(h[slot][0:t.n, :], x_mid[token_rows(pool, t.i, t.n), :]).then_inc(h_in[slot], 16)

            for half in (0, 1):
                if half:
                    all_of(pool, h_turned, HALF - 1)
                    all_of(pool, normed, HALF - 1)
                    load_h(0)
                    load_h(2)
                    pool.wait_ge(u_lo, up_count(0, BLOCKS - 1, 1))
                    load_h(1)
                for n, t in tiles(half):
                    sums_root(pool, summed, rooted, t.i, ms[0:t.n, n], constants[0:t.n])
                    if half:
                        for later in range(HALF + 1):
                            if n and H_BEFORE[later] == n - 1:
                                all_of(pool, h_turned, HALF + n - 1)
                                load_h(later)

        @block.scalar
        def _(act):
            def weights_hi(b, slot, quarters=range(4)):
                for n in quarters:
                    reached(act, raw_in[n % 2], b * 32 + 16 * (n // 2 + 1))
                    act.activation(quarter(slot, n, up_hi, down_hi), raw[:, n % 2, :], ACT.Copy).then_inc(w_hi_made, 1)

            def sum_h(half, n):
                if n >= len(tiles(half)):
                    return
                t = tiles(half)[n][1]
                slot = H_SLOT[n]
                if half:
                    turned_free(act, half, n)
                    act.wait_ge(h_in[slot], 16 * (H_SLOT[:n].count(slot) + 1))
                    src, squares = h[slot][0:t.n, :].rearrange("p (c t) -> p c t", t=P), turned_at(half, n)[0:t.n]
                else:
                    if H_BEFORE[n] is not None:
                        all_of(act, h_turned, H_BEFORE[n])
                    act.wait_ge(acc_in[n], 16)
                    src, squares = acc[0:t.n, n, :], h[slot][0:t.n, :]
                act.activation(squares, src, ACT.Square, scale=D ** -0.5, accum_out=ms[0:t.n, n, 0:1]).then_inc(summed, 1)

            def split_h(half, n):
                t = tiles(half)[n][1]
                all_of(act, h_turned, t.i)
                if half:
                    act.wait_ge(up_done, up_count(0, BLOCKS - 1, 1))
                act.activation(hT_hi[:, :, n * P:n * P + t.n], turned_at(half, n)[:, :, 0:t.n], ACT.Copy).then_inc(h_hi, 1)
                sum_h(half, n + LEAD[half])

            for n in range(LEAD[0]):
                sum_h(0, n)
            weights_hi(0, 0, range(0, 1))
            split_h(0, 0)
            weights_hi(0, 0, range(1, 2))
            split_h(0, 1)
            weights_hi(0, 0, range(2, 3))
            split_h(0, 2)
            weights_hi(0, 0, range(3, 4))
            split_h(0, 3)
            for half in (0, 1):
                def body(b, slot, nxt):
                    for g, cols in enumerate(groups(half)):
                        if isinstance(b, int) and b == half * BLOCKS:
                            for n in turned_in(half, g):
                                split_h(half, n)
                        width = cols.stop - cols.start
                        count = up_count(half, b, g)
                        reached(act, up_done, count)
                        reached(act, u_lo, count - 1)
                        act.activation(u[:, :, 0:width], up_ps[g % 2][:, :, 0:width], ACT.Relu).then_inc(rectified, 1)
                        reached(act, squared, count)
                        reached(act, down_done, down_count(half, b - 1, last_place(cols)))
                        act.activation(uT_hi[:, :, cols], u[:, :, 0:width], ACT.Copy).then_inc(u_hi, 1)
                    if isinstance(nxt, int) and nxt == BLOCKS:
                        weights_hi(nxt, 1 - slot, range(0, 2))
                        sum_h(1, 0)
                        sum_h(1, 1)
                        weights_hi(nxt, 1 - slot, range(2, 3))
                        split_h(1, 0)
                        weights_hi(nxt, 1 - slot, range(3, 4))
                        for n in range(1, 4):
                            split_h(1, n)
                    elif nxt is not None:
                        weights_hi(nxt, 1 - slot)

                blocks(act, half, body)

        @block.tensor
        def _(pe):
            pe.wait_ge(made, 2)
            pe.wait_ge(cleared, 1)

            def turn_h(half, n):
                t = tiles(half)[n][1]
                turned_free(pe, half, n)
                all_of(pe, normed, t.i)
                for c in range(KC):
                    ins = pe.transpose(turned_at(half, n)[:, c, 0:t.n], h[H_SLOT[n]][0:t.n, c * P:(c + 1) * P], ident[0:t.n, 0:t.n])
                ins.then_inc(h_turned, 1)

            for n in range(4):
                turn_h(0, n)
            for half in (0, 1):
                def body(b, slot, nxt):
                    first = isinstance(b, int) and b == half * BLOCKS
                    reached(pe, w_lo_made, b * PIECES + 4)
                    for g, cols in enumerate(groups(half)):
                        if first:
                            all_of(pe, h_lo, half * HALF + last_place(cols))
                        if g == 2:
                            reached(pe, rectified, up_count(half, b, 0))
                        for f in range(FC):
                            fc = slice(f * P, (f + 1) * P)
                            ins = split_product(pe, up_ps[g % 2][:, f, 0:cols.stop - cols.start],
                                                (lambda c: up_hi[:, slot, c, fc], lambda c: up_lo[:, slot, c, fc]),
                                                (lambda c: hT_hi[:, c, cols], lambda c: hT_lo[:, c, cols]), range(KC))
                            if f == FC - 1:
                                ins.then_inc(up_done, 1)
                            if first:
                                for n in TURNED_AFTER[half].get((g, f), []):
                                    turn_h(half, n)
                    reached(pe, w_lo_made, b * PIECES + PIECES)
                    for n in range(HALF + half):
                        for g, cols in enumerate(groups(half)):
                            if cols.start <= n * P < cols.stop or n * P < cols.start < (n + 1) * P:
                                reached(pe, u_lo, up_count(half, b, g))
                        if n >= 2:
                            reached(pe, added, down_count(half, b, n - 2))
                        else:
                            last = HALF - 2 if not half or n else HALF
                            reached(pe, added, down_count(half, b - 1, last if n == 0 else HALF - 1))
                        at = slice(n * P, (n + 1) * P)
                        for c in range(D // NB):
                            cols = slice(c * NB, (c + 1) * NB)
                            ins = split_product(pe, down_ps[n % 2][:, cols], (lambda f: uT_hi[:, f, at], lambda f: uT_lo[:, f, at]),
                                                (lambda f: down_hi[:, slot, f, cols], lambda f: down_lo[:, slot, f, cols]), range(FC))
                        ins.then_inc(down_done, 1)
                        if isinstance(nxt, int) and nxt == BLOCKS and n in TURNED_AHEAD:
                            turn_h(1, TURNED_AHEAD[n])

                blocks(pe, half, body)

        @block.vector
        def _(dve):
            def weights_lo(b, slot, piece):
                n, cols = piece // 2, slice(piece % 2 * NB, (piece % 2 + 1) * NB)
                if piece % 2 == 0:
                    reached(dve, w_hi_made, b * 4 + n + 1)
                dve.tensor_tensor(quarter(slot, n, up_lo, down_lo)[:, cols], raw[:, n % 2, cols],
                                  quarter(slot, n, up_hi, down_hi)[:, cols], ALU.subtract).then_inc(w_lo_made, 1)

            dve.memset(uT_hi[:].bitcast(F32), 0.0)
            dve.memset(uT_lo[:].bitcast(F32), 0.0).then_inc(cleared, 1)
            dve.wait_ge(gain_in, 16)

            def scale_h(half, n):
                if n >= len(tiles(half)):
                    return
                t = tiles(half)[n][1]
                at = h[H_SLOT[n]][0:t.n, :]
                all_of(dve, rooted, t.i, 2)
                dve.scalar_tensor_tensor(at, at if half else acc[0:t.n, n, :], ms[0:t.n, n, 2:3], gmlp[0:t.n, :],
                                         ALU.mult, ALU.mult).then_inc(normed, 1)

            def low_h(half, n):
                t = tiles(half)[n][1]
                all_of(dve, h_hi, t.i)
                dve.tensor_tensor(hT_lo[:, :, n * P:n * P + t.n], turned_at(half, n)[:, :, 0:t.n], hT_hi[:, :, n * P:n * P + t.n],
                                  ALU.subtract).then_inc(h_lo, 1)

            for n in range(LEAD[0]):
                scale_h(0, n)
            for n in range(4):
                low_h(0, n)
                for piece in (2 * n, 2 * n + 1):
                    weights_lo(0, 0, piece)
                scale_h(0, n + LEAD[0])
            AHEAD = {1: [(scale_h, 0)], 2: [(scale_h, 1)], 3: [(low_h, 0)], 4: [(low_h, 1)], 5: [(scale_h, 2)],
                     6: [(scale_h, 3), (low_h, 2)], 7: [(low_h, 3), (scale_h, 4), (scale_h, 5)]}
            for half in (0, 1):
                def add(b, n, t):
                    first = isinstance(b, int) and b == half * BLOCKS
                    reached(dve, down_done, down_count(half, b, n))
                    if first:
                        dve.wait_ge(acc_in[n], 16 * (half + 1) if n < HALF else 16)
                        all_of(dve, normed, t.i)
                    else:
                        reached(dve, added, down_count(half, b - 1, n))
                    dve.tensor_tensor(acc[0:t.n, n, :], acc[0:t.n, n, :], down_ps[n % 2][0:t.n, :], ALU.add).then_inc(added, 1)

                def body(b, slot, nxt):
                    for g, cols in enumerate(groups(half)):
                        if isinstance(b, int) and b == half * BLOCKS:
                            for n in turned_in(half, g):
                                low_h(half, n)
                                scale_h(half, n + LEAD[half])
                        count = up_count(half, b, g)
                        part = u[:, :, 0:cols.stop - cols.start]
                        reached(dve, rectified, count)
                        dve.tensor_tensor(part, part, part, ALU.mult).then_inc(squared, 1)
                        if g == len(groups(half)) - 1:
                            add(b, *tiles(half)[0])
                        reached(dve, u_hi, count)
                        dve.tensor_tensor(uT_lo[:, :, cols], part, uT_hi[:, :, cols], ALU.subtract).then_inc(u_lo, 1)
                    for n, t in tiles(half):
                        if n:
                            add(b, n, t)
                        if nxt is not None and n < PIECES:
                            weights_lo(nxt, 1 - slot, n)
                        if isinstance(nxt, int) and nxt == BLOCKS:
                            for step, place in AHEAD.get(n, []):
                                step(1, place)

                blocks(dve, half, body)


def ple_phase(nc, x_mlp, p_prompt, p_sample, g_ple, w_gate, w_proj, g_final, y_prompt, y_sample):
    PC = PLE // P
    W_PIECES = KC + PC
    SLOTS = 4
    with ExitStack() as ctx:
        def sb(name, shape, dt=F32):
            return ctx.enter_context(nc.sbuf_tensor("e_" + name, shape, dt))

        def ps(name, shape):
            return ctx.enter_context(nc.psum_tensor("e_" + name, shape, F32))

        def sems(names):
            return [ctx.enter_context(nc.semaphore("e_" + n)) for n in names.split()]

        wg_hi, wg_lo = sb("wg_hi", [P, KC, D], F32R), sb("wg_lo", [P, KC, D], F32R)
        wp_hi, wp_lo = sb("wp_hi", [P, PC, D], F32R), sb("wp_lo", [P, PC, D], F32R)
        w_raw = sb("w_raw", [P, W_PIECES, D])
        x, p = sb("x", [P, SLOTS, D]), sb("p", [P, SLOTS, PLE])
        h, y, gate = sb("h", [P, 2, D]), sb("y", [P, 2, D]), sb("gate", [P, D])
        gple, gfinal = sb("gple", [P, D]), sb("gfinal", [P, D])
        hT_hi, hT_lo = sb("hT_hi", [P, 2, KC, P], F32R), sb("hT_lo", [P, 2, KC, P], F32R)
        pT_hi, pT_lo = sb("pT_hi", [P, 2, PC, P], F32R), sb("pT_lo", [P, 2, PC, P], F32R)
        ident = sb("ident", [P, P])
        ms, ms_final = sb("ms", [P, 2, 3]), sb("ms_final", [P, 2, 3])
        constants = sb("constants", [P, 2])

        turned, p_turned_ps = ps("turned", [P, KC, P]), ps("p_turned", [P, 4, P])
        gate_ps, ple_ps = ps("gate_ps", [P, D]), ps("ple_ps", [P, D])

        made, gple_in, gfinal_in, w_hi_made, w_lo_made = sems("made gple_in gfinal_in w_hi_made w_lo_made")
        y_out = sems("y_out0 y_out1")
        w_in_sem = sems("w_in0 w_in1 w_in2 w_in3 w_in4")
        tile_in = sems("tile_in0 tile_in1 tile_in2 tile_in3")
        summed, rooted, normed = sems("summed rooted normed")
        final_summed, final_rooted, finished = sems("final_summed final_rooted finished")
        hp_turned, hp_hi, hp_lo = sems("hp_turned hp_hi hp_lo")
        gate_done, ple_done, gated, mixed_in, x_new = sems("gate_done ple_done gated mixed_in x_new")

        def rounds_of_four(eng, body, last):
            first, turns = 3, (NT - 6) // 4
            for r in range(first):
                body(r, r % SLOTS)
            with eng.Fori(0, turns) as turn:
                for k in range(SLOTS):
                    body(turn * SLOTS + (first + k), (first + k) % SLOTS)
            for r in range(first + turns * SLOTS, last + 1):
                body(r, r % SLOTS)

        def h_part(eng, sem, r):
            reached(eng, sem, r * 2 + 1)

        def p_part(eng, sem, r):
            reached(eng, sem, r * 2 + 2)

        def in_slot(eng, r, slot):
            reached(eng, tile_in[slot], r * 8 + 8 * (4 - slot))

        block = ctx.enter_context(nc.Block())

        @block.sync
        def _(sp):
            def load(r, slot):
                t = tile_at(r, slot)
                sp.dma_start(x[0:t.n, slot, :], x_mlp[token_rows(sp, r, t.n), :]).then_inc(tile_in[slot], 16)
                src = p_sample if t.n < P else p_prompt[token_rows(sp, r, P), :]
                sp.dma_start(p[0:t.n, slot, :], src).then_inc(tile_in[slot], 16)

            load(0, 0)
            sp.dma_start(gple[:], g_ple.partition_broadcast(P)).then_inc(gple_in, 16)
            for n in range(0, W_PIECES, 2):
                src = w_gate[n * P:(n + 2) * P, :] if n < KC else w_proj
                sp.dma_start(w_raw[:, n:n + 2, :], src.rearrange("(c p) d -> p c d", p=P)).then_inc(w_in_sem[n // 2], 16)
                if n == 2:
                    load(1, 1)
            sp.dma_start(gfinal[:], g_final.partition_broadcast(P)).then_inc(gfinal_in, 16)

            def body(r, slot):
                if exists(r - 2):
                    t = tile_at(r - 2, slot % 2)
                    dst = y_sample if t.n < P else y_prompt[token_rows(sp, t.i, P), :]
                    all_of(sp, finished, t.i)
                    sp.dma_start(dst, y[0:t.n, t.slot, :]).then_inc(y_out[t.slot], 16)
                if exists(r + 2):
                    load(r + 2, (slot + 2) % SLOTS)

            rounds_of_four(sp, body, NT + 2)
            for slot in (0, 1):
                sp.wait_ge(y_out[slot], 16 * (NT // 2 + 1 - slot))

        @block.gpsimd
        def _(pool):
            make_identity(pool, ident[:], made)
            pool.memset(constants[:, 0:1], EPS).then_inc(made, 1)
            pool.memset(constants[:, 1:2], -0.5).then_inc(made, 1)
            pool.wait_ge(made, 4)

            def body(r, slot):
                if exists(r + 1):
                    t = tile_at(r + 1, (slot + 1) % 2)
                    sums_root(pool, summed, rooted, t.i, ms[0:t.n, t.slot], constants[0:t.n])
                if exists(r - 1):
                    t = tile_at(r - 1, (slot + 1) % 2)
                    sums_root(pool, final_summed, final_rooted, t.i, ms_final[0:t.n, t.slot], constants[0:t.n])

            body(-1, SLOTS - 1)
            rounds_of_four(pool, body, NT + 1)

        @block.scalar
        def _(act):
            def sum_x(r, slot):
                t = tile_at(r, slot % 2)
                in_slot(act, r, slot)
                h_part(act, hp_turned, r - 2)
                all_of(act, rooted, r - 2, 2)
                act.activation(h[0:t.n, t.slot, :], x[0:t.n, slot, :], ACT.Square, scale=D ** -0.5,
                               accum_out=ms[0:t.n, t.slot, 0:1]).then_inc(summed, 1)

            def split(r, slot):
                t = tile_at(r, slot % 2)
                h_part(act, hp_turned, r)
                all_of(act, gate_done, r - 2)
                act.activation(hT_hi[:, t.slot, :, 0:t.n], turned[:, :, 0:t.n], ACT.Copy).then_inc(hp_hi, 1)
                p_part(act, hp_turned, r)
                all_of(act, ple_done, r - 2)
                act.activation(pT_hi[:, t.slot, :, 0:t.n], p_turned_ps[:, 0:PC, 0:t.n], ACT.Copy).then_inc(hp_hi, 1)

            sum_x(0, 0)
            for n in range(W_PIECES):
                act.wait_ge(w_in_sem[n // 2], 16)
                dst, c = (wg_hi, n) if n < KC else (wp_hi, n - KC)
                act.activation(dst[:, c, :], w_raw[:, n, :], ACT.Copy).then_inc(w_hi_made, 1)
                if n == 0:
                    split(0, 0)

            def body(r, slot):
                before = tile_at(r - 1, (slot + 1) % 2)
                m = before.n
                if exists(r - 1):
                    all_of(act, gate_done, r - 1)
                    all_of(act, x_new, r - 2)
                    act.activation(gate[0:m, :], gate_ps[0:m, :], ACT.Sigmoid).then_inc(gated, 1)
                if exists(r + 1):
                    sum_x(r + 1, (slot + 1) % SLOTS)
                if exists(r - 1):
                    all_of(act, x_new, r - 1)
                    all_of(act, final_rooted, r - 3, 2)
                    slot_loaded(act, y_out, tile_at(r - 3, before.slot))
                    act.activation(y[0:m, before.slot, :], x[0:m, (slot + 3) % SLOTS, :], ACT.Square, scale=D ** -0.5,
                                   accum_out=ms_final[0:m, before.slot, 0:1]).then_inc(final_summed, 1)
                if exists(r + 1):
                    split(r + 1, (slot + 1) % SLOTS)

            rounds_of_four(act, body, NT + 1)

        @block.tensor
        def _(pe):
            pe.wait_ge(made, 2)

            def turn(r, slot):
                t = tile_at(r, slot % 2)
                all_of(pe, normed, r)
                h_part(pe, hp_lo, r - 1)
                for c in range(KC):
                    ins = pe.transpose(turned[:, c, 0:t.n], h[0:t.n, t.slot, c * P:(c + 1) * P], ident[0:t.n, 0:t.n])
                ins.then_inc(hp_turned, 1)
                in_slot(pe, r, slot)
                p_part(pe, hp_lo, r - 1)
                for c in range(PC):
                    ins = pe.transpose(p_turned_ps[:, c, 0:t.n], p[0:t.n, slot, c * P:(c + 1) * P], ident[0:t.n, 0:t.n])
                ins.then_inc(hp_turned, 1)

            turn(0, 0)

            def body(r, slot):
                s = slot % 2
                h_part(pe, hp_lo, r)
                all_of(pe, gated, r - 1)
                for c in range(D // NB):
                    cols = slice(c * NB, (c + 1) * NB)
                    for n in range(KC):
                        if isinstance(r, int) and r == 0 and c == 0:
                            pe.wait_ge(w_lo_made, n + 1)
                        ins = split_product(pe, gate_ps[:, cols], (lambda k: hT_hi[:, s, k, :], lambda k: hT_lo[:, s, k, :]),
                                            (lambda k: wg_hi[:, k, cols], lambda k: wg_lo[:, k, cols]), [n], n == 0, n == KC - 1)
                    if c == 0 and exists(r + 1):
                        turn(r + 1, (slot + 1) % SLOTS)
                ins.then_inc(gate_done, 1)
                p_part(pe, hp_lo, r)
                all_of(pe, mixed_in, r - 1)
                if isinstance(r, int) and r == 0:
                    pe.wait_ge(w_lo_made, W_PIECES)
                for c in range(D // NB):
                    cols = slice(c * NB, (c + 1) * NB)
                    ins = split_product(pe, ple_ps[:, cols], (lambda k: pT_hi[:, s, k, :], lambda k: pT_lo[:, s, k, :]),
                                        (lambda k: wp_hi[:, k, cols], lambda k: wp_lo[:, k, cols]), range(PC))
                ins.then_inc(ple_done, 1)

            rounds_of_four(pe, body, NT)

        @block.vector
        def _(dve):
            def norm(r, slot):
                t = tile_at(r, slot % 2)
                all_of(dve, rooted, r, 2)
                dve.scalar_tensor_tensor(h[0:t.n, t.slot, :], x[0:t.n, slot, :], ms[0:t.n, t.slot, 2:3],
                                         gple[0:t.n, :], ALU.mult, ALU.mult).then_inc(normed, 1)

            def split(r, slot):
                t = tile_at(r, slot % 2)
                h_part(dve, hp_hi, r)
                dve.tensor_tensor(hT_lo[:, t.slot, :, 0:t.n], turned[:, :, 0:t.n], hT_hi[:, t.slot, :, 0:t.n], ALU.subtract).then_inc(hp_lo, 1)
                p_part(dve, hp_hi, r)
                dve.tensor_tensor(pT_lo[:, t.slot, :, 0:t.n], p_turned_ps[:, 0:PC, 0:t.n], pT_hi[:, t.slot, :, 0:t.n], ALU.subtract).then_inc(hp_lo, 1)

            dve.wait_ge(gple_in, 16)
            norm(0, 0)
            for n in range(W_PIECES):
                hi, lo, c = (wg_hi, wg_lo, n) if n < KC else (wp_hi, wp_lo, n - KC)
                dve.wait_ge(w_hi_made, n + 1)
                dve.tensor_tensor(lo[:, c, :], w_raw[:, n, :], hi[:, c, :], ALU.subtract).then_inc(w_lo_made, 1)
                if n == 0:
                    split(0, 0)
            dve.wait_ge(gfinal_in, 16)

            def body(r, slot):
                before = tile_at(r - 1, (slot + 1) % 2)
                m, s = before.n, before.slot
                xb = x[0:m, (slot + 3) % SLOTS, :]
                if exists(r - 1):
                    all_of(dve, ple_done, r - 1)
                    all_of(dve, gated, r - 1)
                    dve.tensor_tensor(gate[0:m, :], gate[0:m, :], ple_ps[0:m, :], ALU.mult).then_inc(mixed_in, 1)
                    all_of(dve, mixed_in, r - 1)
                    dve.tensor_tensor(xb, xb, gate[0:m, :], ALU.add).then_inc(x_new, 1)
                if exists(r + 1):
                    norm(r + 1, (slot + 1) % SLOTS)
                if exists(r - 1):
                    all_of(dve, final_rooted, r - 1, 2)
                    dve.scalar_tensor_tensor(y[0:m, s, :], xb, ms_final[0:m, s, 2:3], gfinal[0:m, :], ALU.mult, ALU.mult).then_inc(finished, 1)
                if exists(r + 1):
                    split(r + 1, (slot + 1) % SLOTS)

            rounds_of_four(dve, body, NT + 1)

def build(nc, x_prompt, x_sample, cache_k, cache_v, state_c, state_n, state_m, p_prompt, p_sample,
          g_mix, w_in, b_igate, b_fgate, g_head, sinks, w_out, g_mlp, w_up, w_down, g_ple,
          w_ple_gate, w_ple_proj, g_final, y_prompt, y_sample, pk, pv, pc, pn, pm, sk, sv, sc, sn, sm):
    mixed = nc.dram_tensor("mixed_heads", [TOK, MW], F32, kind="Internal").ap()
    flat = lambda a: a[0, 0].rearrange("w h d -> w (h d)")
    x_mid = nc.dram_tensor("x_after_mixers", [TOK, D], F32, kind="Internal").ap()
    with nc.sbuf_tensor("x", [P, 2, D], F32) as x, nc.sbuf_tensor("gmix", [P, D], F32) as gmix:
        mlstm_phase(nc, x_prompt[0], x_sample[0], g_mix[0], w_in[0], b_igate[0], b_fgate[0], g_head[0],
                    state_c[0, 0], state_n[0, 0], state_m[0, 0], mixed,
                    (pc[0, 0], sc[0, 0]), (pn[0, 0], sn[0, 0]), (pm[0, 0], sm[0, 0]), x, gmix)
        attention_phase(nc, x_prompt[0], x_sample[0], w_in[0], sinks[0], w_out[0], flat(cache_k), flat(cache_v),
                        mixed, x_mid, (flat(pk), flat(sk)), (flat(pv), flat(sv)), x, gmix)
    x_mlp = nc.dram_tensor("x_after_mlp", [TOK, D], F32, kind="Internal").ap()
    mlp_phase(nc, x_mid, g_mlp[0], w_up[0], w_down[0], x_mlp)
    ple_phase(nc, x_mlp, p_prompt[0, 0], p_sample[0, 0], g_ple[0], w_ple_gate[0], w_ple_proj[0], g_final, y_prompt[0], y_sample[0])



_INS = ["x_prompt", "x_sample", "cache_swa_k", "cache_swa_v", "state_mlstm_c", "state_mlstm_n", "state_mlstm_m",
        "p_prompt", "p_sample", "g_mix", "w_in", "b_igate", "b_fgate", "g_head", "attn_sinks", "w_out", "g_mlp",
        "w_up", "w_down", "g_ple", "w_ple_gate", "w_ple_proj", "g_final"]
_STATE = [(1, 1, HEADS, QK, QK), (1, 1, HEADS, QK), (1, 1, HEADS)]
_WINDOW = (1, 1, P, KVH, HD)
_OUTS = [(1, SEQ, D), (1, DEC, D), _WINDOW, _WINDOW, *_STATE, _WINDOW, _WINDOW, *_STATE]


def kernel(**inputs):
    import numpy as _np
    import concourse.bacc as _bacc
    from concourse import mybir as _mybir
    from concourse.bass_utils import run_bass_kernel_spmd as _run

    nc = _bacc.Bacc("TRN2", target_bir_lowering=False, num_devices=1)
    arrays, args = {}, []
    for name in _INS:
        a = _np.ascontiguousarray(inputs[name])
        arrays[f"in_{name}"] = a
        args.append(nc.dram_tensor(f"in_{name}", a.shape, _mybir.dt.from_np(a.dtype), kind="ExternalInput").ap())
    for i, shape in enumerate(_OUTS):
        args.append(nc.dram_tensor(f"out_{i}", shape, _mybir.dt.float32, kind="ExternalOutput").ap())
    build(nc, *args)
    r = _run(nc, [arrays], core_ids=[0])
    return tuple(r.results[0][f"out_{i}"] for i in range(len(_OUTS)))
```
